# Optimizing a Trainium2 kernel written in Bass

```python
import jax, jax.numpy as jnp
from jax import lax
import numpy as np
import math

D_MODEL = 1024
BATCH = 1
SEQ = 256
DEPTH = 2

CHUNK = 64
EPS = 1e-6
POOL_WINDOWS = (2, 4, 8, 16)
POOL_GROUP = D_MODEL // 4
POOL_WIDTH = 4 * POOL_GROUP
SGU_LEN = 128
SGU_HEAD_DIM = 128
SGU_WIDTH = D_MODEL
SGU_HEADS = SGU_WIDTH // SGU_HEAD_DIM
GLA_HEADS = 4
GLA_KW = D_MODEL // 2
GLA_VW = D_MODEL
GLA_DK = GLA_KW // GLA_HEADS
GLA_DV = GLA_VW // GLA_HEADS
GLA_RANK = 16
GLA_TAU = 16.0
SB_HEAD_DIM = 128
SB_WIDTH = D_MODEL
SB_HEADS = SB_WIDTH // SB_HEAD_DIM
SB_QBLOCK = 128
EVEN_SIZES = (POOL_WIDTH, SGU_WIDTH, SGU_WIDTH, POOL_WIDTH + SGU_WIDTH)
ODD_SIZES = (GLA_KW, GLA_KW, GLA_VW, GLA_RANK, SB_WIDTH, SB_WIDTH, SB_WIDTH, GLA_VW + SB_WIDTH)
EVEN_IN = sum(EVEN_SIZES)
ODD_IN = sum(ODD_SIZES)
EVEN_MIX = POOL_WIDTH + SGU_WIDTH
ODD_MIX = GLA_VW + SB_WIDTH
N_EVEN = (DEPTH + 1) // 2
N_ODD = DEPTH // 2


def _split(t, sizes):
    idx = [int(i) for i in np.cumsum(sizes)[:-1]]
    return jnp.split(t, idx, axis=-1)

def rmsnorm(x, g):
    xf = x.astype(jnp.float32)
    y = xf * lax.rsqrt(jnp.mean(xf * xf, axis=-1, keepdims=True) + EPS)
    return (y * g.astype(jnp.float32)).astype(x.dtype)

def ada_modulate(x, c, norm_g, ada_w, ada_b):
    ada = jax.nn.silu(c) @ ada_w + ada_b
    shift, scale, gate = jnp.split(ada, 3, axis=-1)
    h = rmsnorm(x, norm_g) * (1.0 + scale[:, None, :]) + shift[:, None, :]
    return h, gate[:, None, :]

def pool_mixer(a, pool_w, pool_scale):
    B_, S, _ = a.shape
    af = a.astype(jnp.float32)
    cs = jnp.concatenate([jnp.zeros_like(af[:, :1]), jnp.cumsum(af, axis=1)], axis=1)
    t = np.arange(S)
    outs = []
    for g, w in enumerate(POOL_WINDOWS):
        sl = slice(g * POOL_GROUP, (g + 1) * POOL_GROUP)
        start = np.maximum(t + 1 - w, 0)
        count = jnp.asarray((t + 1 - start).astype(np.float32))
        win_sum = cs[:, 1:, sl] - cs[:, start, sl]
        outs.append(win_sum / count[None, :, None] - af[..., sl])
    p = jnp.stack(outs, axis=2).astype(a.dtype)
    y = jnp.einsum('bsgc,gcd->bsgd', p, pool_w).reshape(B_, S, POOL_WIDTH)
    return y * pool_scale

def spatial_gating(u, v, norm_g, w_s, b_s):
    B_, S, _ = u.shape
    n = S // SGU_LEN
    vh = rmsnorm(v, norm_g).reshape(B_, n, SGU_LEN, SGU_HEADS, SGU_HEAD_DIM)
    mask = jnp.tril(jnp.ones((SGU_LEN, SGU_LEN), dtype=bool))
    w = jnp.where(mask[None], w_s, jnp.zeros_like(w_s))
    z = jnp.einsum('hts,bnshd->bnthd', w, vh) + b_s.T[None, None, :, :, None]
    return u * z.reshape(B_, S, SGU_WIDTH)

def gla(q, k, v, log_a):
    B_, S = q.shape[:2]
    n = S // CHUNK
    r = lambda t: t.astype(jnp.float32).reshape(B_, n, CHUNK, *t.shape[2:])
    qf = r(q) * (GLA_DK ** -0.5)
    kf, vf, la = r(k), r(v), r(log_a)
    bcum = jnp.cumsum(la, axis=2)
    b_last = bcum[:, :, -1]
    q_dec = qf * jnp.exp(bcum)
    k_inv = kf * jnp.exp(-bcum)
    k_end = kf * jnp.exp(b_last[:, :, None] - bcum)
    mask = jnp.tril(jnp.ones((CHUNK, CHUNK), dtype=bool))
    att = jnp.einsum('bnthk,bnshk->bnhts', q_dec, k_inv)
    att = jnp.where(mask, att, 0.0)
    o_intra = jnp.einsum('bnhts,bnshv->bnthv', att, vf)

    def step(state, xs):
        qd, ke, vc, bl = xs
        o = jnp.einsum('bthk,bhkv->bthv', qd, state)
        state = jnp.exp(bl)[..., None] * state + jnp.einsum('bshk,bshv->bhkv', ke, vc)
        return state, o

    s0 = jnp.zeros((B_, GLA_HEADS, GLA_DK, GLA_DV), jnp.float32)
    xs = (jnp.moveaxis(q_dec, 1, 0), jnp.moveaxis(k_end, 1, 0), jnp.moveaxis(vf, 1, 0), jnp.moveaxis(b_last, 1, 0))
    _, o_inter = lax.scan(step, s0, xs)
    o = o_intra + jnp.moveaxis(o_inter, 0, 1)
    return o.reshape(B_, S, GLA_HEADS, GLA_DV).astype(v.dtype)

def stick_breaking(q, k, v):
    B_, S, H, Dh = q.shape
    scale = Dh ** -0.5
    outs = []
    for i in range(S // SB_QBLOCK):
        q0, q1 = i * SB_QBLOCK, (i + 1) * SB_QBLOCK
        z = jnp.einsum('bthd,bshd->bhts', q[:, q0:q1], k[:, :q1]).astype(jnp.float32) * scale
        strict = np.arange(q1)[None, :] < np.arange(q0, q1)[:, None]
        log_beta = jax.nn.log_sigmoid(z)
        log_1m = jnp.where(strict, jax.nn.log_sigmoid(-z), 0.0)
        after = lax.cumsum(log_1m, axis=3, reverse=True) - log_1m
        w = jnp.where(strict, jnp.exp(log_beta + after), 0.0)
        outs.append(jnp.einsum('bhts,bshd->bthd', w.astype(v.dtype), v[:, :q1]))
    return jnp.concatenate(outs, axis=1)

def even_layer(x, c, norm_g, ada_w, ada_b, in_w, pool_w, pool_scale, sgu_norm_g, sgu_w, sgu_b, out_w):
    h, gate_res = ada_modulate(x, c, norm_g, ada_w, ada_b)
    a, u, v, gate = _split(h @ in_w, EVEN_SIZES)
    ya = pool_mixer(a, pool_w, pool_scale)
    yb = spatial_gating(u, v, sgu_norm_g, sgu_w, sgu_b)
    y = jnp.concatenate([ya, yb], axis=-1) * jax.nn.silu(gate)
    return x + gate_res * (y @ out_w)

def odd_layer(x, c, norm_g, ada_w, ada_b, in_w, gate_w, gate_b, gla_norm_g, out_w):
    B_, S, _ = x.shape
    h, gate_res = ada_modulate(x, c, norm_g, ada_w, ada_b)
    gq, gk, gv, glr, sq, sk, sv, gate = _split(h @ in_w, ODD_SIZES)
    log_a = jax.nn.log_sigmoid((glr @ gate_w + gate_b).astype(jnp.float32)) / GLA_TAU
    hd = lambda t, n, d: t.reshape(B_, S, n, d)
    yc = gla(hd(gq, GLA_HEADS, GLA_DK), hd(gk, GLA_HEADS, GLA_DK), hd(gv, GLA_HEADS, GLA_DV),
             hd(log_a, GLA_HEADS, GLA_DK))
    yc = rmsnorm(yc, gla_norm_g).reshape(B_, S, GLA_VW)
    yd = stick_breaking(hd(sq, SB_HEADS, SB_HEAD_DIM), hd(sk, SB_HEADS, SB_HEAD_DIM),
                        hd(sv, SB_HEADS, SB_HEAD_DIM)).reshape(B_, S, SB_WIDTH)
    y = jnp.concatenate([yc, yd], axis=-1) * jax.nn.silu(gate)
    return x + gate_res * (y @ out_w)

def first_inputs(seed: int = 0) -> dict:
    key = jax.random.key(seed)
    ks = jax.random.split(key, 20)
    nrm = lambda k, shape, s: jax.random.normal(k, shape, jnp.float32) * s
    return {
        "x": nrm(ks[0], (BATCH, SEQ, D_MODEL), 1.0),
        "c": nrm(ks[1], (BATCH, D_MODEL), 1.0),
        "ada_w": nrm(ks[2], (DEPTH, D_MODEL, 3 * D_MODEL), 0.5 * D_MODEL ** -0.5),
        "ada_b": nrm(ks[3], (DEPTH, 3 * D_MODEL), 0.02),
        "norm_g": 1.0 + nrm(ks[4], (DEPTH, D_MODEL), 0.05),
        "even_in_w": nrm(ks[5], (N_EVEN, D_MODEL, EVEN_IN), D_MODEL ** -0.5),
        "pool_w": nrm(ks[6], (N_EVEN, 4, POOL_GROUP, POOL_GROUP), POOL_GROUP ** -0.5),
        "pool_scale": 1.0 + nrm(ks[7], (N_EVEN, POOL_WIDTH), 0.1),
        "sgu_norm_g": 1.0 + nrm(ks[8], (N_EVEN, SGU_WIDTH), 0.05),
        "sgu_w": nrm(ks[9], (N_EVEN, SGU_HEADS, SGU_LEN, SGU_LEN), SGU_LEN ** -0.5),
        "sgu_b": 1.0 + nrm(ks[10], (N_EVEN, SGU_HEADS, SGU_LEN), 0.1),
        "even_out_w": nrm(ks[11], (N_EVEN, EVEN_MIX, D_MODEL), EVEN_MIX ** -0.5),
        "odd_in_w": nrm(ks[12], (N_ODD, D_MODEL, ODD_IN), D_MODEL ** -0.5),
        "gla_gate_w": nrm(ks[13], (N_ODD, GLA_RANK, GLA_KW), GLA_RANK ** -0.5),
        "gla_gate_b": nrm(ks[14], (N_ODD, GLA_KW), 0.1),
        "gla_norm_g": 1.0 + nrm(ks[15], (N_ODD, GLA_HEADS, GLA_DV), 0.05),
        "odd_out_w": nrm(ks[16], (N_ODD, ODD_MIX, D_MODEL), ODD_MIX ** -0.5),
        "final_g": 1.0 + nrm(ks[17], (D_MODEL,), 0.05),
    }

def first_block(x, c, ada_w, ada_b, norm_g, even_in_w, pool_w, pool_scale, sgu_norm_g, sgu_w, sgu_b,
              even_out_w, odd_in_w, gla_gate_w, gla_gate_b, gla_norm_g, odd_out_w, final_g):
    for i in range(DEPTH):
        j = i // 2
        if i % 2 == 0:
            x = even_layer(x, c, norm_g[i], ada_w[i], ada_b[i], even_in_w[j], pool_w[j], pool_scale[j],
                           sgu_norm_g[j], sgu_w[j], sgu_b[j], even_out_w[j])
        else:
            x = odd_layer(x, c, norm_g[i], ada_w[i], ada_b[i], odd_in_w[j], gla_gate_w[j], gla_gate_b[j],
                          gla_norm_g[j], odd_out_w[j])
    return rmsnorm(x, final_g)


DEPTH_2 = 1

MIX_WIDTH = D_MODEL
D_CONV = MIX_WIDTH // 2
D_SSM = MIX_WIDTH - D_CONV
CONV_HEAD_DIM = 64
CONV_HEADS = D_CONV // CONV_HEAD_DIM
CONV_WIDTH = 3
SSM_GROUP_CH = 16
SSM_GROUPS = D_SSM // SSM_GROUP_CH
SSM_STATE = 64
D_FF = 256 * ((8 * D_MODEL // 3 + 255) // 256)
N_MOD = 9
DT_MIN = 1e-3
DT_MAX = 1e-1


def rms_norm(x, gain):
    xf = x.astype(jnp.float32)
    y = xf * lax.rsqrt(jnp.mean(xf * xf, axis=-1, keepdims=True) + EPS)
    return (y * gain.astype(jnp.float32)).astype(x.dtype)

def modulate(h, shift, scale):
    return h * (1 + scale[:, None, :]) + shift[:, None, :]

def swiglu(h, w_gate, w_up, w_down):
    return (jax.nn.silu(h @ w_gate) * (h @ w_up)) @ w_down

def short_conv_mixer(b_gate, c_gate, v, conv_w):
    z = c_gate * v
    z = lax.conv_general_dilated(
        z, conv_w[:, None, :].astype(z.dtype),
        window_strides=(1,), padding=[(CONV_WIDTH - 1, 0)],
        dimension_numbers=('NWC', 'WIO', 'NWC'),
        feature_group_count=D_CONV)
    return b_gate * z

def _ssm_combine(left, right):
    a_l, b_l = left
    a_r, b_r = right
    return a_r * a_l, a_r * b_l + b_r

def s5_mixer(u, lambda_re, lambda_im, log_dt, b_re, b_im, c_re, c_im, d_skip, glu_w, glu_b):
    bsz, seq, _ = u.shape
    uf = u.astype(jnp.float32).reshape(bsz, seq, SSM_GROUPS, SSM_GROUP_CH)
    lam = lax.complex(lambda_re.astype(jnp.float32), lambda_im.astype(jnp.float32))
    dt = jnp.exp(log_dt.astype(jnp.float32))[:, None]
    lam_bar = jnp.exp(lam * dt)
    b = lax.complex(b_re.astype(jnp.float32), b_im.astype(jnp.float32))
    b_bar = ((lam_bar - 1) / lam)[..., None] * b
    bu = jnp.einsum('gpc,bsgc->bsgp', b_bar, uf.astype(jnp.complex64))
    a = jnp.broadcast_to(lam_bar, bu.shape)
    _, states = lax.associative_scan(_ssm_combine, (a, bu), axis=1)
    c = lax.complex(c_re.astype(jnp.float32), c_im.astype(jnp.float32))
    y = jnp.einsum('gcp,bsgp->bsgc', c, states).real \
        + d_skip.astype(jnp.float32).reshape(SSM_GROUPS, SSM_GROUP_CH) * uf
    y = jax.nn.gelu(y.reshape(bsz, seq, D_SSM))
    y = y * jax.nn.sigmoid(y @ glu_w.astype(jnp.float32) + glu_b.astype(jnp.float32))
    return y.astype(u.dtype)

def second_inputs(seed: int = 0) -> dict:
    key = jax.random.key(seed)
    ks = jax.random.split(key, 32)
    f32 = jnp.float32

    def nrm(k, shape, std):
        return jax.random.normal(k, shape, f32) * std

    def gain(k, shape):
        return 1.0 + 0.05 * jax.random.normal(k, shape, f32)

    L = DEPTH_2
    n_idx = jnp.arange(SSM_STATE, dtype=f32)
    return {
        "x": nrm(ks[0], (BATCH, SEQ, D_MODEL), 1.0),
        "cond": nrm(ks[1], (BATCH, D_MODEL), 1.0),
        "w_mod": nrm(ks[2], (L, D_MODEL, N_MOD * D_MODEL), 0.5 * D_MODEL ** -0.5),
        "b_mod": nrm(ks[3], (L, N_MOD * D_MODEL), 0.02),
        "ffn1_norm": gain(ks[4], (L, D_MODEL)),
        "ffn1_w_gate": nrm(ks[5], (L, D_MODEL, D_FF), D_MODEL ** -0.5),
        "ffn1_w_up": nrm(ks[6], (L, D_MODEL, D_FF), D_MODEL ** -0.5),
        "ffn1_w_down": nrm(ks[7], (L, D_FF, D_MODEL), D_FF ** -0.5),
        "mix_norm": gain(ks[8], (L, D_MODEL)),
        "w_in": nrm(ks[9], (L, D_MODEL, 3 * D_CONV + D_SSM), D_MODEL ** -0.5),
        "conv_w": nrm(ks[10], (L, CONV_WIDTH, D_CONV), CONV_WIDTH ** -0.5),
        "lambda_re": -0.5 + 0.01 * jax.random.normal(ks[11], (L, SSM_GROUPS, SSM_STATE), f32),
        "lambda_im": math.pi * n_idx + 0.01 * jax.random.normal(ks[12], (L, SSM_GROUPS, SSM_STATE), f32),
        "log_dt": jax.random.uniform(ks[13], (L, SSM_GROUPS), f32, math.log(DT_MIN), math.log(DT_MAX)),
        "ssm_b_re": nrm(ks[14], (L, SSM_GROUPS, SSM_STATE, SSM_GROUP_CH), (2 * SSM_GROUP_CH) ** -0.5),
        "ssm_b_im": nrm(ks[15], (L, SSM_GROUPS, SSM_STATE, SSM_GROUP_CH), (2 * SSM_GROUP_CH) ** -0.5),
        "ssm_c_re": nrm(ks[16], (L, SSM_GROUPS, SSM_GROUP_CH, SSM_STATE), SSM_STATE ** -0.5),
        "ssm_c_im": nrm(ks[17], (L, SSM_GROUPS, SSM_GROUP_CH, SSM_STATE), SSM_STATE ** -0.5),
        "ssm_d": nrm(ks[18], (L, D_SSM), 1.0),
        "glu_w": nrm(ks[19], (L, D_SSM, D_SSM), D_SSM ** -0.5),
        "glu_b": nrm(ks[20], (L, D_SSM), 0.02),
        "out_norm_conv": gain(ks[21], (L, D_CONV)),
        "out_norm_ssm": gain(ks[22], (L, D_SSM)),
        "w_out": nrm(ks[23], (L, MIX_WIDTH, D_MODEL), MIX_WIDTH ** -0.5),
        "ffn2_norm": gain(ks[24], (L, D_MODEL)),
        "ffn2_w_gate": nrm(ks[25], (L, D_MODEL, D_FF), D_MODEL ** -0.5),
        "ffn2_w_up": nrm(ks[26], (L, D_MODEL, D_FF), D_MODEL ** -0.5),
        "ffn2_w_down": nrm(ks[27], (L, D_FF, D_MODEL), D_FF ** -0.5),
        "final_norm": gain(ks[28], (D_MODEL,)),
    }

def second_block(x, cond, w_mod, b_mod, ffn1_norm, ffn1_w_gate, ffn1_w_up, ffn1_w_down,
              mix_norm, w_in, conv_w, lambda_re, lambda_im, log_dt,
              ssm_b_re, ssm_b_im, ssm_c_re, ssm_c_im, ssm_d, glu_w, glu_b,
              out_norm_conv, out_norm_ssm, w_out,
              ffn2_norm, ffn2_w_gate, ffn2_w_up, ffn2_w_down, final_norm):
    c_act = jax.nn.silu(cond)
    for l in range(DEPTH_2):
        mod = c_act @ w_mod[l] + b_mod[l]
        (sh1, sc1, g1, sh2, sc2, g2, sh3, sc3, g3) = jnp.split(mod, N_MOD, axis=-1)

        h = modulate(rms_norm(x, ffn1_norm[l]), sh1, sc1)
        x = x + 0.5 * g1[:, None, :] * swiglu(h, ffn1_w_gate[l], ffn1_w_up[l], ffn1_w_down[l])

        h = modulate(rms_norm(x, mix_norm[l]), sh2, sc2)
        proj = h @ w_in[l]
        b_gate, c_gate, v, u = jnp.split(proj, [D_CONV, 2 * D_CONV, 3 * D_CONV], axis=-1)
        y_conv = short_conv_mixer(b_gate, c_gate, v, conv_w[l])
        y_ssm = s5_mixer(u, lambda_re[l], lambda_im[l], log_dt[l], ssm_b_re[l], ssm_b_im[l],
                         ssm_c_re[l], ssm_c_im[l], ssm_d[l], glu_w[l], glu_b[l])
        y_mix = jnp.concatenate([rms_norm(y_conv, out_norm_conv[l]),
                                 rms_norm(y_ssm, out_norm_ssm[l])], axis=-1)
        x = x + g2[:, None, :] * (y_mix @ w_out[l])

        h = modulate(rms_norm(x, ffn2_norm[l]), sh3, sc3)
        x = x + 0.5 * g3[:, None, :] * swiglu(h, ffn2_w_gate[l], ffn2_w_up[l], ffn2_w_down[l])
    return rms_norm(x, final_norm)


def setup_inputs(seed=0):
    out = dict(first_inputs(seed))
    for name, value in second_inputs(seed + 1).items():
        if name != "x":
            out[name + "_2"] = value
    return out


def reference(
    x, c, ada_w, ada_b, norm_g, even_in_w, pool_w, pool_scale, sgu_norm_g, sgu_w, sgu_b,
    even_out_w, odd_in_w, gla_gate_w, gla_gate_b, gla_norm_g, odd_out_w, final_g, cond_2,
    w_mod_2, b_mod_2, ffn1_norm_2, ffn1_w_gate_2, ffn1_w_up_2, ffn1_w_down_2, mix_norm_2,
    w_in_2, conv_w_2, lambda_re_2, lambda_im_2, log_dt_2, ssm_b_re_2, ssm_b_im_2, ssm_c_re_2,
    ssm_c_im_2, ssm_d_2, glu_w_2, glu_b_2, out_norm_conv_2, out_norm_ssm_2, w_out_2,
    ffn2_norm_2, ffn2_w_gate_2, ffn2_w_up_2, ffn2_w_down_2, final_norm_2,
):
    x = first_block(
        x, c, ada_w, ada_b, norm_g, even_in_w, pool_w, pool_scale, sgu_norm_g, sgu_w, sgu_b,
        even_out_w, odd_in_w, gla_gate_w, gla_gate_b, gla_norm_g, odd_out_w, final_g,
    )
    return second_block(
        x, cond_2, w_mod_2, b_mod_2, ffn1_norm_2, ffn1_w_gate_2, ffn1_w_up_2, ffn1_w_down_2,
        mix_norm_2, w_in_2, conv_w_2, lambda_re_2, lambda_im_2, log_dt_2, ssm_b_re_2,
        ssm_b_im_2, ssm_c_re_2, ssm_c_im_2, ssm_d_2, glu_w_2, glu_b_2, out_norm_conv_2,
        out_norm_ssm_2, w_out_2, ffn2_norm_2, ffn2_w_gate_2, ffn2_w_up_2, ffn2_w_down_2,
        final_norm_2,
    )


_drawn_inputs = setup_inputs


def setup_inputs(seed=0):
    import zlib

    import numpy as np

    out = dict(_drawn_inputs(seed))
    spreads = {}
    factors = {'pool_scale': 4.191,
     'sgu_norm_g': 8.0,
     'sgu_b': 3.499,
     'gla_gate_b': 8.0,
     'gla_norm_g': 8.0,
     'ffn1_norm_2': 7.069,
     'lambda_re_2': 64.0,
     'lambda_im_2': 22.832,
     'log_dt_2': 26.8,
     'ssm_b_re_2': 32.608,
     'ssm_b_im_2': 33.008,
     'ssm_c_re_2': 34.808,
     'ssm_c_im_2': 32.248,
     'glu_b_2': 28.426,
     'out_norm_conv_2': 27.477,
     'out_norm_ssm_2': 24.925,
     'ffn2_norm_2': 8.0}
    for name, (base, spread) in spreads.items():
        noise = np.random.default_rng([zlib.crc32(name.encode()), seed]).standard_normal(out[name].shape)
        drawn = base * np.exp(spread * noise) if base else spread * noise
        out[name] = __import__('jax').numpy.asarray(drawn.astype(out[name].dtype))
    for name, factor in factors.items():
        out[name] = (out[name] * factor).astype(out[name].dtype)
    return out
```

```python
from contextlib import ExitStack

import numpy as np
import concourse.bass as bass
from concourse import mybir

F32 = mybir.dt.float32
BF16 = mybir.dt.bfloat16
ALU = mybir.AluOpType
ACT = mybir.ActivationFunctionType
MUL, ADD, SUB, MAX, MIN = ALU.mult, ALU.add, ALU.subtract, ALU.max, ALU.min

P = 128
T = 256
D = 1024
EPS = 1e-6
TWO_PI = 6.283185307179586
TP_HI = 6.28125
TP_LO = TWO_PI - TP_HI
MAGIC = 12582912.0
GELU_C = 2.0 * 0.7978845608028654

RING = 7
NLO = 3
WORDS = 26880

C_ID, C_ONE, C_NU, C_NONE, C_IC, C_T, C_M2, C_K = 0, 128, 256, 384, 512, 640, 896, 898
C_ALL = 902


def constants():
    c = np.zeros((P, C_ALL), np.float32)
    i = np.arange(P)
    c[:, C_ID:C_ID + P] = np.eye(P)
    c[:, C_ONE:C_ONE + P] = 1.0
    c[:, C_NU:C_NU + P] = np.where(i[:, None] >= i[None, :], -1.0, 0.0)
    c[:, C_NONE:C_NONE + P] = -1.0
    t = np.arange(16)
    ic = np.stack([1.0 / np.minimum(t + 1, w) for w in (2, 2, 4, 4, 8, 8, 16, 16)])
    c[:, C_IC:C_IC + 128] = ic.reshape(1, 128)
    c[:, C_T:C_T + T] = np.arange(T)
    c[:, C_M2] = (i // 16) % 2 == 0
    c[:, C_M2 + 1] = (i // 16) % 2 == 1
    c[:, C_K] = 1.0
    c[:, C_K + 1] = np.pi / 2
    c[:, C_K + 2] = 0.0
    c[:, C_K + 3] = 0.0
    return c


class Queue:

    def __init__(self, sem):
        self.sem, self.n, self.items, self.seen = sem, 0, [], {}

    def wait(self, *marks):
        for s, v in marks:
            if self.seen.get(s.name, 0) < v:
                self.seen[s.name] = v
                self.items.append((None, s, v, None))
        return self

    def do(self, fn, *args, **kw):
        self.n += 1
        self.items.append((fn, args, kw, (self.sem, 1)))
        return (self.sem, self.n)

    def quiet(self, fn, *args, **kw):
        self.items.append((fn, args, kw, None))

    def dma(self, fn, out, src, sem):
        self.items.append((fn, (out, src), {}, (sem, 16)))

    def emit(self, eng):
        for fn, a, b, inc in self.items:
            if fn is None:
                eng.wait_ge(a, b)
            else:
                ins = fn(*a, **b)
                if inc is not None:
                    ins.then_inc(inc[0], inc[1])


def build(nc, I, out):
    ctx = ExitStack()
    with ctx:
        def sb(name, shape, dt=F32):
            return ctx.enter_context(nc.sbuf_tensor(name, shape, dt))

        def sem(name):
            return ctx.enter_context(nc.semaphore(name))

        ring = sb("ring", [P, RING, 2048])
        lo = sb("lo", [P, NLO, 2048], BF16)
        xT = sb("xT", [P, 8, T])
        hh = sb("hh", [P, 8, T], BF16)
        hl = sb("hl", [P, 8, T], BF16)
        SQT = sb("SQT", [P, 4, T])
        RT = sb("RT", [P, 4, T])
        cst = sb("cst", [P, C_ALL])
        VC = sb("VC", [P, 300])
        MOD = sb("MOD", [P, 24 + 24 + 72])
        PC = sb("PC", [P, 64])
        AR = sb("AR", [P, WORDS])
        pacc = ctx.enter_context(nc.psum_tensor("pacc", [P, 8, T], F32))
        pw = [ctx.enter_context(nc.psum_tensor(f"pw{i}", [P, 512], F32)) for i in range(4)]

        PE, V, S, G, SP = (Queue(sem(n)) for n in ("s_pe", "s_v", "s_s", "s_g", "s_sp"))
        s_ring = [sem(f"s_ring{i}") for i in range(RING)]
        s_small = {}

        mm, tr = nc.tensor.matmul, nc.tensor.transpose
        tt, ts, stt = nc.vector.tensor_tensor, nc.vector.tensor_scalar, nc.vector.scalar_tensor_tensor
        act = nc.scalar.activation

        def ar(off, n):
            return AR[:, off:off + n]

        def arb(off, n):
            return AR[:, off:off + n // 2].bitcast(BF16)

        def v3(ap, a):
            return ap.rearrange("p (a n) -> p a n", a=a)

        ident = cst[:, C_ID:C_ID + P]
        ones = cst[:, C_ONE:C_ONE + P]
        negU = cst[:, C_NU:C_NU + P]
        negones = cst[:, C_NONE:C_NONE + P]
        ic = v3(cst[:, C_IC:C_IC + P], 8)
        tvec = cst[:, C_T:C_T + T]
        one_c = cst[:, C_K:C_K + 1]
        hpi_c = cst[:, C_K + 1:C_K + 2]

        def small(q, fn, name, dst, src):
            s = sem("d_" + name)
            q.dma(fn, dst, src, s)
            s_small[name] = (s, 16)
            return (s, 16)

        small(S, nc.scalar.dma_start, "cst", cst[:, :], I["consts"])
        rows = {}
        packs = [[("c", I["c"], 8), ("norm_g", I["norm_g"], 16), ("ada_b", I["ada_b"], 48),
                  ("pool_scale", I["pool_scale"], 8), ("sgu_norm_g", I["sgu_norm_g"], 8),
                  ("final_g", I["final_g"], 8), ("gla_gate_b", I["gla_gate_b"], 4),
                  ("gla_norm_g", I["gla_norm_g"], 8), ("cond", I["cond_2"], 8)],
                 [("b_mod", I["b_mod_2"], 72), ("ffn1_norm", I["ffn1_norm_2"], 8), ("mix_norm", I["mix_norm_2"], 8),
                  ("conv_w", I["conv_w_2"], 12), ("ssm_d", I["ssm_d_2"], 4), ("glu_b", I["glu_b_2"], 4),
                  ("out_norm_conv", I["out_norm_conv_2"], 4), ("out_norm_ssm", I["out_norm_ssm_2"], 4),
                  ("ffn2_norm", I["ffn2_norm_2"], 8)],
                 [("final_norm", I["final_norm_2"], 8), ("lam_re", I["lambda_re_2"], 16),
                  ("lam_im", I["lambda_im_2"], 16)]]
        VR = AR[:, 0:3 * P].rearrange("p (a n) -> p a n", a=3)
        base = 0
        pack_n = []
        for a, pk in enumerate(packs):
            r = 0
            s = sem(f"d_vec{a}")
            for name, src, n in pk:
                flat = src
                while len(flat.shape) > 1:
                    names = " ".join("abcd"[:len(flat.shape)])
                    flat = flat.rearrange(f"{names} -> ({names})")
                S.dma(nc.scalar.dma_start, VR[r:r + n, a, :], flat.rearrange("(r n) -> r n", n=P), s)
                rows[name] = (base + r, n)
                r += n
            if a == 2:
                ldt = AR[:, 3 * P:3 * P + 2]
                S.dma(nc.scalar.dma_start, ldt[r:r + 16, :] if False else AR[0:16, 384:386],
                      I["log_dt_2"].rearrange("o (j e) -> (o j) e", e=2), s)
                s_small["vec2"] = (s, 16 * (len(pk) + 1))
            else:
                s_small[f"vec{a}"] = (s, 16 * len(pk))
            base += r
            pack_n.append(r)

        def col(name, i=0, n=1):
            b, m = rows[name]
            return VC[:, b + i:b + i + n]

        XN = AR[:, 512:512 + 2048].rearrange("p (a n) -> p a n", a=2)
        small(S, nc.scalar.dma_start, "x", XN, I["x"].rearrange("o (a p) n -> p (o a) n", p=P))
        E_SWR, E_BB = 23936, 24960
        small(G, nc.gpsimd.dma_start, "sgu_w", v3(ar(E_SWR, 1024), 8),
              I["sgu_w"].rearrange("o h t s -> t (o h) s"))
        small(G, nc.gpsimd.dma_start, "sgu_b", AR[0:1, E_BB:E_BB + 1024], I["sgu_b"].rearrange("o h t -> o (h t)"))

        units = []

        def add_cols(name, W, c0, n=256, k=8):
            units.append((name, W[0:k * P, c0:c0 + n].rearrange("(k p) n -> p k n", p=P), k, n))

        def add_rows(name, W, r0):
            units.append((name, W[r0:r0 + 256, :].rearrange("(k p) n -> p k n", p=P), 2, 1024))

        def add_ffn(tag, Wg, Wu, Wd):
            for b in range(12):
                if b < 11:
                    add_cols(f"{tag}g", Wg, 256 * b)
                    add_cols(f"{tag}u", Wu, 256 * b)
                if b > 0:
                    add_rows(f"{tag}d", Wd, 256 * (b - 1))

        ew, ow, wi = I["even_in_w"][0], I["odd_in_w"][0], I["w_in_2"][0]
        for j in range(12):
            add_cols("ada0", I["ada_w"][0], 256 * j)
        for c0 in [2048 + 256 * j for j in range(4)] + [256 * j for j in range(4)]:
            add_cols("ein", ew, c0)
        for c0 in [1024 + 256 * j for j in range(4)]:
            add_cols("ein", ew, c0)
        units.append(("pool", I["pool_w"][0].rearrange("g (k p) n -> p (g k) n", p=P), 8, 256))
        for j in range(8):
            add_cols("ein", ew, 3072 + 256 * j)
        for j in range(8):
            add_rows("eout", I["even_out_w"][0], 256 * j)
        for j in range(12):
            add_cols("ada1", I["ada_w"][1], 256 * j)
        for c0 in [256 * j for j in range(8)] + [2064 + 256 * j for j in range(12)] + [5136 + 256 * j for j in range(8)]:
            add_cols("oin", ow, c0)
        for j in range(8):
            add_rows("oout", I["odd_out_w"][0], 256 * j)
        for j in range(36):
            add_cols("mod", I["w_mod_2"][0], 256 * j)
        add_ffn("f1", I["ffn1_w_gate_2"][0], I["ffn1_w_up_2"][0], I["ffn1_w_down_2"][0])
        for c0 in (1536, 1792, 512, 768, 1024, 1280, 0, 256):
            add_cols("win", wi, c0)
        add_cols("glu", I["glu_w_2"][0], 0, 512, 4)
        for j in range(4):
            add_rows("wout", I["w_out_2"][0], 256 * j)
        add_ffn("f2", I["ffn2_w_gate_2"][0], I["ffn2_w_up_2"][0], I["ffn2_w_down_2"][0])

        FP32_UNITS = ("ada0", "ada1", "mod")
        unit_free = []
        split_at = [i for i, u in enumerate(units) if u[0] not in FP32_UNITS]
        split_of = {i: k for k, i in enumerate(split_at)}
        split_tok = {}
        cur = [0]
        nsplit = [0]

        def landed(i):
            return (s_ring[i % RING], 16 * (i // RING + 1))

        def split_to(i):
            while nsplit[0] < len(split_at) and split_at[nsplit[0]] <= i:
                k = nsplit[0]
                u = split_at[k]
                if k >= NLO:
                    V.wait(unit_free[split_at[k - NLO]])
                V.wait(landed(u))
                slot = ring[:, u % RING, :]
                hi = slot.bitcast(BF16).rearrange("p (n two) -> p n two", two=2)[:, :, 1]
                split_tok[u] = V.do(tt, lo[:, k % NLO, :], slot, hi, SUB)
                nsplit[0] += 1

        class Unit:
            def __init__(self, name):
                i = cur[0]
                cur[0] += 1
                nm, _, k, n = units[i]
                assert nm == name, (nm, name, i)
                assert len(unit_free) == i
                self.i = i
                slot = ring[:, i % RING, :]
                self.w = v3(slot, k)
                self.hi = slot.bitcast(BF16).rearrange("p (k n two) -> p k n two", k=k, two=2)[:, :, :, 1]
                if name not in FP32_UNITS:
                    split_to(i)
                    self.lo = v3(lo[:, split_of[i] % NLO, :], k)
                    PE.wait(split_tok[i])
                PE.wait(landed(i))

            def done(self, tok):
                unit_free.append(tok)
                split_to(self.i + 1)

        def mm3(o, a, b, start, stop):
            PE.quiet(mm, o, a[0], b[0], start=start, stop=False, skip_group_check=True)
            PE.quiet(mm, o, a[0], b[1], start=False, stop=False, skip_group_check=True)
            return PE.do(mm, o, a[1], b[0], start=False, stop=stop, skip_group_check=True)

        def mmf(o, a, b, start=True, stop=True):
            return PE.do(mm, o, a, b, start=start, stop=stop, skip_group_check=True)

        wfree = [[] for _ in range(4)]
        nbank = [0]

        def bank():
            i = nbank[0] % 4
            nbank[0] += 1
            PE.wait(*wfree[i])
            wfree[i] = None
            return i, pw[i]

        def free(i, *toks):
            wfree[i] = list(toks)

        def pair(src, dh, dl, toks, free_toks=()):
            S.wait(*toks, *free_toks)
            a = S.do(act, dh, src, ACT.Copy)
            V.wait(*toks, a, *free_toks)
            return V.do(tt, dl, src, dh, SUB)

        def rsqrt(dst, src, scale, toks, tmp):
            v, t = tmp
            V.wait(*toks)
            a = V.do(ts, v, src, scale, EPS, MUL, ADD)
            S.wait(a)
            b = S.do(act, t, v, ACT.Ln)
            S.wait(b)
            b = S.do(act, dst, t, ACT.Exp, scale=-0.5)
            V.wait(b, a)
            c = V.do(tt, t, dst, dst, MUL)
            V.wait(c)
            c = V.do(tt, t, t, v, MUL)
            V.wait(c)
            c = V.do(ts, t, t, -0.5, 1.5, MUL, ADD)
            V.wait(c)
            return a, V.do(tt, dst, dst, t, MUL)

        sq_free = [[], [], [], []]
        nsq = [0]

        def sumsq(o, tiles, toks, start=True):
            for k, (x, tk) in enumerate(zip(tiles, toks)):
                i = nsq[0] % 4
                nsq[0] += 1
                S.wait(*sq_free[i], *tk)
                a = S.do(act, SQT[:, i, :], x, ACT.Square)
                PE.wait(a)
                r = mmf(o, ones, SQT[:, i, :], start and k == 0, k == len(tiles) - 1)
                sq_free[i] = [r]
            return r

        rt_last = []

        def norm_r(tiles, toks, n):
            b, pb = bank()
            r = sumsq(pb[:, 0:T], tiles, toks)
            V.wait(*rt_last)
            a, z = rsqrt(RT[:, 0, :], pb[:, 0:T], 1.0 / n, [r], (RT[:, 1, :], RT[:, 2, :]))
            free(b, a)
            return z

        x_tok = [[] for _ in range(8)]
        h_free = []

        def norm_mod(gs, sh, toks):
            r = norm_r([xT[:, k, :] for k in range(8)], x_tok, D)
            del rt_last[:]
            res = []
            for k in range(8):
                i = nsq[0] % 4
                nsq[0] += 1
                V.wait(r, *toks, *sq_free[i])
                a = V.do(tt, SQT[:, i, :], xT[:, k, :], RT[:, 0, :], MUL)
                V.wait(a)
                a = V.do(ts, SQT[:, i, :], SQT[:, i, :], gs[:, k:k + 1], sh[:, k:k + 1], MUL, ADD)
                c = pair(SQT[:, i, :], hh[:, k, :], hl[:, k, :], [a], h_free)
                sq_free[i] = [c]
                res.append(c)
            rt_last.append(res[-1])
            del h_free[:]
            return res

        def hpair(k, sl=slice(0, T)):
            return (hh[:, k, sl], hl[:, k, sl])

        acc_free = []
        acc_on = [False]

        def acc_rows(u, act_pair, first, last):
            if first:
                PE.wait(*acc_free)
            for k in range(2):
                yh, yl = act_pair(k)
                for n in range(8):
                    sl = slice(n * P, n * P + P)
                    tk = mm3(pacc[:, n, :], (u.hi[:, k, sl], u.lo[:, k, sl]), (yh, yl),
                             first and k == 0 and n % 2 == 0, last and k == 1)
            u.done(tk)
            return tk

        def residual(gate, tk, gtoks):
            del acc_free[:]
            for n in range(8):
                V.wait(tk, *gtoks, *x_tok[n], *rt_last)
                a = V.do(stt, out=xT[:, n, :], in0=pacc[:, n, :], scalar=gate[:, n:n + 1], in1=xT[:, n, :],
                         op0=MUL, op1=ADD)
                x_tok[n] = [a]
            acc_free.append(a)

        def ada(name, n_units, csil, dst, bias, toks):
            b, pb = bank()
            PE.wait(*toks)
            for j in range(n_units):
                u = Unit(name)
                for m in range(2):
                    o = 2 * j + m
                    for k in range(8):
                        tk = mmf(pb[:, o:o + 1], u.w[:, k, m * P:m * P + P], csil[:, k:k + 1], k == 0, k == 7)
                u.done(tk)
            V.wait(tk)
            r = V.do(tt, dst, pb[:, 0:2 * n_units], bias, ADD)
            free(b, r)
            return r

        def cols_T(u, banks_of, evac):
            b, pb = bank()
            for m in range(2):
                for k in range(8):
                    tk = mm3(pb[:, m * T:m * T + T], (u.hi[:, k, m * P:m * P + P], u.lo[:, k, m * P:m * P + P]),
                             hpair(k), k == 0 , k == 7)
            u.done(tk)
            free(b, *evac(pb, tk))
            return tk

        def cols_N(u, dst, dtoks):
            b, pb = bank()
            for m in range(2):
                for k in range(8):
                    tk = mm3(pb[:, m * T:m * T + T], hpair(k, slice(m * P, m * P + P)),
                             (u.hi[:, k, :], u.lo[:, k, :]), k == 0, k == 7)
            u.done(tk)
            S.wait(tk, *dtoks)
            r = S.do(act, dst, v3(pb[:, :], 2), ACT.Copy)
            free(b, r)
            return r

        def silu_bank(pb, tk, e, dst, toks, n=512):
            S.wait(tk, *toks)
            a = S.do(act, e, pb[:, 0:n], ACT.Exp, scale=-1.0)
            V.wait(a)
            a = V.do(ts, e, e, 1.0, None, ADD)
            V.wait(a)
            a = V.do(nc.vector.reciprocal, e, e)
            V.wait(a, *toks)
            return V.do(tt, dst, pb[:, 0:n], e, MUL)

        PE.wait(s_small["cst"], s_small["vec0"], s_small["vec1"], s_small["vec2"])
        b, pb = bank()
        base = 0
        for a, n in enumerate(pack_n):
            tk = PE.do(tr, pb[:, base:base + n], VR[0:n, a, :], ident[0:n, 0:n])
            base += n
        V.wait(tk)
        vc_tok = V.do(nc.vector.tensor_copy, VC[:, 0:base], pb[:, 0:base])
        free(b, vc_tok)
        DTC = PC[:, 0:16]
        dtr = AR[0:16, 400:528]
        V.wait(s_small["vec2"])
        a = V.do(nc.vector.tensor_copy, AR[0:16, 2560:2688].rearrange("p (e n) -> p e n", e=2),
                 AR[0:16, 384:386].unsqueeze(2).to_broadcast([16, 2, 64]))
        b, pb = bank()
        PE.wait(a)
        tk = PE.do(tr, pb[:, 0:16], AR[0:16, 2560:2688], ident[0:16, 0:16])
        S.wait(tk)
        dt_tok = S.do(act, DTC, pb[:, 0:16], ACT.Exp)
        free(b, dt_tok)

        SIL = PC[:, 16:32]
        sil_e = PC[:, 32:48]
        S.wait(vc_tok)
        a = S.do(act, sil_e[:, 0:8], col("c", 0, 8), ACT.Exp, scale=-1.0)
        a = S.do(act, sil_e[:, 8:16], col("cond", 0, 8), ACT.Exp, scale=-1.0)
        V.wait(a)
        a = V.do(ts, sil_e, sil_e, 1.0, None, ADD)
        V.wait(a)
        a = V.do(nc.vector.reciprocal, sil_e, sil_e)
        V.wait(a)
        a = V.do(tt, SIL[:, 0:8], sil_e[:, 0:8], col("c", 0, 8), MUL)
        sil_tok = V.do(tt, SIL[:, 8:16], sil_e[:, 8:16], col("cond", 0, 8), MUL)

        PE.wait(s_small["x"])
        for q in range(4):
            b, pb = bank()
            for kk in range(2):
                k = 2 * q + kk
                for m in range(2):
                    tk = PE.do(tr, pb[:, kk * T + m * P:kk * T + m * P + P], XN[:, m, k * P:k * P + P], ident)
            S.wait(tk)
            r = S.do(act, xT[:, 2 * q:2 * q + 2, :], v3(pb[:, :], 2), ACT.Copy)
            free(b, r)
            x_tok[2 * q] = [r]
            x_tok[2 * q + 1] = [r]
        start_done = tk

        PE.wait(s_small["sgu_w"], s_small["sgu_b"])
        E_SWT = 22912
        swT = v3(ar(E_SWT, 1024), 8)
        swR = v3(ar(E_SWR, 1024), 8)
        ptok = []
        for q in range(2):
            b, pb = bank()
            for m in range(4):
                tk = PE.do(tr, pb[:, m * P:m * P + P], swR[:, 4 * q + m, :], ident)
            S.wait(tk)
            r = S.do(act, swT[:, 4 * q:4 * q + 4, :], v3(pb[:, :], 4), ACT.Copy)
            free(b, r)
            ptok.append(r)
        sw_tr = tk
        G.wait(*ptok)
        swt_tok = G.do(nc.gpsimd.affine_select, out=swT, in_=swT, compare_op=ALU.is_ge, fill=0.0, base=0,
                       pattern=[[0, 8], [1, P]], channel_multiplier=-1)
        bB = ar(E_BB, 1024)
        pend = []
        for q in range(2):
            b, pb = bank()
            tk = mmf(pb[:, :], ones[0:1, :], AR[0:1, E_BB + 512 * q:E_BB + 512 * q + 512])
            pend.append((b, pb, tk))
        for q, (b, pb, tk) in enumerate(pend):
            S.wait(pend[-1][2])
            bb_tok = S.do(act, bB[:, 512 * q:512 * q + 512], pb[:, :], ACT.Copy)
            free(b, bb_tok)

        def mod_cols(m, gname, goff, dst, toks):
            V.wait(*toks)
            return V.do(stt, out=dst, in0=m[:, 8:16], scalar=1.0, in1=col(gname, goff, 8), op0=ADD, op1=MUL)

        M0, M1, M2 = MOD[:, 0:24], MOD[:, 24:48], MOD[:, 48:120]
        GS = PC[:, 48:56]
        m0_tok = ada("ada0", 12, SIL[:, 0:8], M0, col("ada_b", 0, 24), [sil_tok])
        g_tok = mod_cols(M0, "norm_g", 0, GS, [m0_tok])
        hp = norm_mod(GS, M0[:, 0:8], [g_tok, m0_tok])

        GT = v3(ar(0, 4096), 16)
        YH = v3(arb(4096, 4096), 16)
        YL = v3(arb(6144, 4096), 16)
        VV = v3(ar(8192, 2048), 2)
        UU = v3(ar(10240, 2048), 8)
        AP_ = v3(ar(12288, 2176), 8)
        S1 = v3(ar(14464, 2176), 8)
        S2 = v3(ar(16640, 2176), 8)
        PH = v3(arb(18816, 2048), 8)
        PL = v3(arb(19840, 2048), 8)
        YP = v3(ar(20864, 2048), 8)
        TMP = [ar(23936, 512), ar(24448, 512)]

        pads = []
        G.wait(start_done)
        for buf in (AP_, S1, S2):
            pads.append(G.do(nc.gpsimd.memset, buf[:, :, 0:16], 0.0))

        PE.wait(*hp)
        for j in range(4):
            r = cols_N(Unit("ein"), VV[:, :, 256 * j:256 * j + 256], [start_done])
        for m in range(2):
            S.wait(r)
            a = S.do(act, YP[:, 4 * m:4 * m + 4, :].rearrange("p a n -> p (a n)"), VV[:, m, :], ACT.Square,
                     accum_out=PC[:, 56 + m:57 + m])
        rs_t = (PC[:, 60:62], PC[:, 62:64])
        _, rs = rsqrt(PC[:, 58:60], PC[:, 56:58], 1.0 / D, [a], rs_t)
        vh_tok = []
        for m in range(2):
            V.wait(rs, r)
            vh_tok.append(V.do(ts, VV[:, m, :], VV[:, m, :], PC[:, 58 + m:59 + m], None, MUL))

        a_tok = []
        for j in range(4):
            def ev(pb, tk, j=j):
                S.wait(tk, start_done)
                r = S.do(act, AP_[:, 2 * j:2 * j + 2, 16:272], v3(pb[:, :], 2), ACT.Copy)
                a_tok.append(r)
                return [r]
            cols_T(Unit("ein"), None, ev)

        V.wait(*a_tok, *pads)
        p_tok = []
        src, toks = AP_, []
        for g, w in enumerate((2, 4, 8, 16)):
            dst = (S1, S2)[g % 2]
            half = w // 2
            V.wait(*toks)
            a = V.do(tt, dst[:, 2 * g:8, 16:272], src[:, 2 * g:8, 16:272], src[:, 2 * g:8, 16 - half:272 - half], ADD)
            V.wait(a)
            z = AP_[:, 2 * g:2 * g + 2, :]
            w_ = dst[:, 2 * g:2 * g + 2, :]
            y = YP[:, 2 * g:2 * g + 2, :]
            b1 = V.do(stt, out=y, in0=w_[:, :, 16:272], scalar=1.0 / w, in1=z[:, :, 16:272], op0=MUL, op1=SUB)
            V.wait(b1)
            b2 = V.do(tt, y[:, :, 0:16], w_[:, :, 16:32], ic[:, 2 * g:2 * g + 2, :], MUL)
            V.wait(b2)
            b3 = V.do(tt, y[:, :, 0:16], y[:, :, 0:16], z[:, :, 16:32], SUB)
            p_tok.append(pair(y, PH[:, 2 * g:2 * g + 2, :], PL[:, 2 * g:2 * g + 2, :], [b3]))
            toks = [a]
            src = dst

        u_tok = []
        for j in range(4):
            def ev(pb, tk, j=j):
                S.wait(tk, start_done)
                r = S.do(act, UU[:, 2 * j:2 * j + 2, :], v3(pb[:, :], 2), ACT.Copy)
                u_tok.append(r)
                return [r]
            cols_T(Unit("ein"), None, ev)

        u = Unit("pool")
        yp_tok = []
        for g in range(4):
            PE.wait(p_tok[g])
            b, pb = bank()
            for m in range(2):
                for k in range(2):
                    kk = 2 * g + k
                    tk = mm3(pb[:, m * T:m * T + T], (u.hi[:, kk, m * P:m * P + P], u.lo[:, kk, m * P:m * P + P]),
                             (PH[:, kk, :], PL[:, kk, :]), k == 0, k == 1)
            for m in range(2):
                n = 2 * g + m
                S.wait(tk, p_tok[g])
                r = S.do(act, YP[:, n, :], pb[:, m * T:m * T + T], ACT.Copy, scale=col("pool_scale", n))
            yp_tok.append(r)
            free(b, r)
        u.done(tk)

        PE.wait(*vh_tok, swt_tok)
        z_tok = []
        for q in range(4):
            b, pb = bank()
            for m in range(2):
                h = 2 * q + m
                for n in range(2):
                    tk = mmf(pb[:, m * T + n * P:m * T + n * P + P], VV[:, n, h * P:h * P + P], swT[:, h, :])
            for m in range(2):
                h = 2 * q + m
                V.wait(tk, bb_tok, *u_tok, sw_tr)
                a = V.do(stt, out=v3(TMP[m][:, 0:T], 2), in0=v3(pb[:, m * T:m * T + T], 2),
                         scalar=col("sgu_norm_g", h),
                         in1=bB[:, h * P:h * P + P].unsqueeze(1).to_broadcast([P, 2, P]), op0=MUL, op1=ADD)
                V.wait(a)
                r = V.do(tt, UU[:, h, :], TMP[m][:, 0:T], UU[:, h, :], MUL)
            z_tok.append(r)
            free(b, a)

        y_tok = []
        for j in range(8):
            def ev(pb, tk, j=j):
                e = TMP[j % 2]
                g2 = GT[:, 2 * j:2 * j + 2, :].rearrange("p a n -> p (a n)")
                r = silu_bank(pb, tk, e, g2, [z_tok[-1]] + y_tok[-2:])
                V.wait(r, *yp_tok)
                other = YP[:, 2 * j:2 * j + 2, :] if j < 4 else UU[:, 2 * j - 8:2 * j - 6, :]
                a = V.do(tt, g2, g2, other.rearrange("p a n -> p (a n)"), MUL)
                y_tok.append(pair(g2, YH[:, 2 * j:2 * j + 2, :].rearrange("p a n -> p (a n)"),
                                  YL[:, 2 * j:2 * j + 2, :].rearrange("p a n -> p (a n)"), [a]))
                return [r]
            last_h = cols_T(Unit("ein"), None, ev)
        h_free.append(last_h)

        for j in range(8):
            PE.wait(y_tok[j])
            tk = acc_rows(Unit("eout"), lambda k, j=j: (YH[:, 2 * j + k, :], YL[:, 2 * j + k, :]), j == 0, j == 7)
        residual(M0[:, 16:24], tk, [m0_tok])
        even_done = tk

        m1_tok = ada("ada1", 12, SIL[:, 0:8], M1, col("ada_b", 24, 24), [sil_tok])
        GLRW = v3(ar(8192, 128), 8)
        GLRL = v3(arb(8320, 128), 8)
        GLW = AR[0:16, 8448:8960]
        G.wait(even_done)
        small(G, nc.gpsimd.dma_start, "glr", GLRW, ow[:, 2048:2064].rearrange("(k p) n -> p k n", p=P))
        small(G, nc.gpsimd.dma_start, "glw", GLW, I["gla_gate_w"][0])
        SM = 18432
        V.wait(hp[-1])
        g_tok = mod_cols(M1, "norm_g", 8, GS, [m1_tok])
        hp = norm_mod(GS, M1[:, 0:8], [g_tok, m1_tok])
        PE.wait(*hp)

        ao = even_done
        GV = v3(ar(8192, 2048), 2)
        SQ_ = v3(ar(10240, 2048), 8)
        SK_ = v3(ar(12288, 2048), 8)
        SV_ = v3(ar(14336, 2048), 2)
        GQ, GK = ar(16384, 1024), ar(17408, 1024)
        T0, T1, T2, T3, T4, T5 = (ar(18432 + 1024 * i, 1024) for i in range(6))

        V.wait(s_small["glr"])
        hi16 = GLRW.rearrange("p a n -> p (a n)").bitcast(BF16).rearrange("p (a n two) -> p a n two", a=8, two=2)[:, :, :, 1]
        a = V.do(tt, GLRL, GLRW, hi16, SUB)
        b, pb = bank()
        PE.wait(a)
        for k in range(8):
            tk = mm3(pb[0:16, 0:T], (hi16[:, k, :], GLRL[:, k, :]), hpair(k), k == 0, k == 7)
        GLT = AR[0:16, 8960:9216]
        S.wait(tk, ao)
        a = S.do(act, GLT, pb[0:16, 0:T], ACT.Copy)
        free(b, a)
        PE.wait(a, s_small["glw"])
        la_tok = []
        for q in range(2):
            b, pb = bank()
            for m in range(2):
                h = 2 * q + m
                tk = mmf(pb[:, m * T:m * T + T], GLW[:, h * P:h * P + P], GLT)
            glr_done = tk
            for m in range(2):
                h = 2 * q + m
                src = pb[:, m * T:m * T + T]
                e, la = T4[:, h * T:h * T + T], T0[:, h * T:h * T + T]
                S.wait(tk, ao)
                a = S.do(act, e, src, ACT.Abs, bias=col("gla_gate_b", h))
                S.wait(a)
                c = S.do(act, e, e, ACT.Exp, scale=-1.0)
                S.wait(c)
                c = S.do(act, e, e, ACT.Ln, bias=one_c)
                V.wait(a, ao)
                d = V.do(ts, la, src, col("gla_gate_b", h), 0.0, ADD, MIN)
                V.wait(d, c)
                la_tok.append(V.do(tt, la, la, e, SUB))
                S.wait(d)
            free(b, d, a)
        G.wait(ao)
        a = G.do(nc.gpsimd.memset, T5, 1.0)
        G.wait(a)
        a = G.do(nc.gpsimd.memset, T5.rearrange("p (c n) -> p c n", n=64)[:, :, 0:1], 0.0)
        V.wait(a, *la_tok)
        bc_tok = V.do(nc.vector.tensor_tensor_scan, T1, T5, T0, 0.0, MUL, ADD)
        BC = T1.rearrange("p (c n) -> p c n", n=64)
        EBL = PC[:, 32:48]
        S.wait(bc_tok)
        ebl_tok = S.do(act, EBL.unsqueeze(2), BC[:, :, 63:64], ACT.Exp, scale=1.0 / 16)
        e1 = S.do(act, T0, T1, ACT.Exp, scale=1.0 / 16)
        e2 = S.do(act, T2, T1, ACT.Exp, scale=-1.0 / 16)
        V.wait(bc_tok)
        dd = V.do(tt, T3.rearrange("p (c n) -> p c n", n=64), BC[:, :, 63:64].to_broadcast([P, 16, 64]), BC, SUB)
        S.wait(dd)
        e3 = S.do(act, T3, T3, ACT.Exp, scale=1.0 / 16)

        qk_tok = []
        for j in range(4):
            def ev(pb, tk, j=j):
                dst = (GQ if j < 2 else GK)[:, (j % 2) * 512:(j % 2) * 512 + 512]
                S.wait(tk, ao)
                r = S.do(act, dst, pb[:, :], ACT.Copy, scale=float(P) ** -0.5 if j < 2 else 1.0)
                qk_tok.append(r)
                return [r]
            cols_T(Unit("oin"), None, ev)
        V.wait(*qk_tok, e1, e2, e3)
        qd = V.do(tt, GQ, GQ, T0, MUL)
        ki = V.do(tt, T2, T2, GK, MUL)
        ke = V.do(tt, T3, T3, GK, MUL)
        for j in range(4):
            gv_tok = cols_N(Unit("oin"), GV[:, :, 256 * j:256 * j + 256], [ao, glr_done])

        PE.wait(ke, ki, qd)
        att_tok, kt_tok = [], []
        AT = T5.rearrange("p (b h t) -> p b h t", b=2, h=4)
        KT = T4.rearrange("p (b h t) -> p b h t", b=2, h=4)
        for blk in range(2):
            b, pb = bank()
            for h in range(4):
                sl = slice(h * T + blk * P, h * T + blk * P + P)
                tk = mmf(pb[:, h * P:h * P + P], T2[:, sl], GQ[:, sl])
            S.wait(tk, bc_tok)
            r = S.do(act, AT[:, blk], v3(pb[:, :], 4), ACT.Copy)
            free(b, r)
            G.wait(r)
            r = G.do(nc.gpsimd.affine_select, out=AT[:, blk], in_=AT[:, blk], compare_op=ALU.is_ge, fill=0.0,
                     base=0, pattern=[[0, 4], [1, P]], channel_multiplier=-1)
            G.wait(r)
            r = G.do(nc.gpsimd.memset, AT[0:64, blk, :, 64:128], 0.0)
            att_tok.append(r)
            b, pb = bank()
            for h in range(4):
                sl = slice(h * T + blk * P, h * T + blk * P + P)
                tk = PE.do(tr, pb[:, h * P:h * P + P], T3[:, sl], ident)
            S.wait(tk, *la_tok)
            r = S.do(act, KT[:, blk], v3(pb[:, :], 4), ACT.Copy)
            free(b, r)
            kt_tok.append(r)
        t3_done = tk

        ST = [v3(GK, 4), v3(T0, 4), v3(T1, 4)]
        PE.wait(*kt_tok, gv_tok)
        st_tok = []
        prev = None
        for c in range(3):
            rr = slice(64 * (c % 2), 64 * (c % 2) + 64)
            cur_t = []
            for q in range(2):
                b, pb = bank()
                for m in range(2):
                    h = 2 * q + m
                    tk = mmf(pb[:, m * T:m * T + T], KT[rr, c // 2, h, :], GV[rr, c // 2, h * T:h * T + T])
                for m in range(2):
                    h = 2 * q + m
                    V.wait(tk, ke, qd, dd, ebl_tok, e3, e1, e2)
                    if c == 0:
                        r = V.do(nc.vector.tensor_copy, ST[0][:, h, :], pb[:, m * T:m * T + T])
                    else:
                        V.wait(*prev)
                        r = V.do(stt, out=ST[c][:, h, :], in0=ST[c - 1][:, h, :],
                                 scalar=EBL[:, 4 * h + c:4 * h + c + 1], in1=pb[:, m * T:m * T + T],
                                 op0=MUL, op1=ADD)
                    cur_t.append(r)
                free(b, r)
            prev = cur_t
            st_tok.append(cur_t)

        YC = ar(20480, 2048).rearrange("p (a n) -> p a n", a=8)
        PE.wait(*att_tok)
        yc_tok = []
        for h in range(4):
            b, pb = bank()
            for v in range(2):
                for blk in range(2):
                    tk = mmf(pb[:, v * T + blk * P:v * T + blk * P + P], GV[:, blk, h * T + v * P:h * T + v * P + P],
                             AT[:, blk, h, :], start=(v == 0 and blk == 0), stop=False)
            for v in range(2):
                for c in range(1, 4):
                    PE.wait(*st_tok[c - 1])
                    tk = mmf(pb[:, v * T + 64 * c:v * T + 64 * c + 64], ST[c - 1][:, h, v * P:v * P + P],
                             GQ[:, h * T + 64 * c:h * T + 64 * c + 64], start=False, stop=(c == 3))
            S.wait(tk, t3_done)
            r = S.do(act, YC[:, 2 * h:2 * h + 2, :], v3(pb[:, :], 2), ACT.Copy)
            free(b, r)
            yc_tok.append(r)
        gla_pe = tk
        RG = ar(18432, 1024)
        RGV = T4
        RGT = T5
        for q in range(2):
            b, pb = bank()
            for m in range(2):
                h = 2 * q + m
                tk = sumsq(pb[:, m * T:m * T + T], [YC[:, 2 * h, :], YC[:, 2 * h + 1, :]], [[yc_tok[h]]] * 2)
            S.wait(gla_pe)
            a, z = rsqrt(RG[:, 512 * q:512 * q + 512], pb[:, :], 1.0 / 256, [tk, gla_pe],
                         (RGV[:, 512 * q:512 * q + 512], RGT[:, 512 * q:512 * q + 512]))
            free(b, a)
            for m in range(2):
                h = 2 * q + m
                for v in range(2):
                    n = 2 * h + v
                    V.wait(z)
                    ycn = V.do(stt, out=YC[:, n, :], in0=YC[:, n, :], scalar=col("gla_norm_g", n),
                               in1=RG[:, h * T:h * T + T], op0=MUL, op1=MUL)

        sqk_tok = []
        for j in range(8):
            def ev(pb, tk, j=j):
                jj = j % 4
                dst = (SQ_ if j < 4 else SK_)[:, 2 * jj:2 * jj + 2, :]
                S.wait(tk, ao)
                r = S.do(act, dst, v3(pb[:, :], 2), ACT.Copy, scale=float(P) ** -0.5 if j < 4 else 1.0)
                sqk_tok.append(r)
                return [r]
            cols_T(Unit("oin"), None, ev)
        for j in range(4):
            sv_tok = cols_N(Unit("oin"), SV_[:, :, 256 * j:256 * j + 256], [ao])
        GT = v3(ar(0, 4096), 16)
        g_toks = []
        for j in range(8):
            def ev(pb, tk, j=j):
                g2 = GT[:, 2 * j:2 * j + 2, :].rearrange("p a n -> p (a n)")
                e = ar(24576 + 512 * (j % 2), 512)
                r = silu_bank(pb, tk, e, g2, [ao] + g_toks[-2:])
                g_toks.append(r)
                return [r]
            last_h = cols_T(Unit("oin"), None, ev)
        h_free.append(last_h)

        y_tok = []
        for j in range(4):
            g2 = GT[:, 2 * j:2 * j + 2, :].rearrange("p a n -> p (a n)")
            V.wait(g_toks[j], ycn)
            a = V.do(tt, g2, g2, YC[:, 2 * j:2 * j + 2, :].rearrange("p a n -> p (a n)"), MUL)
            y_tok.append(pair(g2, YH[:, 2 * j:2 * j + 2, :].rearrange("p a n -> p (a n)"),
                              YL[:, 2 * j:2 * j + 2, :].rearrange("p a n -> p (a n)"), [a], [ao]))

        PE.wait(*sqk_tok, sv_tok)
        sb_free = [[g_toks[-1]], [g_toks[-1]]]
        heads = []

        def sb_scores(h):
            b, pb = bank()
            mmf(pb[:, 0:256], SK_[:, h, 0:128], SQ_[:, h, :], True, True)
            tk = mmf(pb[:, 256:384], SK_[:, h, 128:256], SQ_[:, h, 128:256], False, True)
            o = 24576 + 1152 * (h % 2)
            e, sp, w = ar(o, 384), ar(o + 384, 384), ar(o + 768, 384)
            S.wait(tk, *sb_free[h % 2])
            a = S.do(act, e, pb[:, 0:384], ACT.Abs)
            S.wait(a)
            c = S.do(act, e, e, ACT.Exp, scale=-1.0)
            S.wait(c)
            c = S.do(act, e, e, ACT.Ln, bias=one_c)
            V.wait(c, *sb_free[h % 2])
            d = V.do(stt, out=sp, in0=pb[:, 0:384], scalar=0.0, in1=e, op0=MAX, op1=ADD)
            G.wait(d)
            for o2 in (0, 256):
                m = G.do(nc.gpsimd.affine_select, out=sp[:, o2:o2 + P], in_=sp[:, o2:o2 + P], compare_op=ALU.is_gt,
                         fill=0.0, base=0, pattern=[[1, P]], channel_multiplier=-1)
            return b, pb, sp, w, m, d, a

        def sb_weights(st):
            b, pb, sp, w, m, d, a = st
            PE.wait(m, d, a)
            mmf(pb[:, 0:256], negU, sp[:, 0:256], False, False)
            mmf(pb[:, 128:256], negones, sp[:, 256:384], False, False)
            tk = mmf(pb[:, 256:384], negU, sp[:, 256:384], False, True)
            S.wait(tk)
            r = S.do(act, w, pb[:, 0:384], ACT.Exp)
            free(b, r)
            G.wait(r)
            for o2 in (0, 256):
                m = G.do(nc.gpsimd.affine_select, out=w[:, o2:o2 + P], in_=w[:, o2:o2 + P], compare_op=ALU.is_gt,
                         fill=0.0, base=0, pattern=[[1, P]], channel_multiplier=-1)
            return w, m, r

        def sb_out(h, w, m, r, pb, half):
            PE.wait(m, r)
            o = pb[:, half * T:half * T + T]
            mmf(o, SV_[:, 0, h * P:h * P + P], w[:, 0:256], half == 0, False)
            tk = mmf(o[:, 128:256], SV_[:, 1, h * P:h * P + P], w[:, 256:384], False, True)
            sb_free[h % 2] = [tk]
            return tk

        for q in range(4):
            s0 = sb_scores(2 * q)
            s1 = sb_scores(2 * q + 1)
            w0 = sb_weights(s0)
            w1 = sb_weights(s1)
            b, pb = bank()
            sb_out(2 * q, *w0, pb, 0)
            tk = sb_out(2 * q + 1, *w1, pb, 1)
            j = 4 + q
            g2 = GT[:, 2 * j:2 * j + 2, :].rearrange("p a n -> p (a n)")
            V.wait(tk, g_toks[j])
            a = V.do(tt, g2, g2, pb[:, :], MUL)
            free(b, a)
            y_tok.append(pair(g2, YH[:, 2 * j:2 * j + 2, :].rearrange("p a n -> p (a n)"),
                              YL[:, 2 * j:2 * j + 2, :].rearrange("p a n -> p (a n)"), [a], [ao]))

        for j in range(8):
            PE.wait(y_tok[j])
            tk = acc_rows(Unit("oout"), lambda k, j=j: (YH[:, 2 * j + k, :], YL[:, 2 * j + k, :]), j == 0, j == 7)
        residual(M1[:, 16:24], tk, [m1_tok])
        odd_done = tk

        m2_tok = ada("mod", 36, SIL[:, 8:16], M2, col("b_mod", 0, 72), [sil_tok])
        r = norm_r([xT[:, k, :] for k in range(8)], x_tok, D)
        for k in range(8):
            V.wait(r, *x_tok[k])
            a = V.do(stt, out=xT[:, k, :], in0=xT[:, k, :], scalar=col("final_g", k), in1=RT[:, 0, :],
                     op0=MUL, op1=MUL)
            x_tok[k] = [a]
        rt_last.append(a)

        ao = odd_done
        COS = v3(ar(4096, 4096), 16)
        SIN = v3(ar(8192, 4096), 16)
        BT = [v3(ar(12288 + 512 * i, 512), 4) for i in range(2)]
        CT = [v3(ar(13312 + 512 * i, 512), 4) for i in range(3)]
        BR = [v3(ar(14848 + 256 * i, 256), 16) for i in range(2)]
        BB = [v3(ar(15360 + 512 * i, 512), 16) for i in range(2)]
        CR = [v3(ar(16384 + 256 * i, 256), 4) for i in range(2)]
        CM = [ar(16896 + 512 * i, 512) for i in range(2)]
        LC = v3(ar(26632, 16 * 12), 12)
        S5T = [ar(18432 + 256 * i, 256) for i in range(3)]
        G.wait(ao)
        for i, nm in enumerate(("ssm_b_re_2", "ssm_b_im_2")):
            small(G, nc.gpsimd.dma_start, nm, BR[i], I[nm].rearrange("o (j e) p c -> (o e p) j c", e=2)
                  if False else I[nm][0].rearrange("(j e) p c -> (e p) j c", e=2))
        for i, nm in enumerate(("ssm_c_re_2", "ssm_c_im_2")):
            small(G, nc.gpsimd.dma_start, nm, CR[i], I[nm][0].rearrange("(m g) c p -> (g c) m p", g=8))

        def s5_coefs():
            lre, lim = col("lam_re", 0, 16), col("lam_im", 0, 16)
            A_, TH, RR, SN, CN, T1_, T2_, T3_, CFR, CFI, X1, X2 = (LC[:, i, :] for i in range(12))
            V.wait(dt_tok, vc_tok, ao)
            a = V.do(tt, A_, lre, DTC, MUL)
            a = V.do(tt, TH, lim, DTC, MUL)
            S.wait(a)
            rr = S.do(act, RR, A_, ACT.Exp)
            V.wait(a)
            a = V.do(ts, T1_, TH, 1.0 / TWO_PI, MAGIC, MUL, ADD)
            V.wait(a)
            a = V.do(ts, T1_, T1_, MAGIC, None, SUB)
            V.wait(a)
            a = V.do(stt, out=TH, in0=T1_, scalar=-TP_HI, in1=TH, op0=MUL, op1=ADD)
            V.wait(a)
            a = V.do(stt, out=TH, in0=T1_, scalar=-TP_LO, in1=TH, op0=MUL, op1=ADD)
            V.wait(a)
            a = V.do(ts, TH, TH, float(np.pi), -float(np.pi), MIN, MAX)
            S.wait(a)
            sn = S.do(act, SN, TH, ACT.Sin)
            c = S.do(act, CN, TH, ACT.Abs)
            S.wait(c)
            cn = S.do(act, CN, CN, ACT.Sin, scale=-1.0, bias=hpi_c)
            V.wait(sn, cn, rr)
            a = V.do(tt, CN, CN, RR, MUL)
            b_ = V.do(tt, SN, SN, RR, MUL)
            V.wait(a, b_)
            a = V.do(ts, CN, CN, 1.0, None, SUB)
            c = V.do(tt, T2_, lre, lre, MUL)
            d = V.do(tt, T3_, lim, lim, MUL)
            V.wait(a, c, d)
            a = V.do(tt, T2_, T2_, T3_, ADD)
            V.wait(a)
            a = V.do(nc.vector.reciprocal, T2_, T2_)
            c = V.do(tt, X1, CN, lre, MUL)
            d = V.do(tt, X2, SN, lim, MUL)
            V.wait(c, d, a)
            c = V.do(tt, CFR, X1, X2, ADD)
            V.wait(c)
            d = V.do(tt, X1, SN, lre, MUL)
            e = V.do(tt, X2, CN, lim, MUL)
            V.wait(d, e)
            d = V.do(tt, CFI, X1, X2, SUB)
            V.wait(d, c)
            c = V.do(tt, CFR, CFR, T2_, MUL)
            d = V.do(tt, CFI, CFI, T2_, MUL)
            return RR, TH, CFR, CFI, [c, d]

        def s5_blocks(CFR, CFI, cf_tok):
            bd = lambda x: x.unsqueeze(2).to_broadcast([P, 16, 16])
            t = [v3(S5T[i], 16) for i in range(3)]
            G.wait(ao)
            z = [G.do(nc.gpsimd.memset, BB[i].rearrange("p a n -> p (a n)"), 0.0) for i in range(2)]
            V.wait(s_small["ssm_b_re_2"], s_small["ssm_b_im_2"], *cf_tok, *z)
            a = V.do(tt, t[0], BR[0], bd(CFR), MUL)
            b_ = V.do(tt, t[1], BR[1], bd(CFI), MUL)
            V.wait(a, b_)
            for e in range(2):
                r = slice(64 * e, 64 * e + 64)
                a = V.do(tt, BB[0][r, :, 16 * e:16 * e + 16], t[0][r], t[1][r], SUB)
            V.wait(a)
            c = V.do(tt, t[0], BR[0], bd(CFI), MUL)
            b_ = V.do(tt, t[1], BR[1], bd(CFR), MUL)
            V.wait(c, b_)
            for e in range(2):
                r = slice(64 * e, 64 * e + 64)
                c = V.do(tt, BB[1][r, :, 16 * e:16 * e + 16], t[0][r], t[1][r], ADD)
            PE.wait(c, a)
            res = []
            for i in range(2):
                b, pb = bank()
                for m in range(4):
                    tk = PE.do(tr, pb[:, m * P:m * P + P], BB[i][:, 4 * m:4 * m + 4, :].rearrange("p a n -> p (a n)"),
                               ident)
                S.wait(tk)
                r = S.do(act, BT[i].rearrange("p a n -> p (a n)"), pb[:, :], ACT.Copy)
                free(b, r)
                res.append(r)
            V.wait(s_small["ssm_c_re_2"], s_small["ssm_c_im_2"])
            for i in range(2):
                b, pb = bank()
                cm = CM[i].rearrange("p (m e n) -> p m e n", m=4, e=2)
                for e in range(2):
                    c = V.do(ts, cm[:, :, e, :], CR[i], cst[:, C_M2 + e:C_M2 + e + 1], None, MUL)
                PE.wait(c)
                for m in range(4):
                    tk = PE.do(tr, pb[:, m * P:m * P + P], CM[i][:, m * P:m * P + P], ident)
                S.wait(tk)
                if i == 0:
                    S.do(act, CT[0].rearrange("p a n -> p (a n)"), pb[:, :], ACT.Copy)
                    r = S.do(act, CT[1].rearrange("p a n -> p (a n)"), pb[:, :], ACT.Copy, scale=-1.0)
                else:
                    r = S.do(act, CT[2].rearrange("p a n -> p (a n)"), pb[:, :], ACT.Copy, scale=-1.0)
                free(b, r)
                res.append(r)
            return res

        tab_tok = {}
        r_tab = []
        nt = [0]

        def s5_table(j, TH):
            x, k = S5T[0], S5T[1]
            x_ = ar(19200 + 256 * (j % 4), 256)
            k_ = ar(20224 + 256 * (j % 4), 256)
            V.wait(*s5c["tok"], *tab_tok.get(j - 4, []))
            a = V.do(ts, x_, tvec, TH[:, j:j + 1], None, MUL)
            V.wait(a)
            a = V.do(ts, k_, x_, 1.0 / TWO_PI, MAGIC, MUL, ADD)
            V.wait(a)
            a = V.do(ts, k_, k_, MAGIC, None, SUB)
            V.wait(a)
            a = V.do(stt, out=x_, in0=k_, scalar=-TP_HI, in1=x_, op0=MUL, op1=ADD)
            V.wait(a)
            a = V.do(stt, out=x_, in0=k_, scalar=-TP_LO, in1=x_, op0=MUL, op1=ADD)
            V.wait(a)
            a = V.do(ts, x_, x_, float(np.pi), -float(np.pi), MIN, MAX)
            S.wait(a)
            s = S.do(act, SIN[:, j, :], x_, ACT.Sin)
            c = S.do(act, COS[:, j, :], x_, ACT.Abs)
            S.wait(c)
            c = S.do(act, COS[:, j, :], COS[:, j, :], ACT.Sin, scale=-1.0, bias=hpi_c)
            tab_tok[j] = [s, c]

        s5c = {}

        AHL = [(v3(arb(0 + 512 * i, 512), 2), v3(arb(256 + 512 * i, 512), 2)) for i in range(2)]
        ffn_free = [[], []]

        def ffn(tag, hook=None):
            pend = None
            for blk in range(12):
                new = None
                if blk < 11:
                    ug, uu = Unit(f"{tag}g"), None
                    bks = [bank(), bank()]
                    for m in range(2):
                        for k in range(8):
                            tk = mm3(bks[m][1][:, 0:T], (ug.hi[:, k, m * P:m * P + P], ug.lo[:, k, m * P:m * P + P]),
                                     hpair(k), k == 0, k == 7)
                    ug.done(tk)
                    uu = Unit(f"{tag}u")
                    ah, al = AHL[blk % 2]
                    toks = []
                    for m in range(2):
                        for k in range(8):
                            tk = mm3(bks[m][1][:, T:2 * T], (uu.hi[:, k, m * P:m * P + P], uu.lo[:, k, m * P:m * P + P]),
                                     hpair(k), False, k == 7)
                        if m == 1:
                            uu.done(tk)
                        pb = bks[m][1]
                        o = 1024 + 1024 * (blk % 2) + 512 * m
                        e, f = ar(o, 256), ar(o + 256, 256)
                        r = silu_bank(pb, tk, e, f, ffn_free[blk % 2], T)
                        V.wait(r)
                        r = V.do(tt, f, f, pb[:, T:2 * T], MUL)
                        free(bks[m][0], r)
                        toks.append(pair(f, ah[:, m, :], al[:, m, :], [r], ffn_free[blk % 2]))
                    new = (ah, al, toks, blk)
                    last_h = tk
                if pend is not None:
                    pah, pal, ptoks, pblk = pend
                    PE.wait(*ptoks)
                    tk = acc_rows(Unit(f"{tag}d"), lambda k: (pah[:, k, :], pal[:, k, :]), pblk == 0, pblk == 10)
                    ffn_free[pblk % 2] = [tk]
                pend = new
                if hook is not None:
                    hook(blk)
            h_free.append(last_h)
            return tk

        HG = PC[:, 32:40]

        def ffn_layer(tag, mo, gname, hook=None):
            M = M2[:, mo:mo + 24]
            V.wait(*hp_last)
            g = mod_cols(M, gname, 0, GS, [m2_tok])
            hp = norm_mod(GS, M[:, 0:8], [g, m2_tok])
            del hp_last[:]
            hp_last.append(hp[-1])
            PE.wait(*hp)
            V.wait(*st_tok[-1])
            hg = V.do(ts, HG, M[:, 16:24], 0.5, None, MUL)
            tk = ffn(tag, hook)
            residual(HG, tk, [hg])
            return tk

        hp_last = [hp[-1]]
        ffn_free = [[ao], [ao]]

        def hook(blk):
            if blk == 0:
                RR, TH, CFR, CFI, t = s5_coefs()
                s5c["RR"], s5c["TH"], s5c["tok"] = RR, TH, t
                s5c["blk"] = s5_blocks(CFR, CFI, t)
            elif 1 <= blk <= 8:
                s5_table(2 * blk - 2, s5c["TH"])
                s5_table(2 * blk - 1, s5c["TH"])

        f1_done = ffn_layer("f1", 0, "ffn1_norm", hook)

        M = M2[:, 24:48]
        V.wait(*hp_last)
        g = mod_cols(M, "mix_norm", 0, GS, [m2_tok])
        hp = norm_mod(GS, M[:, 0:8], [g, m2_tok])
        hp_last[:] = [hp[-1]]
        PE.wait(*hp)
        UT = v3(ar(16384, 1024), 4)
        BG = v3(ar(17408, 1024), 4)
        ZP = v3(ar(18432, 1032), 4)
        YCV = v3(ar(19464, 1024), 4)
        YS = v3(ar(20488, 1024), 4)
        MT = [ar(0, 1024), ar(1024, 1024), ar(2048, 1024)]
        YMH = v3(arb(21512, 2048), 8)
        YML = v3(arb(22536, 2048), 8)
        PT = [ar(23560 + 256 * i, 256) for i in range(12)]
        prep_done = [s5c["blk"][-1]] + tab_tok[14] + tab_tok[15]
        u_tok = []
        for j in range(2):
            def ev(pb, tk, j=j):
                S.wait(tk, f1_done, *prep_done)
                r = S.do(act, UT[:, 2 * j:2 * j + 2, :], v3(pb[:, :], 2), ACT.Copy)
                u_tok.append(r)
                return [r]
            cols_T(Unit("win"), None, ev)

        cv = {}
        cv_tok = []

        def win_c(j):
            def ev(pb, tk):
                S.wait(tk, *prep_done)
                r = S.do(act, ZP[:, 2 * j:2 * j + 2, 2:258], v3(pb[:, :], 2), ACT.Copy)
                cv[("c", j)] = r
                return [r]
            cols_T(Unit("win"), None, ev)

        def win_v(j):
            def ev(pb, tk):
                V.wait(tk, cv[("c", j)])
                r = V.do(tt, ZP[:, 2 * j:2 * j + 2, 2:258], ZP[:, 2 * j:2 * j + 2, 2:258], v3(pb[:, :], 2), MUL)
                cv[("z", j)] = r
                return [r]
            cols_T(Unit("win"), None, ev)

        def win_b(j):
            def ev(pb, tk):
                S.wait(tk, *prep_done)
                r = S.do(act, BG[:, 2 * j:2 * j + 2, :], v3(pb[:, :], 2), ACT.Copy)
                cv[("b", j)] = r
                return [r]
            return cols_T(Unit("win"), None, ev)

        G.wait(*prep_done)
        zp_tok = G.do(nc.gpsimd.memset, ZP[:, :, 0:2], 0.0)

        def conv_tile(n):
            y = YCV[:, n, :]
            V.wait(cv[("z", n // 2)], cv[("b", n // 2)], zp_tok)
            a = V.do(ts, y, ZP[:, n, 2:258], col("conv_w", 8 + n), None, MUL)
            V.wait(a)
            a = V.do(stt, out=y, in0=ZP[:, n, 1:257], scalar=col("conv_w", 4 + n), in1=y, op0=MUL, op1=ADD)
            V.wait(a)
            a = V.do(stt, out=y, in0=ZP[:, n, 0:256], scalar=col("conv_w", n), in1=y, op0=MUL, op1=ADD)
            V.wait(a)
            cv_tok.append(V.do(tt, y, y, BG[:, n, :], MUL))

        yb = []
        PE.wait(*u_tok, *s5c["blk"], *acc_free)
        pt_free = {0: [], 1: []}
        ys_toks = []

        def s5_tile(j, first):
            m, jj = j // 4, j % 4
            b, pb = bank()
            r = slice(32 * jj, 32 * jj + 32)
            PE.quiet(mm, pb[:, 0:T], BT[0][r, m, :], UT[r, m, :], start=True, stop=True, skip_group_check=True)
            tk = mmf(pb[:, T:2 * T], BT[1][r, m, :], UT[r, m, :], False, True)
            o = 6 * (j % 2)
            p1, p2, p3, p4, zr, zi = PT[o:o + 6]
            C_, S_ = COS[:, j, :], SIN[:, j, :]
            V.wait(tk, *tab_tok[j], *pt_free[j % 2])
            a1 = V.do(tt, p1, pb[:, 0:T], C_, MUL)
            a2 = V.do(tt, p2, pb[:, T:2 * T], S_, MUL)
            a3 = V.do(tt, p3, pb[:, T:2 * T], C_, MUL)
            a4 = V.do(tt, p4, pb[:, 0:T], S_, MUL)
            free(b, a4)
            G.wait(a2)
            g1 = G.do(nc.gpsimd.tensor_tensor, p1, p1, p2, ADD)
            G.wait(a4)
            g2 = G.do(nc.gpsimd.tensor_tensor, p3, p3, p4, SUB)
            return j, g1, g2

        def s5_rest(st):
            j, g1, g2 = st
            m, jj = j // 4, j % 4
            o = 6 * (j % 2)
            p1, p2, p3, p4, zr, zi = PT[o:o + 6]
            C_, S_ = COS[:, j, :], SIN[:, j, :]
            rb = s5c["RR"][:, j:j + 1].to_broadcast([P, T])
            V.wait(g1)
            s1 = V.do(nc.vector.tensor_tensor_scan, zr, rb, p1, 0.0, MUL, ADD)
            V.wait(g2)
            s2 = V.do(nc.vector.tensor_tensor_scan, zi, rb, p3, 0.0, MUL, ADD)
            V.wait(s1)
            q1 = V.do(tt, p1, C_, zr, MUL)
            q2 = V.do(tt, p2, S_, zr, MUL)
            V.wait(s2)
            q3 = V.do(tt, p3, S_, zi, MUL)
            q4 = V.do(tt, p4, C_, zi, MUL)
            PE.wait(q1, q2, q3, q4)
            r = slice(32 * jj, 32 * jj + 32)
            o_ = pacc[r, 2 * m, :]
            PE.quiet(mm, o_, CT[0][:, m, r], p1, start=True, stop=False, skip_group_check=True)
            PE.quiet(mm, o_, CT[1][:, m, r], p3, start=False, stop=False, skip_group_check=True)
            PE.quiet(mm, o_, CT[2][:, m, r], p2, start=False, stop=False, skip_group_check=True)
            tk = mmf(o_, CT[2][:, m, r], p4, False, True)
            pt_free[j % 2] = [tk]
            if jj == 3:
                V.wait(tk, *prep_done)
                ys_toks.append(V.do(stt, out=YS[:, m, :], in0=UT[:, m, :], scalar=col("ssm_d", m),
                                    in1=pacc[:, 2 * m, :], op0=MUL, op1=ADD))

        jobs = [lambda: win_c(0), lambda: win_c(1), lambda: win_v(0), lambda: win_v(1), lambda: win_b(0),
                lambda: win_b(1)]
        prev = None
        for j in range(16):
            cur_s = s5_tile(j, j % 4 == 0)
            if j % 2 == 0 and jobs:
                last_h = jobs.pop(0)()
            if prev is not None:
                s5_rest(prev)
            prev = cur_s
            if j >= 12:
                conv_tile(j - 12)
        s5_rest(prev)
        h_free.append(last_h)
        acc_free[:] = [ys_toks[-1]]

        def rms_half(tiles, toks, gname, off):
            b, pb = bank()
            r = sumsq(pb[:, 0:T], tiles, toks)
            V.wait(*rt_last)
            a, z = rsqrt(RT[:, 0, :], pb[:, 0:T], 1.0 / 512, [r], (RT[:, 1, :], RT[:, 2, :]))
            free(b, a)
            res = []
            for n in range(4):
                V.wait(z)
                a = V.do(stt, out=tiles[n], in0=tiles[n], scalar=col(gname, n), in1=RT[:, 0, :], op0=MUL, op1=MUL)
                res.append(pair(tiles[n], YMH[:, off + n, :], YML[:, off + n, :], [a], prep_done))
            rt_last[:] = [res[-1]]
            return res

        YSf = YS.rearrange("p a n -> p (a n)")
        E1, E2, E3 = MT
        glh, gll = v3(arb(3072, 1024), 4), v3(arb(3584, 1024), 4)
        S.wait(*ys_toks, f1_done)
        a = S.do(act, E1, YSf, ACT.Square)
        V.wait(a)
        a = V.do(ts, E1, E1, GELU_C * 0.044715, GELU_C, MUL, ADD)
        V.wait(a, *ys_toks)
        a = V.do(tt, E1, E1, YSf, MUL)
        V.wait(a)
        a = V.do(ts, E1, E1, -80.0, None, MAX)
        S.wait(a)
        a = S.do(act, E1, E1, ACT.Exp, scale=-1.0)
        V.wait(a)
        a = V.do(ts, E1, E1, 1.0, None, ADD)
        V.wait(a)
        a = V.do(nc.vector.reciprocal, E1, E1)
        V.wait(a)
        a = V.do(tt, YSf, YSf, E1, MUL)
        gl_tok = pair(YSf, glh.rearrange("p a n -> p (a n)"), gll.rearrange("p a n -> p (a n)"), [a], [f1_done])
        cvn = rms_half([YCV[:, n, :] for n in range(4)], [[t] for t in cv_tok], "out_norm_conv", 0)
        NGB = PC[:, 40:44]
        V.wait(vc_tok, ebl_tok)
        nb = V.do(ts, NGB, col("glu_b", 0, 4), -1.0, None, MUL)
        u = Unit("glu")
        PE.wait(gl_tok)
        eg = []
        for q in range(2):
            b, pb = bank()
            for m in range(2):
                n = 2 * q + m
                for k in range(4):
                    tk = mm3(pb[:, m * T:m * T + T], (u.hi[:, k, n * P:n * P + P], u.lo[:, k, n * P:n * P + P]),
                             (glh[:, k, :], gll[:, k, :]), k == 0, k == 3)
            for m in range(2):
                n = 2 * q + m
                S.wait(tk, nb)
                r = S.do(act, E2[:, n * T:n * T + T], pb[:, m * T:m * T + T], ACT.Exp, scale=-1.0,
                         bias=NGB[:, n:n + 1])
            free(b, r)
        u.done(tk)
        V.wait(r)
        a = V.do(ts, E2, E2, 1.0, None, ADD)
        V.wait(a)
        a = V.do(nc.vector.reciprocal, E2, E2)
        V.wait(a)
        a = V.do(tt, YSf, YSf, E2, MUL)
        ysn = rms_half([YS[:, n, :] for n in range(4)], [[a]] * 4, "out_norm_ssm", 4)
        for j in range(4):
            PE.wait((cvn + ysn)[2 * j], (cvn + ysn)[2 * j + 1])
            tk = acc_rows(Unit("wout"), lambda k, j=j: (YMH[:, 2 * j + k, :], YML[:, 2 * j + k, :]), j == 0, j == 3)
        residual(M[:, 16:24], tk, [m2_tok])
        ffn_free[:] = [[tk, a], [tk, a]]
        glu_done = a

        f2_done = ffn_layer("f2", 48, "ffn2_norm")

        r = norm_r([xT[:, k, :] for k in range(8)], x_tok, D)
        OUT = v3(ar(4096, 2048), 2)
        st = []
        for k in range(8):
            V.wait(r, *x_tok[k])
            a = V.do(stt, out=xT[:, k, :], in0=xT[:, k, :], scalar=col("final_norm", k), in1=RT[:, 0, :],
                     op0=MUL, op1=MUL)
            st.append(a)
        for m in range(2):
            for q in range(2):
                b, pb = bank()
                for kk in range(4):
                    k = 4 * q + kk
                    PE.wait(st[k])
                    tk = PE.do(tr, pb[:, kk * P:kk * P + P], xT[:, k, m * P:m * P + P], ident)
                S.wait(tk, ys_toks[-1])
                o_tok = S.do(act, OUT[:, m, 512 * q:512 * q + 512], pb[:, :], ACT.Copy)
                free(b, o_tok)
            S.wait(o_tok)
            so = sem(f"s_out{m}")
            S.dma(nc.scalar.dma_start, out[0, m * P:m * P + P, :], OUT[:, m, :], so)
            S.wait((so, 16)) if m == 1 else None
            if m == 0:
                so0 = so
        S.wait((so0, 16))

        assert cur[0] == len(units)
        for i, (nm, src, k, n) in enumerate(units):
            if i >= RING:
                SP.wait(unit_free[i - RING])
                if (i - RING) in split_tok:
                    SP.wait(split_tok[i - RING])
            SP.dma(nc.sync.dma_start, v3(ring[:, i % RING, 0:k * n], k), src, s_ring[i % RING])

        block = ctx.enter_context(nc.Block())

        @block.sync
        def _(eng):
            SP.emit(eng)

        @block.tensor
        def _(eng):
            PE.emit(eng)

        @block.vector
        def _(eng):
            V.emit(eng)

        @block.scalar
        def _(eng):
            S.emit(eng)

        @block.gpsimd
        def _(eng):
            G.emit(eng)


_INS = ["x", "c", "ada_w", "ada_b", "norm_g", "even_in_w", "pool_w", "pool_scale", "sgu_norm_g", "sgu_w", "sgu_b",
        "even_out_w", "odd_in_w", "gla_gate_w", "gla_gate_b", "gla_norm_g", "odd_out_w", "final_g", "cond_2",
        "w_mod_2", "b_mod_2", "ffn1_norm_2", "ffn1_w_gate_2", "ffn1_w_up_2", "ffn1_w_down_2", "mix_norm_2",
        "w_in_2", "conv_w_2", "lambda_re_2", "lambda_im_2", "log_dt_2", "ssm_b_re_2", "ssm_b_im_2", "ssm_c_re_2",
        "ssm_c_im_2", "ssm_d_2", "glu_w_2", "glu_b_2", "out_norm_conv_2", "out_norm_ssm_2", "w_out_2",
        "ffn2_norm_2", "ffn2_w_gate_2", "ffn2_w_up_2", "ffn2_w_down_2", "final_norm_2"]


def kernel(**inputs):
    import concourse.bacc as _bacc
    from concourse.bass_utils import run_bass_kernel_spmd as _run

    nc = _bacc.Bacc("TRN2", target_bir_lowering=False, num_devices=1)
    arrays, aps = {}, {}
    given = {n: np.ascontiguousarray(inputs[n]) for n in _INS}
    given["consts"] = constants()
    for name, a in given.items():
        arrays[f"in_{name}"] = a
        aps[name] = nc.dram_tensor(f"in_{name}", a.shape, mybir.dt.from_np(a.dtype), kind="ExternalInput").ap()
    out = nc.dram_tensor("out_0", (1, T, D), F32, kind="ExternalOutput").ap()
    build(nc, aps, out)
    r = _run(nc, [arrays], core_ids=[0])
    return r.results[0]["out_0"]
```

```python
from contextlib import ExitStack

import numpy as np
import concourse.bass as bass
from concourse import mybir

F32 = mybir.dt.float32
F32R = mybir.dt.float32r
U32 = mybir.dt.uint32
I32 = mybir.dt.int32
ALU = mybir.AluOpType
ACT = mybir.ActivationFunctionType
MUL, ADD, SUB, MAX, MIN = ALU.mult, ALU.add, ALU.subtract, ALU.max, ALU.min

P = 128
T = 256
D = 1024
EPS = 1e-6
TWO_PI = 6.283185307179586
TP_HI = 6.28125
TP_LO = TWO_PI - TP_HI
MAGIC = 12582912.0
GELU_C = 2.0 * 0.7978845608028654

RING = 5
NW = 4
AHEAD = 2
WORDS = 20480
RSQRT_MAGIC = 1597463007.0

C_ID, C_ONE, C_NU, C_NONE, C_IC, C_T, C_M2, C_K = 0, 128, 256, 384, 512, 640, 896, 898
C_ALL = 902


def constants():
    c = np.zeros((P, C_ALL), np.float32)
    i = np.arange(P)
    c[:, C_ID:C_ID + P] = np.eye(P)
    c[:, C_ONE:C_ONE + P] = 1.0
    c[:, C_NU:C_NU + P] = np.where(i[:, None] >= i[None, :], -1.0, 0.0)
    c[:, C_NONE:C_NONE + P] = -1.0
    t = np.arange(16)
    ic = np.stack([1.0 / np.minimum(t + 1, w) for w in (2, 2, 4, 4, 8, 8, 16, 16)])
    c[:, C_IC:C_IC + 128] = ic.reshape(1, 128)
    c[:, C_T:C_T + T] = np.arange(T)
    c[:, C_M2] = (i // 16) % 2 == 0
    c[:, C_M2 + 1] = (i // 16) % 2 == 1
    c[:, C_K] = 1.0
    c[:, C_K + 1] = np.pi / 2
    c[:, C_K + 2] = 0.0
    c[:, C_K + 3] = 0.0
    return c


class Queue:

    def __init__(self, sem):
        self.sem, self.n, self.items, self.seen = sem, 0, [], {}

    def wait(self, *marks):
        for s, v in marks:
            if self.seen.get(s.name, 0) < v:
                self.seen[s.name] = v
                self.items.append((None, s, v, None))
        return self

    def do(self, fn, *args, **kw):
        self.n += 1
        self.items.append((fn, args, kw, (self.sem, 1)))
        return (self.sem, self.n)

    def quiet(self, fn, *args, **kw):
        self.items.append((fn, args, kw, None))

    def dma(self, fn, out, src, sem):
        self.items.append((fn, (out, src), {}, (sem, 16)))

    def emit(self, eng):
        for fn, a, b, inc in self.items:
            if fn is None:
                eng.wait_ge(a, b)
            else:
                ins = fn(*a, **b)
                if inc is not None:
                    ins.then_inc(inc[0], inc[1])


def build(nc, I, out):
    ctx = ExitStack()
    with ctx:
        def sb(name, shape, dt=F32):
            return ctx.enter_context(nc.sbuf_tensor(name, shape, dt))

        def sem(name):
            return ctx.enter_context(nc.semaphore(name))

        ring = sb("ring", [P, RING, 2048])
        WH = sb("WH", [P, NW, 1024], F32R)
        WL = sb("WL", [P, NW, 1024], F32R)
        hh = sb("hh", [P, 8, T], F32R)
        hl = sb("hl", [P, 8, T], F32R)
        YH = sb("YH", [P, 3, 2, T], F32R)
        YL = sb("YL", [P, 3, 2, T], F32R)
        GRH = sb("GRH", [P, 8, 16], F32R)
        GRL = sb("GRL", [P, 8, 16], F32R)
        GRW = sb("GRW", [P, 8, 16])
        xT = sb("xT", [P, 8, T])
        SQT = sb("SQT", [P, 4, T])
        RT = sb("RT", [P, 4, T])
        cst = sb("cst", [P, C_ALL])
        VC = sb("VC", [P, 300])
        MOD = sb("MOD", [P, 24 + 24 + 72])
        PC = sb("PC", [P, 64])
        ACC = sb("ACC", [P, 1024])
        AR = sb("AR", [P, WORDS])
        pacc = ctx.enter_context(nc.psum_tensor("pacc", [P, 8, T], F32))
        pw = [ctx.enter_context(nc.psum_tensor(f"pw{i}", [P, 512], F32)) for i in range(4)]

        PE, V, S, G, SP = (Queue(sem(n)) for n in ("s_pe", "s_v", "s_s", "s_g", "s_sp"))
        s_ring = [sem(f"s_ring{i}") for i in range(RING)]
        s_small = {}

        mm, tr = nc.tensor.matmul, nc.tensor.transpose
        tt, ts, stt = nc.vector.tensor_tensor, nc.vector.tensor_scalar, nc.vector.scalar_tensor_tensor
        act = nc.scalar.activation

        def ar(off, n):
            return AR[:, off:off + n]

        def v3(ap, a):
            return ap.rearrange("p (a n) -> p a n", a=a)

        ident = cst[:, C_ID:C_ID + P]
        ones = cst[:, C_ONE:C_ONE + P]
        negU = cst[:, C_NU:C_NU + P]
        negones = cst[:, C_NONE:C_NONE + P]
        ic = v3(cst[:, C_IC:C_IC + P], 8)
        tvec = cst[:, C_T:C_T + T]
        one_c = cst[:, C_K:C_K + 1]
        hpi_c = cst[:, C_K + 1:C_K + 2]

        def small(q, fn, name, dst, src):
            s = sem("d_" + name)
            q.dma(fn, dst, src, s)
            s_small[name] = (s, 16)
            return (s, 16)

        small(S, nc.scalar.dma_start, "cst", cst[:, :], I["consts"])
        rows = {}
        packs = [[("c", I["c"], 8), ("norm_g", I["norm_g"], 16), ("ada_b", I["ada_b"], 48),
                  ("pool_scale", I["pool_scale"], 8), ("sgu_norm_g", I["sgu_norm_g"], 8),
                  ("final_g", I["final_g"], 8), ("gla_gate_b", I["gla_gate_b"], 4),
                  ("gla_norm_g", I["gla_norm_g"], 8), ("cond", I["cond_2"], 8)],
                 [("b_mod", I["b_mod_2"], 72), ("ffn1_norm", I["ffn1_norm_2"], 8), ("mix_norm", I["mix_norm_2"], 8),
                  ("conv_w", I["conv_w_2"], 12), ("ssm_d", I["ssm_d_2"], 4), ("glu_b", I["glu_b_2"], 4),
                  ("out_norm_conv", I["out_norm_conv_2"], 4), ("out_norm_ssm", I["out_norm_ssm_2"], 4),
                  ("ffn2_norm", I["ffn2_norm_2"], 8)],
                 [("final_norm", I["final_norm_2"], 8), ("lam_re", I["lambda_re_2"], 16),
                  ("lam_im", I["lambda_im_2"], 16)]]
        VR = AR[:, 0:3 * P].rearrange("p (a n) -> p a n", a=3)
        base = 0
        pack_n = []
        for a, pk in enumerate(packs):
            r = 0
            s = sem(f"d_vec{a}")
            for name, src, n in pk:
                flat = src
                while len(flat.shape) > 1:
                    names = " ".join("abcd"[:len(flat.shape)])
                    flat = flat.rearrange(f"{names} -> ({names})")
                S.dma(nc.scalar.dma_start, VR[r:r + n, a, :], flat.rearrange("(r n) -> r n", n=P), s)
                rows[name] = (base + r, n)
                r += n
            if a == 2:
                ldt = AR[:, 3 * P:3 * P + 2]
                S.dma(nc.scalar.dma_start, ldt[r:r + 16, :] if False else AR[0:16, 384:386],
                      I["log_dt_2"].rearrange("o (j e) -> (o j) e", e=2), s)
                s_small["vec2"] = (s, 16 * (len(pk) + 1))
            else:
                s_small[f"vec{a}"] = (s, 16 * len(pk))
            base += r
            pack_n.append(r)

        def col(name, i=0, n=1):
            b, m = rows[name]
            return VC[:, b + i:b + i + n]

        XN = AR[:, 512:512 + 2048].rearrange("p (a n) -> p a n", a=2)
        small(S, nc.scalar.dma_start, "x", XN, I["x"].rearrange("o (a p) n -> p (o a) n", p=P))
        E_SWR, E_BB = 17792, 18816
        GLW = AR[0:16, 19840:20352]
        small(G, nc.gpsimd.dma_start, "sgu_w", v3(ar(E_SWR, 1024), 8),
              I["sgu_w"].rearrange("o h t s -> t (o h) s"))
        small(G, nc.gpsimd.dma_start, "glr", GRW[:, :, :],
              I["odd_in_w"][0, :, 2048:2064].rearrange("(k p) n -> p k n", p=P))
        small(G, nc.gpsimd.dma_start, "glw", GLW, I["gla_gate_w"][0])
        small(G, nc.gpsimd.dma_start, "sgu_b", AR[0:1, E_BB:E_BB + 1024], I["sgu_b"].rearrange("o h t -> o (h t)"))

        units = []

        def add_cols(name, W, c0, n=256, k=8):
            units.append((name, W[0:k * P, c0:c0 + n].rearrange("(k p) n -> p k n", p=P), k, n))

        def add_rows(name, W, r0):
            units.append((name, W[r0:r0 + 256, :].rearrange("(k p) n -> p k n", p=P), 2, 1024))

        def add_ada(W, n0, n1):
            return [("ada", W[256 * r:256 * r + 256, 1024 * cc:1024 * cc + 1024].rearrange("(k p) n -> p k n", p=P),
                     2, 1024) for cc in range(n0, n1) for r in range(4)]

        def weave(side, from_):
            main = units[from_:]
            del units[from_:]
            k = 0
            for i, u in enumerate(main):
                while k < len(side) and k * len(main) <= i * len(side):
                    units.append(side[k])
                    k += 1
                units.append(u)
            units.extend(side[k:])

        def add_ffn(tag, Wg, Wu, Wd):
            for b in range(12):
                if b < 11:
                    add_cols(f"{tag}g", Wg, 256 * b)
                    add_cols(f"{tag}u", Wu, 256 * b)
                if b > 0:
                    add_rows(f"{tag}d", Wd, 256 * (b - 1))

        ew, ow, wi = I["even_in_w"][0], I["odd_in_w"][0], I["w_in_2"][0]
        a0, a1, a2 = I["ada_w"][0], I["ada_w"][1], I["w_mod_2"][0]
        units += add_ada(a0, 0, 2)
        at = len(units)
        for c0 in [2048 + 256 * j for j in range(4)] + [256 * j for j in range(4)]:
            add_cols("ein", ew, c0)
        for c0 in [1024 + 256 * j for j in range(4)]:
            add_cols("ein", ew, c0)
        units.append(("pool", I["pool_w"][0].rearrange("g (k p) n -> p (g k) n", p=P), 8, 256))
        for j in range(8):
            add_cols("ein", ew, 3072 + 256 * j)
        weave(add_ada(a0, 2, 3) + add_ada(a1, 0, 2), at)
        at = len(units)
        for j in range(8):
            add_rows("eout", I["even_out_w"][0], 256 * j)
        at = len(units)
        for c0 in [256 * j for j in range(8)] + [2064 + 256 * j for j in range(12)]:
            add_cols("oin", ow, c0)
        for j in range(8):
            add_cols("oin", ow, 5136 + 256 * j)
        for j in range(8):
            add_rows("oout", I["odd_out_w"][0], 256 * j)
        weave(add_ada(a1, 2, 3) + add_ada(a2, 0, 3), at)
        at = len(units)
        add_ffn("f1", I["ffn1_w_gate_2"][0], I["ffn1_w_up_2"][0], I["ffn1_w_down_2"][0])
        weave(add_ada(a2, 3, 7), at)
        at = len(units)
        for c0 in (1536, 1792, 512, 768, 1024, 1280, 0, 256):
            add_cols("win", wi, c0)
        add_cols("glu", I["glu_w_2"][0], 0, 512, 4)
        for j in range(4):
            add_rows("wout", I["w_out_2"][0], 256 * j)
        weave(add_ada(a2, 7, 8), at)
        at = len(units)
        add_ffn("f2", I["ffn2_w_gate_2"][0], I["ffn2_w_up_2"][0], I["ffn2_w_down_2"][0])
        weave(add_ada(a2, 8, 9), at)

        pieces = [(i, h) for i, u in enumerate(units) if u[0] != "ada" for h in range(2)]
        piece_of = {p: k for k, p in enumerate(pieces)}
        piece_tok, piece_done = {}, {}
        unit_free = {}
        cur, ncut = [0], [0]

        def landed(i):
            return (s_ring[i % RING], 16 * (i // RING + 1))

        def cut_to(k):
            while ncut[0] < len(pieces) and ncut[0] <= k:
                q = ncut[0]
                ncut[0] += 1
                u, half = pieces[q]
                if q >= NW:
                    S.wait(piece_done[q - NW])
                    V.wait(piece_done[q - NW])
                S.wait(landed(u))
                V.wait(landed(u))
                w = ring[:, u % RING, 1024 * half:1024 * half + 1024]
                H, L = WH[:, q % NW, :], WL[:, q % NW, :]
                a = S.do(act, H, w, ACT.Copy)
                V.wait(a)
                b = V.do(tt, L, w, H.bitcast(F32), SUB)
                piece_tok[q] = [a, b]
                unit_free[u] = [b]

        ada_out = []
        M0, M1, M2 = MOD[:, 0:24], MOD[:, 24:48], MOD[:, 48:120]
        ada_state = {"n": 0, "red": [], "tok": None}

        def ada_unit(i):
            n = ada_state["n"]
            ada_state["n"] += 1
            chunk, r = n // 4, n % 4
            sc = SIL[:, 0:8] if chunk < 6 else SIL[:, 8:16]
            slot = v3(ring[:, i % RING, :], 2)
            if r == 0:
                ada_reduce()
                ada_add()
            V.wait(landed(i))
            for k in range(2):
                c = sc[:, 2 * r + k:2 * r + k + 1]
                if r == 0 and k == 0:
                    V.wait(sil_tok, *ada_state["red"])
                    t = V.do(ts, ACC[:, :], slot[:, 0, :], c, None, MUL)
                else:
                    V.wait(ada_state["tok"])
                    t = V.do(stt, out=ACC[:, :], in0=slot[:, k, :], scalar=c, in1=ACC[:, :], op0=MUL, op1=ADD)
                ada_state["tok"] = t
            unit_free[i] = [t]
            if r == 3:
                ada_state["pend"] = (chunk, t)

        def ada_reduce():
            if ada_state.get("pend"):
                chunk, t = ada_state.pop("pend")
                b, pb = bank()
                PE.wait(t)
                for m in range(8):
                    tk = mmf(pb[:, m:m + 1], ACC[:, m * P:m * P + P], ones[:, 0:1])
                ada_state["red"] = [tk]
                ada_state["add"] = (chunk, b, pb, tk)

        def ada_add():
            if ada_state.get("add"):
                chunk, b, pb, tk = ada_state.pop("add")
                V.wait(tk)
                bias = col("ada_b", 8 * chunk, 8) if chunk < 6 else col("b_mod", 8 * (chunk - 6), 8)
                z = V.do(tt, MOD[:, 8 * chunk:8 * chunk + 8], pb[:, 0:8], bias, ADD)
                free(b, z)
                ada_out.append(z)

        def ada_step():
            ada_add()
            ada_reduce()

        def ada_flush():
            ada_reduce()
            ada_add()

        def ada_drain():
            while cur[0] < len(units) and units[cur[0]][0] == "ada":
                ada_unit(cur[0])
                cur[0] += 1

        class Unit:

            def __init__(self, name):
                ada_step()
                ada_drain()
                self.i = cur[0]
                cur[0] += 1
                nm, _, self.k, self.n = units[self.i]
                assert nm == name, (nm, name, self.i)

            def piece(self, half):
                q = piece_of[(self.i, half)]
                cut_to(q + AHEAD)
                PE.wait(*piece_tok[q])
                a = self.k // 2
                return v3(WH[:, q % NW, :], a), v3(WL[:, q % NW, :], a)

            def done(self, half, tok):
                piece_done[piece_of[(self.i, half)]] = tok

        def mm3(o, a, b, start, stop):
            PE.quiet(mm, o, a[0], b[0], start=start, stop=False, skip_group_check=True)
            PE.quiet(mm, o, a[0], b[1], start=False, stop=False, skip_group_check=True)
            return PE.do(mm, o, a[1], b[0], start=False, stop=stop, skip_group_check=True)

        def mmf(o, a, b, start=True, stop=True):
            return PE.do(mm, o, a, b, start=start, stop=stop, skip_group_check=True)

        wfree = [[] for _ in range(4)]
        border = [0, 1, 2, 3]

        def bank():
            i = [x for x in border if wfree[x] is not None][0]
            border.remove(i)
            PE.wait(*wfree[i])
            wfree[i] = None
            return i, pw[i]

        def free(i, *toks):
            wfree[i] = list(toks)
            border.append(i)

        def pair(src, dh, dl, toks, free_toks=()):
            S.wait(*toks, *free_toks)
            a = S.do(act, dh, src, ACT.Copy)
            V.wait(*toks, a, *free_toks)
            return V.do(tt, dl, src, dh.bitcast(F32), SUB)

        yfree = [[], [], []]
        ny = [0]

        def ypair(src, toks):
            i = ny[0] % 3
            ny[0] += 1
            f = lambda x: x.rearrange("p a n -> p (a n)")
            t = pair(src, f(YH[:, i]), f(YL[:, i]), toks, yfree[i])
            yfree[i] = None
            return i, t

        def rsqrt(dst, src, scale, toks, tmp):
            h, t = tmp
            V.wait(*toks)
            a = V.do(ts, t, src, scale, EPS, MUL, ADD)
            V.wait(a)
            c = V.do(ts, h, t, 0.5, None, MUL)
            b = V.do(ts, dst.bitcast(U32), t.bitcast(U32), 1, None, ALU.logical_shift_right)
            V.wait(b)
            y = V.do(ts, dst.bitcast(I32), dst.bitcast(I32), -1.0, RSQRT_MAGIC, MUL, ADD)
            for i in range(3):
                V.wait(y, c)
                b = V.do(tt, t, dst, dst, MUL)
                V.wait(b)
                b = V.do(tt, t, t, h, MUL)
                V.wait(b)
                y = V.do(stt, out=dst, in0=t, scalar=1.5, in1=dst, op0=SUB, op1=MUL, **({"reverse0": True} if i == 2 else {}))
            return a, y

        sq_free = [[], [], [], []]
        nsq = [0]

        def sumsq(o, tiles, toks, start=True):
            for k, (x, tk) in enumerate(zip(tiles, toks)):
                i = nsq[0] % 4
                nsq[0] += 1
                S.wait(*sq_free[i], *tk)
                a = S.do(act, SQT[:, i, :], x, ACT.Square)
                PE.wait(a)
                r = mmf(o, ones, SQT[:, i, :], start and k == 0, k == len(tiles) - 1)
                sq_free[i] = [r]
            return r

        rt_last = []

        def norm_r(tiles, toks, n):
            b, pb = bank()
            r = sumsq(pb[:, 0:T], tiles, toks)
            V.wait(*rt_last)
            a, z = rsqrt(RT[:, 0, :], pb[:, 0:T], 1.0 / n, [r], (RT[:, 1, :], RT[:, 2, :]))
            free(b, a)
            return z

        x_tok = [[] for _ in range(8)]
        h_free = []

        def norm_mod(gs, sh, toks):
            r = norm_r([xT[:, k, :] for k in range(8)], x_tok, D)
            del rt_last[:]
            res = []
            for q in range(4):
                ks = (2 * q, 2 * q + 1)
                i = nsq[0] % 4
                i += i % 2
                i %= 4
                nsq[0] = i + 2
                x2 = SQT[:, i:i + 2, :]
                V.wait(r, *toks, *sq_free[i], *sq_free[i + 1])
                a = V.do(tt, x2, xT[:, 2 * q:2 * q + 2, :], RT[:, 0:1, :].to_broadcast([P, 2, T]), MUL)
                S.wait(a, *toks, *h_free)
                hs = [S.do(act, hh[:, k, :], SQT[:, i + k % 2, :], ACT.Identity, scale=gs[:, k:k + 1],
                           bias=sh[:, k:k + 1]) for k in ks]
                V.wait(a, hs[-1])
                us = [V.do(ts, SQT[:, i + k % 2, :], SQT[:, i + k % 2, :], gs[:, k:k + 1], sh[:, k:k + 1], MUL, ADD)
                      for k in ks]
                V.wait(us[-1], *h_free)
                c = V.do(tt, hl[:, 2 * q:2 * q + 2, :], x2, hh[:, 2 * q:2 * q + 2, :].bitcast(F32), SUB)
                sq_free[i] = sq_free[i + 1] = [c]
                res.append(c)
            rt_last.append(res[-1])
            del h_free[:]
            return res

        def hpair(k, sl=slice(0, T)):
            return (hh[:, k, sl], hl[:, k, sl])

        acc_free = []
        acc_on = [False]

        def acc_rows(u, place, first, last):
            i, t = place
            if first:
                PE.wait(*acc_free)
            PE.wait(t)
            for k in range(2):
                H, L = u.piece(k)
                for n in range(8):
                    sl = slice(n * P, n * P + P)
                    tk = mm3(pacc[:, n, :], (H[:, 0, sl], L[:, 0, sl]), (YH[:, i, k, :], YL[:, i, k, :]),
                             first and k == 0 and n % 2 == 0, last and k == 1)
                u.done(k, tk)
            yfree[i] = [tk]
            return tk

        def residual(gate, tk, gtoks):
            del acc_free[:]
            for n in range(8):
                V.wait(tk, *gtoks, *x_tok[n], *rt_last)
                a = V.do(stt, out=xT[:, n, :], in0=pacc[:, n, :], scalar=gate[:, n:n + 1], in1=xT[:, n, :],
                         op0=MUL, op1=ADD)
                x_tok[n] = [a]
            acc_free.append(a)

        def cols_T(u, banks_of, evac):
            b, pb = bank()
            for half in range(2):
                H, L = u.piece(half)
                for m in range(2):
                    for kk in range(4):
                        sl = slice(m * P, m * P + P)
                        tk = mm3(pb[:, m * T:m * T + T], (H[:, kk, sl], L[:, kk, sl]), hpair(4 * half + kk),
                                 half == 0 and kk == 0 and m == 0, half == 1 and kk == 3)
                u.done(half, tk)
            free(b, *evac(pb, tk))
            return tk

        def cols_N(u, dst, dtoks):
            b, pb = bank()
            for half in range(2):
                H, L = u.piece(half)
                for m in range(2):
                    for kk in range(4):
                        tk = mm3(pb[:, m * T:m * T + T], hpair(4 * half + kk, slice(m * P, m * P + P)),
                                 (H[:, kk, :], L[:, kk, :]), half == 0 and kk == 0 and m == 0,
                                 half == 1 and kk == 3)
                u.done(half, tk)
            S.wait(tk, *dtoks)
            r = S.do(act, dst, v3(pb[:, :], 2), ACT.Copy)
            free(b, r)
            return r

        def silu_t(pb, tk, dst, toks, n=512):
            S.wait(tk, *toks)
            return S.do(act, dst, pb[:, 0:n], ACT.Silu)

        def silu_bank(pb, tk, e, dst, toks, n=512):
            S.wait(tk, *toks)
            a = S.do(act, e, pb[:, 0:n], ACT.Exp, scale=-1.0)
            V.wait(a)
            a = V.do(ts, e, e, 1.0, None, ADD)
            V.wait(a)
            a = V.do(nc.vector.reciprocal, e, e)
            V.wait(a, *toks)
            return V.do(tt, dst, pb[:, 0:n], e, MUL)

        S.quiet(nc.scalar.preload_act_table_set, "exp_and_others")
        PE.wait(s_small["cst"], s_small["vec0"], s_small["vec1"], s_small["vec2"])
        b, pb = bank()
        base = 0
        for a, n in enumerate(pack_n):
            tk = PE.do(tr, pb[:, base:base + n], VR[0:n, a, :], ident[0:n, 0:n])
            base += n
        V.wait(tk)
        vc_tok = V.do(nc.vector.tensor_copy, VC[:, 0:base], pb[:, 0:base])
        free(b, vc_tok)
        DTC = PC[:, 0:16]
        dtr = AR[0:16, 400:528]
        V.wait(s_small["vec2"])
        a = V.do(nc.vector.tensor_copy, AR[0:16, 2560:2688].rearrange("p (e n) -> p e n", e=2),
                 AR[0:16, 384:386].unsqueeze(2).to_broadcast([16, 2, 64]))
        b, pb = bank()
        PE.wait(a)
        tk = PE.do(tr, pb[:, 0:16], AR[0:16, 2560:2688], ident[0:16, 0:16])
        S.wait(tk)
        dt_tok = S.do(act, DTC, pb[:, 0:16], ACT.Exp)
        free(b, dt_tok)

        SIL = PC[:, 16:32]
        sil_e = PC[:, 32:48]
        S.wait(vc_tok)
        a = S.do(act, sil_e[:, 0:8], col("c", 0, 8), ACT.Exp, scale=-1.0)
        a = S.do(act, sil_e[:, 8:16], col("cond", 0, 8), ACT.Exp, scale=-1.0)
        V.wait(a)
        a = V.do(ts, sil_e, sil_e, 1.0, None, ADD)
        V.wait(a)
        a = V.do(nc.vector.reciprocal, sil_e, sil_e)
        V.wait(a)
        a = V.do(tt, SIL[:, 0:8], sil_e[:, 0:8], col("c", 0, 8), MUL)
        sil_tok = V.do(tt, SIL[:, 8:16], sil_e[:, 8:16], col("cond", 0, 8), MUL)

        PE.wait(s_small["x"])
        for q in range(4):
            b, pb = bank()
            for kk in range(2):
                k = 2 * q + kk
                for m in range(2):
                    tk = PE.do(tr, pb[:, kk * T + m * P:kk * T + m * P + P], XN[:, m, k * P:k * P + P], ident)
            S.wait(tk)
            r = S.do(act, xT[:, 2 * q:2 * q + 2, :], v3(pb[:, :], 2), ACT.Copy)
            free(b, r)
            x_tok[2 * q] = [r]
            x_tok[2 * q + 1] = [r]
        start_done = tk

        PE.wait(s_small["sgu_w"], s_small["sgu_b"])
        E_SWT = 16768
        swT = v3(ar(E_SWT, 1024), 8)
        swR = v3(ar(E_SWR, 1024), 8)
        ptok = []
        for q in range(2):
            b, pb = bank()
            for m in range(4):
                tk = PE.do(tr, pb[:, m * P:m * P + P], swR[:, 4 * q + m, :], ident)
            S.wait(tk)
            r = S.do(act, swT[:, 4 * q:4 * q + 4, :], v3(pb[:, :], 4), ACT.Copy)
            free(b, r)
            ptok.append(r)
        sw_tr = tk
        G.wait(*ptok)
        swt_tok = G.do(nc.gpsimd.affine_select, out=swT, in_=swT, compare_op=ALU.is_ge, fill=0.0, base=0,
                       pattern=[[0, 8], [1, P]], channel_multiplier=-1)
        bB = ar(E_BB, 1024)
        pend = []
        for q in range(2):
            b, pb = bank()
            tk = mmf(pb[:, :], ones[0:1, :], AR[0:1, E_BB + 512 * q:E_BB + 512 * q + 512])
            pend.append((b, pb, tk))
        for q, (b, pb, tk) in enumerate(pend):
            S.wait(pend[-1][2])
            bb_tok = S.do(act, bB[:, 512 * q:512 * q + 512], pb[:, :], ACT.Copy)
            free(b, bb_tok)

        def mod_cols(m, gname, goff, dst, toks):
            V.wait(*toks)
            return V.do(stt, out=dst, in0=m[:, 8:16], scalar=1.0, in1=col(gname, goff, 8), op0=ADD, op1=MUL)

        GS = PC[:, 48:56]
        ada_drain()
        ada_flush()
        g_tok = mod_cols(M0, "norm_g", 0, GS, [ada_out[1]])
        hp = norm_mod(GS, M0[:, 0:8], [g_tok, ada_out[0]])

        GT = v3(ar(0, 4096), 16)
        VV = v3(ar(4096, 2048), 2)
        UU = v3(ar(6144, 2048), 8)
        AP_ = v3(ar(8192, 2176), 8)
        S1 = v3(ar(10368, 2176), 8)
        S2 = v3(ar(12544, 2176), 8)
        YP = v3(ar(14720, 2048), 8)
        TMP = [ar(17792, 512), ar(18304, 512)]
        S.quiet(nc.scalar.preload_act_table_set, "silu_and_others")

        pads = []
        G.wait(start_done)
        for buf in (AP_, S1, S2):
            pads.append(G.do(nc.gpsimd.memset, buf[:, :, 0:16], 0.0))

        PE.wait(*hp)
        for j in range(4):
            r = cols_N(Unit("ein"), VV[:, :, 256 * j:256 * j + 256], [start_done])
        for m in range(2):
            S.wait(r)
            a = S.do(act, YP[:, 4 * m:4 * m + 4, :].rearrange("p a n -> p (a n)"), VV[:, m, :], ACT.Square,
                     accum_out=PC[:, 56 + m:57 + m])
        rs_t = (PC[:, 60:62], PC[:, 62:64])
        _, rs = rsqrt(PC[:, 58:60], PC[:, 56:58], 1.0 / D, [a], rs_t)
        vh_tok = []
        for m in range(2):
            V.wait(rs, r)
            vh_tok.append(V.do(ts, VV[:, m, :], VV[:, m, :], PC[:, 58 + m:59 + m], None, MUL))

        a_tok = []
        for j in range(4):
            def ev(pb, tk, j=j):
                S.wait(tk, start_done)
                r = S.do(act, AP_[:, 2 * j:2 * j + 2, 16:272], v3(pb[:, :], 2), ACT.Copy)
                a_tok.append(r)
                return [r]
            cols_T(Unit("ein"), None, ev)

        V.wait(*a_tok, *pads)
        p_tok = []
        src, toks = AP_, []
        for g, w in enumerate((2, 4, 8, 16)):
            dst = (S1, S2)[g % 2]
            half = w // 2
            V.wait(*toks)
            a = V.do(tt, dst[:, 2 * g:8, 16:272], src[:, 2 * g:8, 16:272], src[:, 2 * g:8, 16 - half:272 - half], ADD)
            V.wait(a)
            z = AP_[:, 2 * g:2 * g + 2, :]
            w_ = dst[:, 2 * g:2 * g + 2, :]
            y = YP[:, 2 * g:2 * g + 2, :]
            b1 = V.do(stt, out=y, in0=w_[:, :, 16:272], scalar=1.0 / w, in1=z[:, :, 16:272], op0=MUL, op1=SUB)
            V.wait(b1)
            b2 = V.do(tt, y[:, :, 0:16], w_[:, :, 16:32], ic[:, 2 * g:2 * g + 2, :], MUL)
            V.wait(b2)
            b3 = V.do(tt, y[:, :, 0:16], y[:, :, 0:16], z[:, :, 16:32], SUB)
            p_tok.append(b3)
            toks = [a]
            src = dst

        u_tok = []
        for j in range(4):
            def ev(pb, tk, j=j):
                S.wait(tk, start_done)
                r = S.do(act, UU[:, 2 * j:2 * j + 2, :], v3(pb[:, :], 2), ACT.Copy)
                u_tok.append(r)
                return [r]
            cols_T(Unit("ein"), None, ev)

        f2 = lambda x: x.rearrange("p a n -> p (a n)")
        pu = Unit("pool")
        yp_tok = []
        pl = [ypair(YP[:, 0:2, :].rearrange("p a n -> p (a n)"), [p_tok[0]])]
        for g in range(4):
            if g < 3:
                pl.append(ypair(f2(YP[:, 2 * g + 2:2 * g + 4, :]), [p_tok[g + 1]]))
            i, t = pl[g]
            if g % 2 == 0:
                H, L = pu.piece(g // 2)
            PE.wait(t)
            b, pb = bank()
            for m in range(2):
                for k in range(2):
                    kk = 2 * (g % 2) + k
                    tk = mm3(pb[:, m * T:m * T + T], (H[:, kk, m * P:m * P + P], L[:, kk, m * P:m * P + P]),
                             (YH[:, i, k, :], YL[:, i, k, :]), m == 0 and k == 0, k == 1)
            yfree[i] = [tk]
            if g % 2 == 1:
                pu.done(g // 2, tk)
            for m in range(2):
                n = 2 * g + m
                S.wait(tk, t)
                r = S.do(act, YP[:, n, :], pb[:, m * T:m * T + T], ACT.Copy, scale=col("pool_scale", n))
            yp_tok.append(r)
            free(b, r)

        PE.wait(*vh_tok, swt_tok)
        z_tok = []
        for q in range(4):
            b, pb = bank()
            for m in range(2):
                h = 2 * q + m
                for n in range(2):
                    tk = mmf(pb[:, m * T + n * P:m * T + n * P + P], VV[:, n, h * P:h * P + P], swT[:, h, :])
            for m in range(2):
                h = 2 * q + m
                V.wait(tk, bb_tok, *u_tok, sw_tr)
                a = V.do(stt, out=v3(TMP[m][:, 0:T], 2), in0=v3(pb[:, m * T:m * T + T], 2),
                         scalar=col("sgu_norm_g", h),
                         in1=bB[:, h * P:h * P + P].unsqueeze(1).to_broadcast([P, 2, P]), op0=MUL, op1=ADD)
                V.wait(a)
                r = V.do(tt, UU[:, h, :], TMP[m][:, 0:T], UU[:, h, :], MUL)
            z_tok.append(r)
            free(b, a)

        yf = []
        for j in range(8):
            def ev(pb, tk, j=j):
                g2 = f2(GT[:, 2 * j:2 * j + 2, :])
                r = silu_t(pb, tk, g2, [z_tok[-1]])
                V.wait(r, *yp_tok)
                other = YP[:, 2 * j:2 * j + 2, :] if j < 4 else UU[:, 2 * j - 8:2 * j - 6, :]
                yf.append(V.do(tt, g2, g2, f2(other), MUL))
                return [r]
            last_h = cols_T(Unit("ein"), None, ev)
        h_free.append(last_h)

        def out_proj(name, tiles, toks, n):
            pl = [ypair(tiles[j], toks[j]) for j in range(2)]
            for j in range(n):
                if j + 2 < n:
                    pl.append(ypair(tiles[j + 2], toks[j + 2]))
                tk = acc_rows(Unit(name), pl[j], j == 0, j == n - 1)
            return tk

        tk = out_proj("eout", [f2(GT[:, 2 * j:2 * j + 2, :]) for j in range(8)], [[t] for t in yf], 8)
        ada_flush()
        residual(M0[:, 16:24], tk, [ada_out[2]])
        even_done = tk

        V.wait(hp[-1])
        g_tok = mod_cols(M1, "norm_g", 8, GS, [ada_out[4]])
        hp = norm_mod(GS, M1[:, 0:8], [g_tok, ada_out[3]])
        S.quiet(nc.scalar.preload_act_table_set, "natural_log_exp_and_others")
        PE.wait(*hp)

        ao = even_done
        GV = v3(ar(4096, 2048), 2)
        SQ_ = v3(ar(6144, 2048), 8)
        SK_ = v3(ar(8192, 2048), 8)
        SV_ = v3(ar(10240, 2048), 2)
        GQ, GK = ar(12288, 1024), ar(13312, 1024)
        T0, T1, T2, T3, T4, T5 = (ar(14336 + 1024 * i, 1024) for i in range(6))

        gr = lambda x: x[:, :, :].rearrange("p a n -> p (a n)")
        grp = pair(gr(GRW), gr(GRH), gr(GRL), [s_small["glr"]])
        b, pb = bank()
        PE.wait(grp)
        for k in range(8):
            tk = mm3(pb[0:16, 0:T], (GRH[:, k, :], GRL[:, k, :]), hpair(k), k == 0, k == 7)
        GLT = AR[0:16, 4096:4352]
        S.wait(tk, ao)
        a = S.do(act, GLT, pb[0:16, 0:T], ACT.Copy)
        free(b, a)
        PE.wait(a, s_small["glw"])
        la_tok = []
        for q in range(2):
            b, pb = bank()
            for m in range(2):
                h = 2 * q + m
                tk = mmf(pb[:, m * T:m * T + T], GLW[:, h * P:h * P + P], GLT)
            glr_done = tk
            for m in range(2):
                h = 2 * q + m
                src = pb[:, m * T:m * T + T]
                e, la = T4[:, h * T:h * T + T], T0[:, h * T:h * T + T]
                S.wait(tk, ao)
                a = S.do(act, e, src, ACT.Abs, bias=col("gla_gate_b", h))
                S.wait(a)
                c = S.do(act, e, e, ACT.Exp, scale=-1.0)
                S.wait(c)
                c = S.do(act, e, e, ACT.Ln, bias=one_c)
                V.wait(a, ao)
                d = V.do(ts, la, src, col("gla_gate_b", h), 0.0, ADD, MIN)
                V.wait(d, c)
                la_tok.append(V.do(tt, la, la, e, SUB))
                S.wait(d)
            free(b, d, a)
        G.wait(ao, glr_done)
        a = G.do(nc.gpsimd.memset, T5, 1.0)
        G.wait(a)
        a = G.do(nc.gpsimd.memset, T5.rearrange("p (c n) -> p c n", n=64)[:, :, 0:1], 0.0)
        V.wait(a, *la_tok)
        bc_tok = V.do(nc.vector.tensor_tensor_scan, T1, T5, T0, 0.0, MUL, ADD)
        BC = T1.rearrange("p (c n) -> p c n", n=64)
        EBL = PC[:, 32:48]
        S.wait(bc_tok)
        ebl_tok = S.do(act, EBL.unsqueeze(2), BC[:, :, 63:64], ACT.Exp, scale=1.0 / 16)
        e1 = S.do(act, T0, T1, ACT.Exp, scale=1.0 / 16)
        e2 = S.do(act, T2, T1, ACT.Exp, scale=-1.0 / 16)
        V.wait(bc_tok)
        dd = V.do(tt, T3.rearrange("p (c n) -> p c n", n=64), BC[:, :, 63:64].to_broadcast([P, 16, 64]), BC, SUB)
        S.wait(dd)
        e3 = S.do(act, T3, T3, ACT.Exp, scale=1.0 / 16)

        qk_tok = []
        for j in range(4):
            def ev(pb, tk, j=j):
                dst = (GQ if j < 2 else GK)[:, (j % 2) * 512:(j % 2) * 512 + 512]
                S.wait(tk, ao)
                r = S.do(act, dst, pb[:, :], ACT.Copy, scale=float(P) ** -0.5 if j < 2 else 1.0)
                qk_tok.append(r)
                return [r]
            cols_T(Unit("oin"), None, ev)
        V.wait(*qk_tok, e1, e2, e3)
        qd = V.do(tt, GQ, GQ, T0, MUL)
        ki = V.do(tt, T2, T2, GK, MUL)
        ke = V.do(tt, T3, T3, GK, MUL)
        for j in range(4):
            gv_tok = cols_N(Unit("oin"), GV[:, :, 256 * j:256 * j + 256], [ao, glr_done])

        sqk_tok = []
        for j in range(8):
            def ev(pb, tk, j=j):
                jj = j % 4
                dst = (SQ_ if j < 4 else SK_)[:, 2 * jj:2 * jj + 2, :]
                S.wait(tk, ao)
                r = S.do(act, dst, v3(pb[:, :], 2), ACT.Copy, scale=float(P) ** -0.5 if j < 4 else 1.0)
                sqk_tok.append(r)
                return [r]
            cols_T(Unit("oin"), None, ev)
        for j in range(4):
            sv_tok = cols_N(Unit("oin"), SV_[:, :, 256 * j:256 * j + 256], [ao])

        g_toks = []
        g_e = [RT[:, 0:2, :].rearrange("p a n -> p (a n)"), RT[:, 2:4, :].rearrange("p a n -> p (a n)")]

        def gate_unit():
            j = len(g_toks)
            if j == 8:
                return

            def ev(pb, tk):
                g2 = f2(GT[:, 2 * j:2 * j + 2, :])
                e = g_e[j % 2]
                S.wait(tk, ao, *rt_last, *g_toks[-2:])
                a = S.do(act, e, pb[:, :], ACT.Exp, scale=-1.0)
                V.wait(a, *rt_last)
                a = V.do(ts, e, e, 1.0, None, ADD)
                V.wait(a)
                a = V.do(nc.vector.reciprocal, e, e)
                V.wait(a)
                r = V.do(tt, g2, pb[:, :], e, MUL)
                g_toks.append(r)
                return [r]
            g_last[:] = [cols_T(Unit("oin"), None, ev)]

        g_last = []
        PE.wait(ke, ki, qd)
        att_tok, kt_tok = [], []
        AT = T5.rearrange("p (b h t) -> p b h t", b=2, h=4)
        KT = T4.rearrange("p (b h t) -> p b h t", b=2, h=4)
        for blk in range(2):
            b, pb = bank()
            for h in range(4):
                sl = slice(h * T + blk * P, h * T + blk * P + P)
                tk = PE.do(tr, pb[:, h * P:h * P + P], T3[:, sl], ident)
            S.wait(tk, *la_tok)
            r = S.do(act, KT[:, blk], v3(pb[:, :], 4), ACT.Copy)
            free(b, r)
            kt_tok.append(r)
        t3_done = tk
        for blk in range(2):
            b, pb = bank()
            for h in range(4):
                sl = slice(h * T + blk * P, h * T + blk * P + P)
                tk = mmf(pb[:, h * P:h * P + P], T2[:, sl], GQ[:, sl])
            S.wait(tk, bc_tok)
            r = S.do(act, AT[:, blk], v3(pb[:, :], 4), ACT.Copy)
            free(b, r)
            G.wait(r)
            r = G.do(nc.gpsimd.affine_select, out=AT[:, blk], in_=AT[:, blk], compare_op=ALU.is_ge, fill=0.0,
                     base=0, pattern=[[0, 4], [1, P]], channel_multiplier=-1)
            G.wait(r)
            r = G.do(nc.gpsimd.memset, AT[0:64, blk, :, 64:128], 0.0)
            att_tok.append(r)
        att_pe = tk

        ST = [v3(GK, 4), v3(T0, 4), v3(T1, 4)]
        PE.wait(*kt_tok, gv_tok)
        st_tok = []
        prev = None
        for c in range(3):
            gate_unit()
            rr = slice(64 * (c % 2), 64 * (c % 2) + 64)
            cur_t = []
            for q in range(2):
                b, pb = bank()
                for m in range(2):
                    h = 2 * q + m
                    tk = mmf(pb[:, m * T:m * T + T], KT[rr, c // 2, h, :], GV[rr, c // 2, h * T:h * T + T])
                for m in range(2):
                    h = 2 * q + m
                    V.wait(tk, ke, qd, dd, ebl_tok, e3, e1, e2)
                    if c == 0:
                        r = V.do(nc.vector.tensor_copy, ST[0][:, h, :], pb[:, m * T:m * T + T])
                    else:
                        V.wait(*prev)
                        r = V.do(stt, out=ST[c][:, h, :], in0=ST[c - 1][:, h, :],
                                 scalar=EBL[:, 4 * h + c:4 * h + c + 1], in1=pb[:, m * T:m * T + T],
                                 op0=MUL, op1=ADD)
                    cur_t.append(r)
                free(b, r)
            prev = cur_t
            st_tok.append(cur_t)
        gate_unit()

        YC = v3(ar(16384, 2048), 8)
        PE.wait(*att_tok)
        yc_tok = []
        for h in range(4):
            b, pb = bank()
            for v in range(2):
                for blk in range(2):
                    tk = mmf(pb[:, v * T + blk * P:v * T + blk * P + P], GV[:, blk, h * T + v * P:h * T + v * P + P],
                             AT[:, blk, h, :], start=(v == 0 and blk == 0), stop=False)
            for v in range(2):
                for c in range(1, 4):
                    PE.wait(*st_tok[c - 1])
                    tk = mmf(pb[:, v * T + 64 * c:v * T + 64 * c + 64], ST[c - 1][:, h, v * P:v * P + P],
                             GQ[:, h * T + 64 * c:h * T + 64 * c + 64], start=False, stop=(c == 3))
            S.wait(tk, t3_done, att_pe)
            r = S.do(act, YC[:, 2 * h:2 * h + 2, :], v3(pb[:, :], 2), ACT.Copy)
            free(b, r)
            yc_tok.append(r)
        gla_pe = tk
        gate_unit()
        ycn = []

        def gla_norm(q):
            b, pb = bank()
            for m in range(2):
                h = 2 * q + m
                tk = sumsq(pb[:, m * T:m * T + T], [YC[:, 2 * h, :], YC[:, 2 * h + 1, :]], [[yc_tok[h]]] * 2)
            o = 14336 + 512 * q
            a, z = rsqrt(ar(o, 512), pb[:, :], 1.0 / 256, [tk, gla_pe], (ar(15360, 512), ar(15872, 512)))
            free(b, a)
            for m in range(2):
                h = 2 * q + m
                for v in range(2):
                    n = 2 * h + v
                    V.wait(z)
                    ycn.append(V.do(stt, out=YC[:, n, :], in0=YC[:, n, :], scalar=col("gla_norm_g", n),
                                    in1=ar(o + m * T, T), op0=MUL, op1=MUL))

        PE.wait(*sqk_tok, sv_tok)
        sb_free = [[gla_pe], [gla_pe]]

        def sb_scores(h):
            b, pb = bank()
            mmf(pb[:, 0:256], SK_[:, h, 0:128], SQ_[:, h, :], True, True)
            tk = mmf(pb[:, 256:384], SK_[:, h, 128:256], SQ_[:, h, 128:256], False, True)
            o = 18432 + 768 * (h % 2)
            e, sp = ar(o, 384), ar(o + 384, 384)
            S.wait(tk, *sb_free[h % 2])
            a = S.do(act, e, pb[:, 0:384], ACT.Abs)
            S.wait(a)
            c = S.do(act, e, e, ACT.Exp, scale=-1.0)
            S.wait(c)
            c = S.do(act, e, e, ACT.Ln, bias=one_c)
            V.wait(c, *sb_free[h % 2])
            d = V.do(stt, out=sp, in0=pb[:, 0:384], scalar=0.0, in1=e, op0=MAX, op1=ADD)
            G.wait(d)
            for o2 in (0, 256):
                m = G.do(nc.gpsimd.affine_select, out=sp[:, o2:o2 + P], in_=sp[:, o2:o2 + P], compare_op=ALU.is_gt,
                         fill=0.0, base=0, pattern=[[1, P]], channel_multiplier=-1)
            return b, pb, sp, e, m, d, a

        def sb_weights(st):
            b, pb, sp, w, m, d, a = st
            PE.wait(m, d, a)
            mmf(pb[:, 0:256], negU, sp[:, 0:256], False, False)
            mmf(pb[:, 128:256], negones, sp[:, 256:384], False, False)
            tk = mmf(pb[:, 256:384], negU, sp[:, 256:384], False, True)
            S.wait(tk, d)
            r = S.do(act, w, pb[:, 0:384], ACT.Exp)
            free(b, r)
            G.wait(r)
            for o2 in (0, 256):
                m = G.do(nc.gpsimd.affine_select, out=w[:, o2:o2 + P], in_=w[:, o2:o2 + P], compare_op=ALU.is_gt,
                         fill=0.0, base=0, pattern=[[1, P]], channel_multiplier=-1)
            return w, m, r

        def sb_out(h, w, m, r, pb, half):
            PE.wait(m, r)
            o = pb[:, half * T:half * T + T]
            mmf(o, SV_[:, 0, h * P:h * P + P], w[:, 0:256], half == 0, False)
            tk = mmf(o[:, 128:256], SV_[:, 1, h * P:h * P + P], w[:, 256:384], False, True)
            sb_free[h % 2] = [tk]
            return tk

        yf = []

        def y_gla(j):
            g2 = f2(GT[:, 2 * j:2 * j + 2, :])
            V.wait(g_toks[j], *ycn)
            yf.append(V.do(tt, g2, g2, f2(YC[:, 2 * j:2 * j + 2, :]), MUL))

        places = []
        out_n = [0]

        def out_unit():
            j = out_n[0]
            out_n[0] += 1
            while len(places) < min(j + 2, len(yf)):
                q = len(places)
                places.append(ypair(f2(GT[:, 2 * q:2 * q + 2, :]), [yf[q]]))
            return acc_rows(Unit("oout"), places[j], j == 0, j == 7)

        for q in range(4):
            s0 = sb_scores(2 * q)
            s1 = sb_scores(2 * q + 1)
            if q == 0:
                gate_unit()
            elif q == 1:
                gate_unit()
                h_free.append(g_last[0])
            else:
                out_unit()
            w0 = sb_weights(s0)
            w1 = sb_weights(s1)
            if q < 2:
                gla_norm(q)
                y_gla(2 * q)
                y_gla(2 * q + 1)
            if q == 0:
                gate_unit()
            else:
                out_unit()
            b, pb = bank()
            sb_out(2 * q, *w0, pb, 0)
            tk = sb_out(2 * q + 1, *w1, pb, 1)
            j = 4 + q
            g2 = f2(GT[:, 2 * j:2 * j + 2, :])
            V.wait(tk, g_toks[j])
            a = V.do(tt, g2, g2, pb[:, :], MUL)
            free(b, a)
            yf.append(a)
        while out_n[0] < 8:
            tk = out_unit()
        S.quiet(nc.scalar.preload_act_table_set, "silu_and_others")
        ada_flush()
        residual(M1[:, 16:24], tk, [ada_out[5]])
        odd_done = tk

        r = norm_r([xT[:, k, :] for k in range(8)], x_tok, D)
        for k in range(8):
            V.wait(r, *x_tok[k])
            a = V.do(stt, out=xT[:, k, :], in0=xT[:, k, :], scalar=col("final_g", k), in1=RT[:, 0, :],
                     op0=MUL, op1=MUL)
            x_tok[k] = [a]
        rt_last.append(a)

        ao = odd_done
        COS = v3(ar(2048, 4096), 16)
        SIN = v3(ar(6144, 4096), 16)
        BT = [v3(ar(10240 + 512 * i, 512), 4) for i in range(2)]
        CT = [v3(ar(11264 + 512 * i, 512), 4) for i in range(3)]
        BR = [v3(ar(12800 + 256 * i, 256), 16) for i in range(2)]
        BB = [v3(ar(13312 + 512 * i, 512), 16) for i in range(2)]
        CR = [v3(ar(14336 + 256 * i, 256), 4) for i in range(2)]
        CM = [ar(14848 + 512 * i, 512) for i in range(2)]
        LC = v3(ar(20288, 16 * 12), 12)
        S5T = [ar(15872 + 256 * i, 256) for i in range(3)]
        G.wait(ao)
        for i, nm in enumerate(("ssm_b_re_2", "ssm_b_im_2")):
            small(G, nc.gpsimd.dma_start, nm, BR[i], I[nm].rearrange("o (j e) p c -> (o e p) j c", e=2)
                  if False else I[nm][0].rearrange("(j e) p c -> (e p) j c", e=2))
        for i, nm in enumerate(("ssm_c_re_2", "ssm_c_im_2")):
            small(G, nc.gpsimd.dma_start, nm, CR[i], I[nm][0].rearrange("(m g) c p -> (g c) m p", g=8))

        def s5_coefs():
            lre, lim = col("lam_re", 0, 16), col("lam_im", 0, 16)
            A_, TH, RR, SN, CN, T1_, T2_, T3_, CFR, CFI, X1, X2 = (LC[:, i, :] for i in range(12))
            V.wait(dt_tok, vc_tok, ao)
            a = V.do(tt, A_, lre, DTC, MUL)
            a = V.do(tt, TH, lim, DTC, MUL)
            S.wait(a)
            rr = S.do(act, RR, A_, ACT.Exp)
            V.wait(a)
            a = V.do(ts, T1_, TH, 1.0 / TWO_PI, MAGIC, MUL, ADD)
            V.wait(a)
            a = V.do(ts, T1_, T1_, MAGIC, None, SUB)
            V.wait(a)
            a = V.do(stt, out=TH, in0=T1_, scalar=-TP_HI, in1=TH, op0=MUL, op1=ADD)
            V.wait(a)
            a = V.do(stt, out=TH, in0=T1_, scalar=-TP_LO, in1=TH, op0=MUL, op1=ADD)
            V.wait(a)
            a = V.do(ts, TH, TH, float(np.pi), -float(np.pi), MIN, MAX)
            S.wait(a)
            sn = S.do(act, SN, TH, ACT.Sin)
            c = S.do(act, CN, TH, ACT.Abs)
            S.wait(c)
            cn = S.do(act, CN, CN, ACT.Sin, scale=-1.0, bias=hpi_c)
            V.wait(sn, cn, rr)
            a = V.do(tt, CN, CN, RR, MUL)
            b_ = V.do(tt, SN, SN, RR, MUL)
            V.wait(a, b_)
            a = V.do(ts, CN, CN, 1.0, None, SUB)
            c = V.do(tt, T2_, lre, lre, MUL)
            d = V.do(tt, T3_, lim, lim, MUL)
            V.wait(a, c, d)
            a = V.do(tt, T2_, T2_, T3_, ADD)
            V.wait(a)
            a = V.do(nc.vector.reciprocal, T2_, T2_)
            c = V.do(tt, X1, CN, lre, MUL)
            d = V.do(tt, X2, SN, lim, MUL)
            V.wait(c, d, a)
            c = V.do(tt, CFR, X1, X2, ADD)
            V.wait(c)
            d = V.do(tt, X1, SN, lre, MUL)
            e = V.do(tt, X2, CN, lim, MUL)
            V.wait(d, e)
            d = V.do(tt, CFI, X1, X2, SUB)
            V.wait(d, c)
            c = V.do(tt, CFR, CFR, T2_, MUL)
            d = V.do(tt, CFI, CFI, T2_, MUL)
            return RR, TH, CFR, CFI, [c, d]

        def s5_blocks(CFR, CFI, cf_tok):
            bd = lambda x: x.unsqueeze(2).to_broadcast([P, 16, 16])
            t = [v3(S5T[i], 16) for i in range(3)]
            G.wait(ao)
            z = [G.do(nc.gpsimd.memset, BB[i].rearrange("p a n -> p (a n)"), 0.0) for i in range(2)]
            V.wait(s_small["ssm_b_re_2"], s_small["ssm_b_im_2"], *cf_tok, *z)
            a = V.do(tt, t[0], BR[0], bd(CFR), MUL)
            b_ = V.do(tt, t[1], BR[1], bd(CFI), MUL)
            V.wait(a, b_)
            for e in range(2):
                r = slice(64 * e, 64 * e + 64)
                a = V.do(tt, BB[0][r, :, 16 * e:16 * e + 16], t[0][r], t[1][r], SUB)
            V.wait(a)
            c = V.do(tt, t[0], BR[0], bd(CFI), MUL)
            b_ = V.do(tt, t[1], BR[1], bd(CFR), MUL)
            V.wait(c, b_)
            for e in range(2):
                r = slice(64 * e, 64 * e + 64)
                c = V.do(tt, BB[1][r, :, 16 * e:16 * e + 16], t[0][r], t[1][r], ADD)
            PE.wait(c, a)
            res = []
            for i in range(2):
                b, pb = bank()
                for m in range(4):
                    tk = PE.do(tr, pb[:, m * P:m * P + P], BB[i][:, 4 * m:4 * m + 4, :].rearrange("p a n -> p (a n)"),
                               ident)
                S.wait(tk)
                r = S.do(act, BT[i].rearrange("p a n -> p (a n)"), pb[:, :], ACT.Copy)
                free(b, r)
                res.append(r)
            V.wait(s_small["ssm_c_re_2"], s_small["ssm_c_im_2"])
            for i in range(2):
                b, pb = bank()
                cm = CM[i].rearrange("p (m e n) -> p m e n", m=4, e=2)
                for e in range(2):
                    c = V.do(ts, cm[:, :, e, :], CR[i], cst[:, C_M2 + e:C_M2 + e + 1], None, MUL)
                PE.wait(c)
                for m in range(4):
                    tk = PE.do(tr, pb[:, m * P:m * P + P], CM[i][:, m * P:m * P + P], ident)
                S.wait(tk)
                if i == 0:
                    S.do(act, CT[0].rearrange("p a n -> p (a n)"), pb[:, :], ACT.Copy)
                    r = S.do(act, CT[1].rearrange("p a n -> p (a n)"), pb[:, :], ACT.Copy, scale=-1.0)
                else:
                    r = S.do(act, CT[2].rearrange("p a n -> p (a n)"), pb[:, :], ACT.Copy, scale=-1.0)
                free(b, r)
                res.append(r)
            return res

        tab_tok = {}
        r_tab = []
        nt = [0]

        def s5_table(j, TH):
            x_ = ar(16640 + 256 * (j % 4), 256)
            k_ = ar(17664 + 256 * (j % 4), 256)
            S.wait(*s5c["tok"], *tab_tok.get(j - 4, []))
            a = S.do(act, x_, tvec, ACT.Copy, scale=TH[:, j:j + 1])
            V.wait(a)
            a = V.do(ts, k_, x_, 1.0 / TWO_PI, MAGIC, MUL, ADD)
            V.wait(a)
            a = V.do(ts, k_, k_, MAGIC, None, SUB)
            V.wait(a)
            a = V.do(stt, out=x_, in0=k_, scalar=-TP_HI, in1=x_, op0=MUL, op1=ADD)
            V.wait(a)
            a = V.do(stt, out=x_, in0=k_, scalar=-TP_LO, in1=x_, op0=MUL, op1=ADD)
            V.wait(a)
            a = V.do(ts, x_, x_, float(np.pi), -float(np.pi), MIN, MAX)
            S.wait(a)
            s = S.do(act, SIN[:, j, :], x_, ACT.Sin)
            c = S.do(act, COS[:, j, :], x_, ACT.Abs)
            S.wait(c)
            c = S.do(act, COS[:, j, :], COS[:, j, :], ACT.Sin, scale=-1.0, bias=hpi_c)
            tab_tok[j] = [s, c]

        s5c = {}

        def ffn(tag, hook=None):
            pend = None
            for blk in range(12):
                new = None
                if blk < 11:
                    bks = [bank(), bank()]
                    for part, nm in enumerate((f"{tag}g", f"{tag}u")):
                        u = Unit(nm)
                        for half in range(2):
                            H, L = u.piece(half)
                            for m in range(2):
                                for kk in range(4):
                                    sl = slice(m * P, m * P + P)
                                    tk = mm3(bks[m][1][:, part * T:part * T + T], (H[:, kk, sl], L[:, kk, sl]),
                                             hpair(4 * half + kk), part == 0 and half == 0 and kk == 0,
                                             half == 1 and kk == 3)
                            u.done(half, tk)
                    o = 512 * (blk % 4)
                    toks = []
                    for m in range(2):
                        pb = bks[m][1]
                        f = ar(o + T * m, T)
                        r = silu_t(pb, tk, f, f_free[blk % 4], T)
                        V.wait(r)
                        r = V.do(tt, f, f, pb[:, T:2 * T], MUL)
                        free(bks[m][0], r)
                        toks.append(r)
                    new = (ypair(ar(o, 512), toks), blk)
                    f_free[blk % 4] = [new[0][1]]
                    last_h = tk
                if pend is not None:
                    tk = acc_rows(Unit(f"{tag}d"), pend[0], pend[1] == 0, pend[1] == 10)
                pend = new
                if hook is not None:
                    hook(blk)
            h_free.append(last_h)
            return tk

        HG = PC[:, 32:40]

        def ffn_layer(tag, mo, gname, hook=None):
            M = M2[:, mo:mo + 24]
            c0 = 6 + mo // 8
            ada_flush()
            V.wait(*hp_last)
            g = mod_cols(M, gname, 0, GS, [ada_out[c0 + 1]])
            hp = norm_mod(GS, M[:, 0:8], [g, ada_out[c0]])
            del hp_last[:]
            hp_last.append(hp[-1])
            PE.wait(*hp)
            tk = ffn(tag, hook)
            ada_flush()
            V.wait(*st_tok[-1], ada_out[c0 + 2])
            hg = V.do(ts, HG, M[:, 16:24], 0.5, None, MUL)
            residual(HG, tk, [hg])
            return tk

        hp_last = [hp[-1]]
        f_free = [[ao]] * 4

        def hook(blk):
            if blk == 0:
                RR, TH, CFR, CFI, t = s5_coefs()
                s5c["RR"], s5c["TH"], s5c["tok"] = RR, TH, t
                s5c["blk"] = s5_blocks(CFR, CFI, t)
            elif 1 <= blk <= 8:
                s5_table(2 * blk - 2, s5c["TH"])
                s5_table(2 * blk - 1, s5c["TH"])

        f1_done = ffn_layer("f1", 0, "ffn1_norm", hook)

        M = M2[:, 24:48]
        ada_flush()
        V.wait(*hp_last)
        g = mod_cols(M, "mix_norm", 0, GS, [ada_out[10]])
        hp = norm_mod(GS, M[:, 0:8], [g, ada_out[9]])
        hp_last[:] = [hp[-1]]
        PE.wait(*hp)
        UT = v3(ar(12800, 1024), 4)
        BG = v3(ar(13824, 1024), 4)
        ZP = v3(ar(14848, 1032), 4)
        YCV = v3(ar(15880, 1024), 4)
        YS = v3(ar(16904, 1024), 4)
        PT = [ar(17928 + 256 * i, 256) for i in range(6)] + [ar(256 * i, 256) for i in range(6)]
        MT = [ar(2048, 1024), ar(3072, 1024)]
        prep_done = [s5c["blk"][-1]] + tab_tok[14] + tab_tok[15]
        u_tok = []
        for j in range(2):
            def ev(pb, tk, j=j):
                S.wait(tk, f1_done, *prep_done)
                r = S.do(act, UT[:, 2 * j:2 * j + 2, :], v3(pb[:, :], 2), ACT.Copy)
                u_tok.append(r)
                return [r]
            cols_T(Unit("win"), None, ev)

        cv = {}
        cv_tok = []

        def win_c(j):
            def ev(pb, tk):
                S.wait(tk, *prep_done)
                r = S.do(act, ZP[:, 2 * j:2 * j + 2, 2:258], v3(pb[:, :], 2), ACT.Copy)
                cv[("c", j)] = r
                return [r]
            cols_T(Unit("win"), None, ev)

        def win_v(j):
            def ev(pb, tk):
                V.wait(tk, cv[("c", j)])
                r = V.do(tt, ZP[:, 2 * j:2 * j + 2, 2:258], ZP[:, 2 * j:2 * j + 2, 2:258], v3(pb[:, :], 2), MUL)
                cv[("z", j)] = r
                return [r]
            cols_T(Unit("win"), None, ev)

        def win_b(j):
            def ev(pb, tk):
                S.wait(tk, *prep_done)
                r = S.do(act, BG[:, 2 * j:2 * j + 2, :], v3(pb[:, :], 2), ACT.Copy)
                cv[("b", j)] = r
                return [r]
            return cols_T(Unit("win"), None, ev)

        G.wait(*prep_done)
        zp_tok = G.do(nc.gpsimd.memset, ZP[:, :, 0:2], 0.0)

        def conv_tile(n):
            y = YCV[:, n, :]
            V.wait(cv[("z", n // 2)], cv[("b", n // 2)], zp_tok)
            a = V.do(ts, y, ZP[:, n, 2:258], col("conv_w", 8 + n), None, MUL)
            V.wait(a)
            a = V.do(stt, out=y, in0=ZP[:, n, 1:257], scalar=col("conv_w", 4 + n), in1=y, op0=MUL, op1=ADD)
            V.wait(a)
            a = V.do(stt, out=y, in0=ZP[:, n, 0:256], scalar=col("conv_w", n), in1=y, op0=MUL, op1=ADD)
            V.wait(a)
            cv_tok.append(V.do(tt, y, y, BG[:, n, :], MUL))

        yb = []
        PE.wait(*u_tok, *s5c["blk"], *acc_free)
        pt_free = {0: [], 1: []}
        ys_toks = []

        def s5_tile(j, first):
            m, jj = j // 4, j % 4
            b, pb = bank()
            r = slice(32 * jj, 32 * jj + 32)
            PE.quiet(mm, pb[:, 0:T], BT[0][r, m, :], UT[r, m, :], start=True, stop=True, skip_group_check=True)
            tk = mmf(pb[:, T:2 * T], BT[1][r, m, :], UT[r, m, :], False, True)
            o = 6 * (j % 2)
            p1, p2, p3, p4, zr, zi = PT[o:o + 6]
            C_, S_ = COS[:, j, :], SIN[:, j, :]
            V.wait(tk, *tab_tok[j], *pt_free[j % 2])
            a1 = V.do(tt, p1, pb[:, 0:T], C_, MUL)
            a2 = V.do(tt, p2, pb[:, T:2 * T], S_, MUL)
            a3 = V.do(tt, p3, pb[:, T:2 * T], C_, MUL)
            a4 = V.do(tt, p4, pb[:, 0:T], S_, MUL)
            free(b, a4)
            G.wait(a2)
            g1 = G.do(nc.gpsimd.tensor_tensor, p1, p1, p2, ADD)
            G.wait(a4)
            g2 = G.do(nc.gpsimd.tensor_tensor, p3, p3, p4, SUB)
            return j, g1, g2

        def s5_rest(st):
            j, g1, g2 = st
            m, jj = j // 4, j % 4
            o = 6 * (j % 2)
            p1, p2, p3, p4, zr, zi = PT[o:o + 6]
            C_, S_ = COS[:, j, :], SIN[:, j, :]
            rb = s5c["RR"][:, j:j + 1].to_broadcast([P, T])
            V.wait(g1)
            s1 = V.do(nc.vector.tensor_tensor_scan, zr, rb, p1, 0.0, MUL, ADD)
            V.wait(g2)
            s2 = V.do(nc.vector.tensor_tensor_scan, zi, rb, p3, 0.0, MUL, ADD)
            V.wait(s1)
            q1 = V.do(tt, p1, C_, zr, MUL)
            q2 = V.do(tt, p2, S_, zr, MUL)
            V.wait(s2)
            q3 = V.do(tt, p3, S_, zi, MUL)
            q4 = V.do(tt, p4, C_, zi, MUL)
            PE.wait(q1, q2, q3, q4)
            r = slice(32 * jj, 32 * jj + 32)
            o_ = pacc[r, 2 * m, :]
            PE.quiet(mm, o_, CT[0][:, m, r], p1, start=True, stop=False, skip_group_check=True)
            PE.quiet(mm, o_, CT[1][:, m, r], p3, start=False, stop=False, skip_group_check=True)
            PE.quiet(mm, o_, CT[2][:, m, r], p2, start=False, stop=False, skip_group_check=True)
            tk = mmf(o_, CT[2][:, m, r], p4, False, True)
            pt_free[j % 2] = [tk]
            if jj == 3:
                V.wait(tk, *prep_done)
                ys_toks.append(V.do(stt, out=YS[:, m, :], in0=UT[:, m, :], scalar=col("ssm_d", m),
                                    in1=pacc[:, 2 * m, :], op0=MUL, op1=ADD))

        jobs = [lambda: win_c(0), lambda: win_c(1), lambda: win_v(0), lambda: win_v(1), lambda: win_b(0),
                lambda: win_b(1)]
        prev = None
        for j in range(16):
            cur_s = s5_tile(j, j % 4 == 0)
            if j % 2 == 0 and jobs:
                last_h = jobs.pop(0)()
            if prev is not None:
                s5_rest(prev)
            prev = cur_s
            if j >= 12:
                conv_tile(j - 12)
        s5_rest(prev)
        h_free.append(last_h)
        acc_free[:] = [ys_toks[-1]]

        def rms_half(tiles, toks, gname):
            b, pb = bank()
            r = sumsq(pb[:, 0:T], tiles, toks)
            V.wait(*rt_last)
            a, z = rsqrt(RT[:, 0, :], pb[:, 0:T], 1.0 / 512, [r], (RT[:, 1, :], RT[:, 2, :]))
            free(b, a)
            for n in range(4):
                V.wait(z)
                a = V.do(stt, out=tiles[n], in0=tiles[n], scalar=col(gname, n), in1=RT[:, 0, :], op0=MUL, op1=MUL)
            rt_last[:] = [a]
            return a

        YSf = YS.rearrange("p a n -> p (a n)")
        E1, E2 = MT
        S.wait(*ys_toks, *pt_free[0], *pt_free[1])
        a = S.do(act, E1, YSf, ACT.Square)
        V.wait(a)
        a = V.do(ts, E1, E1, GELU_C * 0.044715, GELU_C, MUL, ADD)
        V.wait(a, *ys_toks)
        a = V.do(tt, E1, E1, YSf, MUL)
        S.wait(a)
        a = S.do(act, E1, E1, ACT.Tanh, scale=0.5)
        V.wait(a)
        a = V.do(ts, E1, E1, 0.5, 0.5, MUL, ADD)
        V.wait(a)
        a = V.do(tt, YSf, YSf, E1, MUL)
        gl = [ypair(YSf[:, 512 * q:512 * q + 512], [a]) for q in range(2)]
        cvn = rms_half([YCV[:, n, :] for n in range(4)], [[t] for t in cv_tok], "out_norm_conv")
        NGB = PC[:, 40:44]
        V.wait(vc_tok, ebl_tok)
        nb = V.do(ts, NGB, col("glu_b", 0, 4), 0.5, None, MUL)
        u = Unit("glu")
        bks = [bank(), bank()]
        for half in range(2):
            H, L = u.piece(half)
            i, t = gl[half]
            PE.wait(t)
            for n in range(4):
                for kk in range(2):
                    sl = slice(n * P, n * P + P)
                    tk = mm3(bks[n // 2][1][:, (n % 2) * T:(n % 2) * T + T], (H[:, kk, sl], L[:, kk, sl]),
                             (YH[:, i, kk, :], YL[:, i, kk, :]), half == 0 and kk == 0 and n % 2 == 0,
                             half == 1 and kk == 1)
            yfree[i] = [tk]
            u.done(half, tk)
        S.wait(tk, nb, *pt_free[0], *pt_free[1])
        for n in range(4):
            r = S.do(act, E2[:, n * T:n * T + T], bks[n // 2][1][:, (n % 2) * T:(n % 2) * T + T], ACT.Tanh,
                     scale=0.5, bias=NGB[:, n:n + 1])
        free(bks[0][0], r)
        free(bks[1][0], r)
        V.wait(r)
        a = V.do(ts, E2, E2, 0.5, 0.5, MUL, ADD)
        V.wait(a)
        a = V.do(tt, YSf, YSf, E2, MUL)
        ysn = rms_half([YS[:, n, :] for n in range(4)], [[a]] * 4, "out_norm_ssm")
        YCf = YCV.rearrange("p a n -> p (a n)")
        tk = out_proj("wout", [YCf[:, 0:512], YCf[:, 512:1024], YSf[:, 0:512], YSf[:, 512:1024]],
                      [[cvn], [cvn], [ysn], [ysn]], 4)
        ada_flush()
        residual(M[:, 16:24], tk, [ada_out[11]])
        f_free[:] = [[tk]] * 4

        f2_done = ffn_layer("f2", 48, "ffn2_norm")

        r = norm_r([xT[:, k, :] for k in range(8)], x_tok, D)
        OUT = v3(ar(4096, 2048), 2)
        S.wait(pt_free[0][0], pt_free[1][0])
        st = []
        for k in range(8):
            V.wait(r, *x_tok[k])
            a = V.do(stt, out=xT[:, k, :], in0=xT[:, k, :], scalar=col("final_norm", k), in1=RT[:, 0, :],
                     op0=MUL, op1=MUL)
            st.append(a)
        for m in range(2):
            for q in range(2):
                b, pb = bank()
                for kk in range(4):
                    k = 4 * q + kk
                    PE.wait(st[k])
                    tk = PE.do(tr, pb[:, kk * P:kk * P + P], xT[:, k, m * P:m * P + P], ident)
                S.wait(tk, ys_toks[-1])
                o_tok = S.do(act, OUT[:, m, 512 * q:512 * q + 512], pb[:, :], ACT.Copy)
                free(b, o_tok)
            S.wait(o_tok)
            so = sem(f"s_out{m}")
            S.dma(nc.scalar.dma_start, out[0, m * P:m * P + P, :], OUT[:, m, :], so)
            S.wait((so, 16)) if m == 1 else None
            if m == 0:
                so0 = so
        S.wait((so0, 16))

        assert cur[0] == len(units)
        for i, (nm, src, k, n) in enumerate(units):
            if i >= RING:
                SP.wait(*unit_free[i - RING])
            SP.dma(nc.sync.dma_start, v3(ring[:, i % RING, 0:k * n], k), src, s_ring[i % RING])

        block = ctx.enter_context(nc.Block())

        @block.sync
        def _(eng):
            SP.emit(eng)

        @block.tensor
        def _(eng):
            PE.emit(eng)

        @block.vector
        def _(eng):
            V.emit(eng)

        @block.scalar
        def _(eng):
            S.emit(eng)

        @block.gpsimd
        def _(eng):
            G.emit(eng)


_INS = ["x", "c", "ada_w", "ada_b", "norm_g", "even_in_w", "pool_w", "pool_scale", "sgu_norm_g", "sgu_w", "sgu_b",
        "even_out_w", "odd_in_w", "gla_gate_w", "gla_gate_b", "gla_norm_g", "odd_out_w", "final_g", "cond_2",
        "w_mod_2", "b_mod_2", "ffn1_norm_2", "ffn1_w_gate_2", "ffn1_w_up_2", "ffn1_w_down_2", "mix_norm_2",
        "w_in_2", "conv_w_2", "lambda_re_2", "lambda_im_2", "log_dt_2", "ssm_b_re_2", "ssm_b_im_2", "ssm_c_re_2",
        "ssm_c_im_2", "ssm_d_2", "glu_w_2", "glu_b_2", "out_norm_conv_2", "out_norm_ssm_2", "w_out_2",
        "ffn2_norm_2", "ffn2_w_gate_2", "ffn2_w_up_2", "ffn2_w_down_2", "final_norm_2"]


def kernel(**inputs):
    import concourse.bacc as _bacc
    from concourse.bass_utils import run_bass_kernel_spmd as _run

    nc = _bacc.Bacc("TRN2", target_bir_lowering=False, num_devices=1)
    arrays, aps = {}, {}
    given = {n: np.ascontiguousarray(inputs[n]) for n in _INS}
    given["consts"] = constants()
    for name, a in given.items():
        arrays[f"in_{name}"] = a
        aps[name] = nc.dram_tensor(f"in_{name}", a.shape, mybir.dt.from_np(a.dtype), kind="ExternalInput").ap()
    out = nc.dram_tensor("out_0", (1, T, D), F32, kind="ExternalOutput").ap()
    build(nc, aps, out)
    r = _run(nc, [arrays], core_ids=[0])
    return r.results[0]["out_0"]
```

```python
from contextlib import ExitStack

import numpy as np
import concourse.bass as bass
from concourse import mybir

F32 = mybir.dt.float32
F32R = mybir.dt.float32r
U32 = mybir.dt.uint32
I32 = mybir.dt.int32
ALU = mybir.AluOpType
ACT = mybir.ActivationFunctionType
MUL, ADD, SUB, MAX, MIN = ALU.mult, ALU.add, ALU.subtract, ALU.max, ALU.min

P = 128
T = 256
D = 1024
EPS = 1e-6
TWO_PI = 6.283185307179586
TP_HI = 6.28125
TP_LO = TWO_PI - TP_HI
MAGIC = 12582912.0
GELU_C = 2.0 * 0.7978845608028654

RING = 10
NH, NL = 4, 4
AHEAD_H, AHEAD_L = 3, 2
WORDS = 20480
RSQRT_MAGIC = 1597463007.0

C_ID, C_ONE, C_NU, C_NONE, C_IC, C_T, C_M2, C_K = 0, 128, 256, 384, 512, 640, 896, 898
C_ALL = 902


def constants():
    c = np.zeros((P, C_ALL), np.float32)
    i = np.arange(P)
    c[:, C_ID:C_ID + P] = np.eye(P)
    c[:, C_ONE:C_ONE + P] = 1.0
    c[:, C_NU:C_NU + P] = np.where(i[:, None] >= i[None, :], -1.0, 0.0)
    c[:, C_NONE:C_NONE + P] = -1.0
    t = np.arange(16)
    ic = np.stack([1.0 / np.minimum(t + 1, w) for w in (2, 2, 4, 4, 8, 8, 16, 16)])
    c[:, C_IC:C_IC + 128] = ic.reshape(1, 128)
    c[:, C_T:C_T + T] = np.arange(T)
    c[:, C_M2] = (i // 16) % 2 == 0
    c[:, C_M2 + 1] = (i // 16) % 2 == 1
    c[:, C_K] = 1.0
    c[:, C_K + 1] = np.pi / 2
    c[:, C_K + 2] = 0.0
    c[:, C_K + 3] = 0.0
    return c


class Queue:

    def __init__(self, sem):
        self.sem, self.n, self.items, self.seen = sem, 0, [], {}

    def wait(self, *marks):
        for s, v in marks:
            if self.seen.get(s.name, 0) < v:
                self.seen[s.name] = v
                self.items.append((None, s, v, None))
        return self

    def do(self, fn, *args, **kw):
        self.n += 1
        self.items.append((fn, args, kw, (self.sem, 1)))
        return (self.sem, self.n)

    def quiet(self, fn, *args, **kw):
        self.items.append((fn, args, kw, None))

    def dma(self, fn, out, src, sem):
        self.items.append((fn, (out, src), {}, (sem, 16)))

    def emit(self, eng):
        for fn, a, b, inc in self.items:
            if fn is None:
                eng.wait_ge(a, b)
            else:
                ins = fn(*a, **b)
                if inc is not None:
                    ins.then_inc(inc[0], inc[1])


def build(nc, I, out):
    ctx = ExitStack()
    with ctx:
        def sb(name, shape, dt=F32):
            return ctx.enter_context(nc.sbuf_tensor(name, shape, dt))

        def sem(name):
            return ctx.enter_context(nc.semaphore(name))

        ring = sb("ring", [P, RING, 1024])
        WH = sb("WH", [P, NH, 1024], F32R)
        WL = sb("WL", [P, NL, 1024], F32R)
        hh = sb("hh", [P, 8, T], F32R)
        hl = sb("hl", [P, 8, T], F32R)
        YH = sb("YH", [P, 3, 2, T], F32R)
        YL = sb("YL", [P, 3, 2, T], F32R)
        GRH = sb("GRH", [P, 8, 16], F32R)
        GRL = sb("GRL", [P, 8, 16], F32R)
        GRW = sb("GRW", [P, 8, 16])
        xT = sb("xT", [P, 8, T])
        SQT = sb("SQT", [P, 8, T])
        RS = sb("RS", [P, 64])
        cst = sb("cst", [P, C_ALL])
        VC = sb("VC", [P, 300])
        MOD = sb("MOD", [P, 24 + 24 + 72])
        PC = sb("PC", [P, 64])
        ACC = sb("ACC", [P, 1024])
        AR = sb("AR", [P, WORDS])
        pacc = ctx.enter_context(nc.psum_tensor("pacc", [P, 8, T], F32))
        pw = [ctx.enter_context(nc.psum_tensor(f"pw{i}", [P, 512], F32)) for i in range(4)]

        PE, V, S, G, SP = (Queue(sem(n)) for n in ("s_pe", "s_v", "s_s", "s_g", "s_sp"))
        s_ring = [sem(f"s_ring{i}") for i in range(RING)]
        s_small = {}

        mm, tr = nc.tensor.matmul, nc.tensor.transpose
        tt, ts, stt = nc.vector.tensor_tensor, nc.vector.tensor_scalar, nc.vector.scalar_tensor_tensor
        act = nc.scalar.activation

        def ar(off, n):
            return AR[:, off:off + n]

        def v3(ap, a):
            return ap.rearrange("p (a n) -> p a n", a=a)

        ident = cst[:, C_ID:C_ID + P]
        ones = cst[:, C_ONE:C_ONE + P]
        negU = cst[:, C_NU:C_NU + P]
        negones = cst[:, C_NONE:C_NONE + P]
        ic = v3(cst[:, C_IC:C_IC + P], 8)
        tvec = cst[:, C_T:C_T + T]
        one_c = cst[:, C_K:C_K + 1]
        hpi_c = cst[:, C_K + 1:C_K + 2]

        def small(q, fn, name, dst, src):
            s = sem("d_" + name)
            q.dma(fn, dst, src, s)
            s_small[name] = (s, 16)
            return (s, 16)

        small(S, nc.scalar.dma_start, "cst", cst[:, :], I["consts"])
        rows = {}
        packs = [[("c", I["c"], 8), ("norm_g", I["norm_g"], 16), ("ada_b", I["ada_b"], 48),
                  ("pool_scale", I["pool_scale"], 8), ("sgu_norm_g", I["sgu_norm_g"], 8),
                  ("final_g", I["final_g"], 8), ("gla_gate_b", I["gla_gate_b"], 4),
                  ("gla_norm_g", I["gla_norm_g"], 8), ("cond", I["cond_2"], 8)],
                 [("b_mod", I["b_mod_2"], 72), ("ffn1_norm", I["ffn1_norm_2"], 8), ("mix_norm", I["mix_norm_2"], 8),
                  ("conv_w", I["conv_w_2"], 12), ("ssm_d", I["ssm_d_2"], 4), ("glu_b", I["glu_b_2"], 4),
                  ("out_norm_conv", I["out_norm_conv_2"], 4), ("out_norm_ssm", I["out_norm_ssm_2"], 4),
                  ("ffn2_norm", I["ffn2_norm_2"], 8)],
                 [("final_norm", I["final_norm_2"], 8), ("lam_re", I["lambda_re_2"], 16),
                  ("lam_im", I["lambda_im_2"], 16)]]
        VR = AR[:, 0:3 * P].rearrange("p (a n) -> p a n", a=3)
        base = 0
        pack_n = []
        for a, pk in enumerate(packs):
            r = 0
            s = sem(f"d_vec{a}")
            for name, src, n in pk:
                flat = src
                while len(flat.shape) > 1:
                    names = " ".join("abcd"[:len(flat.shape)])
                    flat = flat.rearrange(f"{names} -> ({names})")
                q, fn = (SP, nc.sync.dma_start) if a == 0 else (G, nc.gpsimd.dma_start)
                q.dma(fn, VR[r:r + n, a, :], flat.rearrange("(r n) -> r n", n=P), s)
                rows[name] = (base + r, n)
                r += n
            if a == 2:
                G.dma(nc.gpsimd.dma_start, AR[0:16, 384:386],
                      I["log_dt_2"].rearrange("o (j e) -> (o j) e", e=2), s)
                s_small["vec2"] = (s, 16 * (len(pk) + 1))
            else:
                s_small[f"vec{a}"] = (s, 16 * len(pk))
            base += r
            pack_n.append(r)

        def col(name, i=0, n=1):
            b, m = rows[name]
            return VC[:, b + i:b + i + n]

        XN = AR[:, 512:512 + 2048].rearrange("p (a n) -> p a n", a=2)
        small(S, nc.scalar.dma_start, "x", XN, I["x"].rearrange("o (a p) n -> p (o a) n", p=P))
        E_SWR, E_BB = 17792, 18816
        GLW = AR[0:16, 19840:20352]
        small(G, nc.gpsimd.dma_start, "sgu_w", v3(ar(E_SWR, 1024), 8),
              I["sgu_w"].rearrange("o h t s -> t (o h) s"))
        small(G, nc.gpsimd.dma_start, "glr", GRW[:, :, :],
              I["odd_in_w"][0, :, 2048:2064].rearrange("(k p) n -> p k n", p=P))
        small(G, nc.gpsimd.dma_start, "glw", GLW, I["gla_gate_w"][0])
        small(G, nc.gpsimd.dma_start, "sgu_b", AR[0:1, E_BB:E_BB + 1024], I["sgu_b"].rearrange("o h t -> o (h t)"))

        units = []

        def add_cols(name, W, c0, n=256, k=8):
            units.append((name, W[0:k * P, c0:c0 + n].rearrange("(k p) n -> p k n", p=P), k, n))

        def add_rows(name, W, r0):
            units.append((name, W[r0:r0 + 256, :].rearrange("(k p) n -> p k n", p=P), 2, 1024))

        def add_ada(W, n0, n1):
            return [("ada", W[256 * r:256 * r + 256, 1024 * cc:1024 * cc + 1024].rearrange("(k p) n -> p k n", p=P),
                     2, 1024) for cc in range(n0, n1) for r in range(4)]

        def weave(side, from_):
            main = units[from_:]
            del units[from_:]
            k = 0
            for i, u in enumerate(main):
                while k < len(side) and (2 * k + 1) * len(main) <= 2 * i * len(side):
                    units.append(side[k])
                    k += 1
                units.append(u)
            units.extend(side[k:])

        def add_ffn(tag, Wg, Wu, Wd):
            for b in range(12):
                if b < 11:
                    add_cols(f"{tag}g", Wg, 256 * b)
                    add_cols(f"{tag}u", Wu, 256 * b)
                if b > 0:
                    add_rows(f"{tag}d", Wd, 256 * (b - 1))

        ew, ow, wi = I["even_in_w"][0], I["odd_in_w"][0], I["w_in_2"][0]
        a0, a1, a2 = I["ada_w"][0], I["ada_w"][1], I["w_mod_2"][0]
        EORD = (4, 5, 6, 7, 0, 1, 2, 3)
        units += add_ada(a0, 0, 2)
        at = len(units)
        for c0 in [2048 + 256 * j for j in range(4)] + [256 * j for j in range(4)]:
            add_cols("ein", ew, c0)
        for c0 in [1024 + 256 * j for j in range(4)]:
            add_cols("ein", ew, c0)
        for j in EORD:
            if j == 0:
                units.append(("pool", I["pool_w"][0].rearrange("g (k p) n -> p (g k) n", p=P), 8, 256))
            add_cols("ein", ew, 3072 + 256 * j)
        for j in EORD:
            add_rows("eout", I["even_out_w"][0], 256 * j)
        weave(add_ada(a0, 2, 3) + add_ada(a1, 0, 2), at)
        at = len(units)
        for c0 in ([256 * j for j in range(8)] + [5136 + 256 * j for j in range(8)] +
                   [4112 + 256 * j for j in range(4)] + [c + 256 * j for j in range(4) for c in (2064, 3088)]):
            add_cols("oin", ow, c0)
        for j in range(8):
            add_rows("oout", I["odd_out_w"][0], 256 * j)
        weave(add_ada(a1, 2, 3) + add_ada(a2, 0, 4), at)
        at = len(units)
        add_ffn("f1", I["ffn1_w_gate_2"][0], I["ffn1_w_up_2"][0], I["ffn1_w_down_2"][0])
        weave(add_ada(a2, 4, 8), at)
        at = len(units)
        for c0 in (1536, 1792, 512, 1024, 0, 768, 1280, 256):
            add_cols("win", wi, c0)
        for j in range(4):
            add_rows("wout", I["w_out_2"][0], 256 * j)
            if j == 0:
                add_cols("glu", I["glu_w_2"][0], 0, 512, 4)
        at = len(units)
        add_ffn("f2", I["ffn2_w_gate_2"][0], I["ffn2_w_up_2"][0], I["ffn2_w_down_2"][0])
        weave(add_ada(a2, 8, 9), at)

        pieces = [(i, h) for i, u in enumerate(units) if u[0] != "ada" for h in range(2)]
        piece_of = {p: k for k, p in enumerate(pieces)}
        piece_tok, piece_done = {}, {}
        unit_free = {}
        cur, ncut, nlow = [0], [0], [0]
        bg_rate = [3]

        def landed(i, half):
            s = 2 * i + half
            return (s_ring[s % RING], 16 * (s // RING + 1))

        def slot(i, half):
            return ring[:, (2 * i + half) % RING, :]

        def cut_to(q):
            while ncut[0] < len(pieces) and ncut[0] <= q + AHEAD_H:
                n = ncut[0]
                ncut[0] += 1
                u, half = pieces[n]
                if n >= NH:
                    S.wait(piece_done[n - NH])
                S.wait(landed(u, half))
                piece_tok[n] = [S.do(act, WH[:, n % NH, :], slot(u, half), ACT.Copy)]
            while nlow[0] < len(pieces) and nlow[0] <= q + AHEAD_L:
                n = nlow[0]
                nlow[0] += 1
                u, half = pieces[n]
                if n >= NL:
                    V.wait(piece_done[n - NL])
                V.wait(landed(u, half), *piece_tok[n])
                b = V.do(tt, WL[:, n % NL, :], slot(u, half), WH[:, n % NH, :].bitcast(F32), SUB)
                piece_tok[n].append(b)
                unit_free[2 * u + half] = b

        ada_out = []
        M0, M1, M2 = MOD[:, 0:24], MOD[:, 24:48], MOD[:, 48:120]
        ada_state = {"n": 0, "red": [], "tok": None}

        def ada_unit(i):
            n = ada_state["n"]
            ada_state["n"] += 1
            chunk, r = n // 4, n % 4
            sc = SIL[:, 0:8] if chunk < 6 else SIL[:, 8:16]

            def half(k):
                c = sc[:, 2 * r + k:2 * r + k + 1]
                V.wait(landed(i, k))
                if r == 0 and k == 0:
                    ada_reduce()
                    ada_add()
                    V.wait(sil_tok, *ada_state["red"])
                    t = V.do(ts, ACC[:, :], slot(i, 0), c, None, MUL)
                else:
                    V.wait(ada_state["tok"])
                    t = V.do(stt, out=ACC[:, :], in0=slot(i, k), scalar=c, in1=ACC[:, :], op0=MUL, op1=ADD)
                ada_state["tok"] = t
                unit_free[2 * i + k] = t
                if k == 1 and r == 3:
                    ada_state["pend"] = (chunk, t)
            ada_todo.extend([lambda: half(0), lambda: half(1)])

        ada_todo = []

        def ada_work(n=99):
            while n > 0 and ada_todo:
                ada_todo.pop(0)()
                n -= 1

        def ada_reduce():
            if ada_state.get("pend"):
                chunk, t = ada_state.pop("pend")
                b, pb = bank()
                PE.wait(t)
                for m in range(8):
                    tk = mmf(pb[:, m:m + 1], ACC[:, m * P:m * P + P], ones[:, 0:1])
                ada_state["red"] = [tk]
                ada_state["add"] = (chunk, b, pb, tk)

        def ada_add():
            if ada_state.get("add"):
                chunk, b, pb, tk = ada_state.pop("add")
                V.wait(tk)
                bias = col("ada_b", 8 * chunk, 8) if chunk < 6 else col("b_mod", 8 * (chunk - 6), 8)
                z = V.do(tt, MOD[:, 8 * chunk:8 * chunk + 8], pb[:, 0:8], bias, ADD)
                free(b, z)
                ada_out.append(z)

        def ada_step():
            ada_add()
            ada_reduce()

        def ada_flush():
            ada_work()
            ada_reduce()
            ada_add()

        def ada_drain(n=99):
            while n > 0 and cur[0] < len(units) and units[cur[0]][0] == "ada":
                ada_unit(cur[0])
                cur[0] += 1
                n -= 1
                ada_work()

        class Unit:

            def __init__(self, name):
                ada_step()
                ada_drain()
                self.i = cur[0]
                cur[0] += 1
                nm, _, self.k, self.n = units[self.i]
                assert nm == name, (nm, name, self.i)

            def piece(self, half):
                q = piece_of[(self.i, half)]
                cut_to(q)
                bg_step(bg_rate[0])
                PE.wait(*piece_tok[q])
                a = self.k // 2
                return v3(WH[:, q % NH, :], a), v3(WL[:, q % NL, :], a)

            def done(self, half, tok):
                piece_done[piece_of[(self.i, half)]] = tok

        bg = []
        bg_due = [0]

        def bg_step(n):
            bg_due[0] += n
            while bg_due[0] >= 1 and bg:
                try:
                    next(bg[0])
                    bg_due[0] -= 1
                except StopIteration:
                    bg.pop(0)
            if not bg:
                bg_due[0] = 0

        def bg_flush():
            while bg:
                bg_step(1)

        def mm3(o, a, b, start, stop):
            PE.quiet(mm, o, a[0], b[0], start=start, stop=False, skip_group_check=True)
            PE.quiet(mm, o, a[0], b[1], start=False, stop=False, skip_group_check=True)
            return PE.do(mm, o, a[1], b[0], start=False, stop=stop, skip_group_check=True)

        def mmf(o, a, b, start=True, stop=True):
            return PE.do(mm, o, a, b, start=start, stop=stop, skip_group_check=True)

        wfree = [[] for _ in range(4)]
        border = [0, 1, 2, 3]

        def bank():
            i = [x for x in border if wfree[x] is not None][0]
            border.remove(i)
            PE.wait(*wfree[i])
            wfree[i] = None
            return i, pw[i]

        def free(i, *toks):
            wfree[i] = list(toks)
            border.append(i)

        def warm(n):
            b, pb = bank()
            for _ in range(n):
                tk = mmf(pb[:, 0:P], ident, ones)
            free(b, tk)

        def pair(src, dh, dl, toks, free_toks=()):
            S.wait(*toks, *free_toks)
            a = S.do(act, dh, src, ACT.Copy)
            V.wait(*toks, a, *free_toks)
            return V.do(tt, dl, src, dh.bitcast(F32), SUB)

        yfree = [[], [], []]
        ny = [0]

        def ypair(src, toks):
            i = ny[0] % 3
            ny[0] += 1
            f = lambda x: x.rearrange("p a n -> p (a n)")
            t = pair(src, f(YH[:, i]), f(YL[:, i]), toks, yfree[i])
            yfree[i] = None
            return i, t

        def rsqrt(dst, src, scale, toks, tmp):
            h, t = tmp
            V.wait(*toks)
            a = V.do(ts, t, src, scale, EPS, MUL, ADD)
            V.wait(a)
            c = V.do(ts, h, t, 0.5, None, MUL)
            b = V.do(ts, dst.bitcast(U32), t.bitcast(U32), 1, None, ALU.logical_shift_right)
            V.wait(b)
            y = V.do(ts, dst.bitcast(I32), dst.bitcast(I32), -1.0, RSQRT_MAGIC, MUL, ADD)
            for i in range(3):
                V.wait(y, c)
                b = V.do(tt, t, dst, dst, MUL)
                V.wait(b)
                b = V.do(tt, t, t, h, MUL)
                V.wait(b)
                y = V.do(stt, out=dst, in0=t, scalar=1.5, in1=dst, op0=SUB, op1=MUL, **({"reverse0": True} if i == 2 else {}))
            return a, y

        sq_free = [[] for _ in range(8)]
        nsq = [0]

        def sumsq(pb, c, tiles, toks, scales=None):
            for k, (x, tk) in enumerate(zip(tiles, toks)):
                i = nsq[0] % 8
                nsq[0] += 1
                S.wait(*sq_free[i], *tk)
                kw = {} if scales is None else {"scale": scales[:, k:k + 1]}
                a = S.do(act, SQT[:, i, :], x, ACT.Square, **kw)
                PE.wait(a)
                for m in range(2):
                    r = mmf(pb[:, c + m:c + m + 1], SQT[:, i, m * P:m * P + P], ones[:, 0:1],
                            c == 0 and k == 0 and m == 0, k == len(tiles) - 1)
                sq_free[i] = [r]
            return r

        def spread(pb, c, r, tok):
            PE.wait(tok)
            return mmf(pb[:, c:c + P], r.to_broadcast([P, P]), ident)

        def norm_cols(tiles, toks, n):
            b, pb = bank()
            r = sumsq(pb, 0, tiles, toks)
            a, z = rsqrt(RS[:, 0:2], pb[:, 0:2], 1.0 / n, [r], (RS[:, 2:4], RS[:, 4:6]))
            free(b, a)
            return z

        def norm_r(tiles, toks, n):
            return spread_r(norm_cols(tiles, toks, n))

        def spread_r(z, c=0):
            b, pb = bank()
            for m in range(2):
                tk = spread(pb, m * P, RS[:, c + m:c + m + 1], z)
            return b, pb[:, 0:T], tk

        x_tok = [[] for _ in range(8)]
        h_free = []
        h_tok = [None] * 8

        def modulate(rb, gs, sh, toks):
            us = [None] * 8
            for k in range(9):
                if k < 8:
                    V.wait(*toks, *sq_free[k], *x_tok[k])
                    us[k] = V.do(stt, out=SQT[:, k, :], in0=xT[:, k, :], scalar=gs[:, k:k + 1], in1=rb,
                                 op0=MUL, op1=MUL)
                    S.wait(us[k], *h_free)
                    h_tok[k] = S.do(act, hh[:, k, :], SQT[:, k, :], ACT.Identity, bias=sh[:, k:k + 1])
                if k > 0:
                    q = k - 1
                    V.wait(h_tok[q], *h_free)
                    c = V.do(stt, out=hl[:, q, :], in0=SQT[:, q, :], scalar=sh[:, q:q + 1],
                             in1=hh[:, q, :].bitcast(F32), op0=ADD, op1=SUB)
                    h_tok[q] = c
                    sq_free[q] = [c]
            nsq[0] = 0
            del h_free[:]
            return us[7]

        def norm_mod(fin, gs, sh, toks):
            b, rb, tk = spread_r(fin.norm())
            warm(4)
            free(b, modulate(rb, gs, sh, [tk, *toks]))

        def hpair(k, sl=slice(0, T)):
            PE.wait(h_tok[k])
            return (hh[:, k, sl], hl[:, k, sl])

        acc_free = []
        acc_tok = [None] * 4
        acc_on = [False]

        def acc_rows(u, place, first, last, mid=None, tail=None):
            if tail is not None:
                ada_flush()
            i, t = place
            if first:
                PE.wait(*acc_free)
            PE.wait(t)
            for k in range(2):
                H, L = u.piece(k)
                for n in range(8):
                    sl = slice(n * P, n * P + P)
                    tk = mm3(pacc[:, n, :], (H[:, 0, sl], L[:, 0, sl]), (YH[:, i, k, :], YL[:, i, k, :]),
                             first and k == 0 and n % 2 == 0, last and k == 1)
                    acc_tok[n // 2] = tk
                    if tail is not None and k == 1 and n % 2 == 1:
                        tail(n // 2)
                u.done(k, tk)
                if mid is not None and k == 0:
                    for _ in mid:
                        pass
            yfree[i] = [tk]
            return tk

        class Finish:

            def __init__(self, gate, weights=None):
                self.gate, self.w = gate, weights
                self.sq = {}

            def stats(self, q):
                for k in (2 * q, 2 * q + 1):
                    i, a = self.sq[k]
                    PE.wait(a)
                    for m in range(2):
                        sq, first = SQT[:, i, m * P:m * P + P], k == 0 and m == 0
                        if self.w is None:
                            r = mmf(self.pb[:, m:m + 1], sq, ones[:, 0:1], first, k == 7)
                        else:
                            r = mmf(self.pb[:, 2 * m:2 * m + 2], sq, self.w[:, k, :], first, k == 7)
                    sq_free[i] = [r]
                self.tok = r

            def __call__(self, q):
                if q == 0:
                    self.g, self.gt = self.gate()
                    self.b, self.pb = bank()
                    del acc_free[:]
                for n in (2 * q, 2 * q + 1):
                    V.wait(acc_tok[q], *self.gt, *x_tok[n])
                    a = V.do(stt, out=xT[:, n, :], in0=pacc[:, n, :], scalar=self.g[:, n:n + 1], in1=xT[:, n, :],
                             op0=MUL, op1=ADD)
                    x_tok[n] = [a]
                    i = nsq[0] % 8
                    nsq[0] += 1
                    S.wait(*sq_free[i], a)
                    self.sq[n] = (i, S.do(act, SQT[:, i, :], xT[:, n, :], ACT.Square))
                if q >= 2:
                    self.stats(q - 2)
                if q == 3:
                    self.stats(2)
                    self.stats(3)
                    acc_free.append(a)

            def norm(self):
                a, z = rsqrt(RS[:, 0:2], self.pb[:, 0:2], 1.0 / D, [self.tok], (RS[:, 2:4], RS[:, 4:6]))
                free(self.b, a)
                warm(5)
                return z

        def cols_T(u, banks_of, evac):
            b, pb = bank()
            for half in range(2):
                H, L = u.piece(half)
                for m in range(2):
                    for kk in range(4):
                        sl = slice(m * P, m * P + P)
                        tk = mm3(pb[:, m * T:m * T + T], (H[:, kk, sl], L[:, kk, sl]), hpair(4 * half + kk),
                                 half == 0 and kk == 0 and m == 0, half == 1 and kk == 3)
                u.done(half, tk)
            free(b, *evac(pb, tk))
            return tk

        def cols_N(u, dst, dtoks):
            b, pb = bank()
            for half in range(2):
                H, L = u.piece(half)
                for m in range(2):
                    for kk in range(4):
                        tk = mm3(pb[:, m * T:m * T + T], hpair(4 * half + kk, slice(m * P, m * P + P)),
                                 (H[:, kk, :], L[:, kk, :]), half == 0 and kk == 0 and m == 0,
                                 half == 1 and kk == 3)
                u.done(half, tk)
            S.wait(tk, *dtoks)
            r = S.do(act, dst, v3(pb[:, :], 2), ACT.Copy)
            free(b, r)
            return r

        def silu_t(pb, tk, dst, toks, n=512):
            S.wait(tk, *toks)
            return S.do(act, dst, pb[:, 0:n], ACT.Silu)

        S.quiet(nc.scalar.preload_act_table_set, "exp_and_others")
        n0 = pack_n[0]
        PE.wait(s_small["cst"], s_small["vec0"])
        b, pb = bank()
        tk = PE.do(tr, pb[:, 0:n0], VR[0:n0, 0, :], ident[0:n0, 0:n0])
        V.wait(tk)
        vc_tok = V.do(nc.vector.tensor_copy, VC[:, 0:n0], pb[:, 0:n0])
        free(b, vc_tok)
        SIL = PC[:, 16:32]
        sil_e = PC[:, 32:48]
        S.wait(vc_tok)
        a = S.do(act, sil_e[:, 0:8], col("c", 0, 8), ACT.Exp, scale=-1.0)
        a = S.do(act, sil_e[:, 8:16], col("cond", 0, 8), ACT.Exp, scale=-1.0)
        V.wait(a)
        a = V.do(ts, sil_e, sil_e, 1.0, None, ADD)
        V.wait(a)
        a = V.do(nc.vector.reciprocal, sil_e, sil_e)
        V.wait(a)
        a = V.do(tt, SIL[:, 0:8], sil_e[:, 0:8], col("c", 0, 8), MUL)
        sil_tok = V.do(tt, SIL[:, 8:16], sil_e[:, 8:16], col("cond", 0, 8), MUL)

        PE.wait(s_small["x"])
        for q in range(4):
            b, pb = bank()
            for kk in range(2):
                k = 2 * q + kk
                for m in range(2):
                    tk = PE.do(tr, pb[:, kk * T + m * P:kk * T + m * P + P], XN[:, m, k * P:k * P + P], ident)
            S.wait(tk)
            r = S.do(act, xT[:, 2 * q:2 * q + 2, :], v3(pb[:, :], 2), ACT.Copy)
            free(b, r)
            x_tok[2 * q] = [r]
            x_tok[2 * q + 1] = [r]
        b0, pb0 = bank()
        r0 = sumsq(pb0, 0, [xT[:, k, :] for k in range(8)], x_tok)
        ada_drain(4)

        ada_drain(1)
        a, z = rsqrt(RS[:, 0:2], pb0[:, 0:2], 1.0 / D, [r0], (RS[:, 2:4], RS[:, 4:6]))
        free(b0, a)
        x_norm = spread_r(z)
        ada_drain(2)
        PE.wait(s_small["vec1"], s_small["vec2"])
        b, pb = bank()
        base = 0
        for a, n in enumerate(pack_n[1:]):
            tk = PE.do(tr, pb[:, base:base + n], VR[0:n, a + 1, :], ident[0:n, 0:n])
            base += n
        V.wait(tk)
        vc2_tok = V.do(nc.vector.tensor_copy, VC[:, n0:n0 + base], pb[:, 0:base])
        free(b, vc2_tok)
        DTC = PC[:, 0:16]
        V.wait(s_small["vec2"])
        a = V.do(nc.vector.tensor_copy, AR[0:16, 2560:2688].rearrange("p (e n) -> p e n", e=2),
                 AR[0:16, 384:386].unsqueeze(2).to_broadcast([16, 2, 64]))
        b, pb = bank()
        PE.wait(a)
        tk = PE.do(tr, pb[:, 0:16], AR[0:16, 2560:2688], ident[0:16, 0:16])
        S.wait(tk)
        dt_tok = S.do(act, DTC, pb[:, 0:16], ACT.Exp)
        free(b, dt_tok)
        RR = sb("RR", [P, 16])
        start_done = tk

        PE.wait(s_small["sgu_w"], s_small["sgu_b"])
        E_SWT = 16768
        swT = v3(ar(E_SWT, 1024), 8)
        swR = v3(ar(E_SWR, 1024), 8)
        ptok = []
        for q in range(2):
            b, pb = bank()
            for m in range(4):
                tk = PE.do(tr, pb[:, m * P:m * P + P], swR[:, 4 * q + m, :], ident)
            S.wait(tk)
            r = S.do(act, swT[:, 4 * q:4 * q + 4, :], v3(pb[:, :], 4), ACT.Copy)
            free(b, r)
            ptok.append(r)
        sw_tr = tk
        G.wait(*ptok)
        swt_tok = G.do(nc.gpsimd.affine_select, out=swT, in_=swT, compare_op=ALU.is_ge, fill=0.0, base=0,
                       pattern=[[0, 8], [1, P]], channel_multiplier=-1)
        ada_drain()
        ada_reduce()
        cut_to(1 - AHEAD_L)
        ada_flush()

        def mod_cols(m, gname, goff, dst, toks):
            V.wait(*toks)
            return V.do(stt, out=dst, in0=m[:, 8:16], scalar=1.0, in1=col(gname, goff, 8), op0=ADD, op1=MUL)

        GS = PC[:, 48:56]
        g_tok = mod_cols(M0, "norm_g", 0, GS, [ada_out[1]])
        free(x_norm[0], modulate(x_norm[1], GS, M0[:, 0:8], [x_norm[2], g_tok, ada_out[0]]))

        bB = ar(E_BB, 1024)
        pend = []
        for q in range(2):
            b, pb = bank()
            tk = mmf(pb[:, :], ones[0:1, :], AR[0:1, E_BB + 512 * q:E_BB + 512 * q + 512])
            pend.append((b, pb, tk))
        for q, (b, pb, tk) in enumerate(pend):
            S.wait(pend[-1][2])
            bb_tok = S.do(act, bB[:, 512 * q:512 * q + 512], pb[:, :], ACT.Copy)
            free(b, bb_tok)

        V.wait(dt_tok, vc2_tok)
        a = V.do(tt, RS[:, 32:48], col("lam_re", 0, 16), DTC, MUL)
        S.wait(a)
        rr_tok = S.do(act, RR[:, :], RS[:, 32:48], ACT.Exp)
        gr = lambda x: x[:, :, :].rearrange("p a n -> p (a n)")
        grp = pair(gr(GRW), gr(GRH), gr(GRL), [s_small["glr"]])

        GT = v3(ar(0, 4096), 16)
        VV = v3(ar(4096, 2048), 2)
        UU = v3(ar(6144, 2048), 8)
        AP_ = v3(ar(8192, 2176), 8)
        S1 = v3(ar(10368, 2176), 8)
        S2 = v3(ar(12544, 2176), 8)
        YP = v3(ar(14720, 2048), 8)
        TMP = [ar(17792, 512), ar(18304, 512)]
        S.quiet(nc.scalar.preload_act_table_set, "silu_and_others")

        pads = []
        G.wait(start_done)
        for buf in (AP_, S1, S2):
            pads.append(G.do(nc.gpsimd.memset, buf[:, :, 0:16], 0.0))

        for j in range(4):
            r = cols_N(Unit("ein"), VV[:, :, 256 * j:256 * j + 256], [start_done])
        vh_tok = []

        def v_norm(r=r):
            for m in range(2):
                S.wait(r)
                a = S.do(act, YP[:, 4 * m:4 * m + 4, :].rearrange("p a n -> p (a n)"), VV[:, m, :], ACT.Square,
                         accum_out=PC[:, 56 + m:57 + m])
                yield
            _, rs = rsqrt(PC[:, 58:60], PC[:, 56:58], 1.0 / D, [a], (PC[:, 60:62], PC[:, 62:64]))
            yield
            for m in range(2):
                V.wait(rs, r)
                vh_tok.append(V.do(ts, VV[:, m, :], VV[:, m, :], PC[:, 58 + m:59 + m], None, MUL))
                yield

        bg_rate[0] = 1
        bg.append(v_norm())
        a_tok = []
        for j in range(4):
            def ev(pb, tk, j=j):
                S.wait(tk, start_done)
                r = S.do(act, AP_[:, 2 * j:2 * j + 2, 16:272], v3(pb[:, :], 2), ACT.Copy)
                a_tok.append(r)
                return [r]
            cols_T(Unit("ein"), None, ev)

        p_tok = []
        w_tok = {}

        def windows():
            src = AP_
            V.wait(*a_tok, *pads)
            for g, w in enumerate((2, 4, 8, 16)):
                dst = (S1, S2)[g % 2]
                half = w // 2
                for c in range(2 * g, 8, 2):
                    r = slice(c, c + 2)
                    V.wait(*w_tok.get((g, c), []))
                    a = V.do(tt, dst[:, r, 16:272], src[:, r, 16:272], src[:, r, 16 - half:272 - half], ADD)
                    w_tok[(g + 1, c)] = [a]
                    w_tok[(g + 2, c)] = [a]
                    if c % 4 == 2:
                        yield
                V.wait(a)
                z = AP_[:, 2 * g:2 * g + 2, :]
                w_ = dst[:, 2 * g:2 * g + 2, :]
                y = YP[:, 2 * g:2 * g + 2, :]
                b1 = V.do(stt, out=y, in0=w_[:, :, 16:272], scalar=1.0 / w, in1=z[:, :, 16:272], op0=MUL, op1=SUB)
                V.wait(b1)
                b2 = V.do(tt, y[:, :, 0:16], w_[:, :, 16:32], ic[:, 2 * g:2 * g + 2, :], MUL)
                V.wait(b2)
                p_tok.append(V.do(tt, y[:, :, 0:16], y[:, :, 0:16], z[:, :, 16:32], SUB))
                yield
                src = dst

        bg_rate[0] = 1
        bg.append(windows())
        u_tok = []
        for j in range(4):
            def ev(pb, tk, j=j):
                S.wait(tk, start_done)
                r = S.do(act, UU[:, 2 * j:2 * j + 2, :], v3(pb[:, :], 2), ACT.Copy)
                u_tok.append(r)
                return [r]
            cols_T(Unit("ein"), None, ev)

        f2 = lambda x: x.rearrange("p a n -> p (a n)")
        PE.wait(*vh_tok, swt_tok)
        z_tok = []
        for q in range(4):
            b, pb = bank()
            for m in range(2):
                h = 2 * q + m
                for n in range(2):
                    tk = mmf(pb[:, m * T + n * P:m * T + n * P + P], VV[:, n, h * P:h * P + P], swT[:, h, :])
            for m in range(2):
                h = 2 * q + m
                V.wait(tk, bb_tok, *u_tok, sw_tr)
                a = V.do(stt, out=v3(TMP[m][:, 0:T], 2), in0=v3(pb[:, m * T:m * T + T], 2),
                         scalar=col("sgu_norm_g", h),
                         in1=bB[:, h * P:h * P + P].unsqueeze(1).to_broadcast([P, 2, P]), op0=MUL, op1=ADD)
                V.wait(a)
                r = V.do(tt, UU[:, h, :], TMP[m][:, 0:T], UU[:, h, :], MUL)
            z_tok.append(r)
            free(b, a)

        yf = {}
        yp_tok = []

        def pool_unit():
            pu = Unit("pool")
            for g in range(4):
                if g < 2:
                    pl.append(ypair(f2(YP[:, 2 * g + 4:2 * g + 6, :]), [p_tok[g + 2]]))
                i, t = pl[g]
                if g % 2 == 0:
                    H, L = pu.piece(g // 2)
                PE.wait(t)
                b, pb = bank()
                for m in range(2):
                    for k in range(2):
                        kk = 2 * (g % 2) + k
                        tk = mm3(pb[:, m * T:m * T + T], (H[:, kk, m * P:m * P + P], L[:, kk, m * P:m * P + P]),
                                 (YH[:, i, k, :], YL[:, i, k, :]), m == 0 and k == 0, k == 1)
                yfree[i] = [tk]
                if g % 2 == 1:
                    pu.done(g // 2, tk)
                for m in range(2):
                    n = 2 * g + m
                    S.wait(tk, t)
                    r = S.do(act, YP[:, n, :], pb[:, m * T:m * T + T], ACT.Copy, scale=col("pool_scale", n))
                yp_tok.append(r)
                free(b, r)


        for j in EORD:
            if j == 7:
                bg_flush()
                pl = [ypair(f2(YP[:, 2 * g:2 * g + 2, :]), [p_tok[g]]) for g in range(2)]
            if j == 0:
                pool_unit()
            if j == 3:
                epl = [ypair(f2(GT[:, 2 * e:2 * e + 2, :]), [yf[e]]) for e in (4, 5)]

            def ev(pb, tk, j=j):
                g2 = f2(GT[:, 2 * j:2 * j + 2, :])
                r = silu_t(pb, tk, g2, [z_tok[-1]])
                V.wait(r, *yp_tok)
                other = YP[:, 2 * j:2 * j + 2, :] if j < 4 else UU[:, 2 * j - 8:2 * j - 6, :]
                yf[j] = V.do(tt, g2, g2, f2(other), MUL)
                return [r]
            last_h = cols_T(Unit("ein"), None, ev)
        h_free.append(last_h)

        def out_proj(name, pl, tiles, toks, n, tail):
            for j in range(n):
                if j + 2 < n:
                    pl.append(ypair(tiles[j + 2], toks[j + 2]))
                tk = acc_rows(Unit(name), pl[j], j == 0, j == n - 1, tail=tail if j == n - 1 else None)
            return tk

        fin = Finish(lambda: (M0[:, 16:24], [ada_out[2]]))
        tk = out_proj("eout", epl, [f2(GT[:, 2 * j:2 * j + 2, :]) for j in EORD], [[yf[j]] for j in EORD], 8, fin)
        ada_flush()
        even_done = tk

        V.wait(*h_tok)
        g_tok = mod_cols(M1, "norm_g", 8, GS, [ada_out[4]])
        norm_mod(fin, GS, M1[:, 0:8], [g_tok, ada_out[3]])
        S.quiet(nc.scalar.preload_act_table_set, "natural_log_exp_and_others")

        ao = even_done
        GV = v3(ar(4096, 2048), 2)
        SQ_ = v3(ar(6144, 2048), 8)
        SK_ = v3(ar(8192, 2048), 8)
        SV_ = v3(ar(10240, 2048), 2)
        GQ, GK = ar(12288, 1024), ar(13312, 1024)
        T0, T1, T2, T3, T4, T5 = (ar(14336 + 1024 * i, 1024) for i in range(6))

        b, pb = bank()
        PE.wait(grp)
        for k in range(8):
            tk = mm3(pb[0:16, 0:T], (GRH[:, k, :], GRL[:, k, :]), hpair(k), k == 0, k == 7)
        GLT = AR[0:16, 4096:4352]
        S.wait(tk, ao)
        a = S.do(act, GLT, pb[0:16, 0:T], ACT.Copy)
        free(b, a)
        qk_tok = []
        def qk_unit(j):
            def ev(pb, tk):
                dst = (GQ if j < 2 else GK)[:, (j % 2) * 512:(j % 2) * 512 + 512]
                S.wait(tk, ao)
                r = S.do(act, dst, pb[:, :], ACT.Copy, scale=float(P) ** -0.5 if j < 2 else 1.0)
                qk_tok.append(r)
                return [r]
            cols_T(Unit("oin"), None, ev)

        qk_unit(0)
        PE.wait(a, s_small["glw"])
        la_tok = []
        lw = []
        for q in range(2):
            b, pb = bank()
            for m in range(2):
                h = 2 * q + m
                tk = mmf(pb[:, m * T:m * T + T], GLW[:, h * P:h * P + P], GLT)
            lw.append((b, pb, tk))
        glr_done = tk
        EBL = PC[:, 32:48]
        BC = T1.rearrange("p (c n) -> p c n", n=64)
        gk = {}

        def decay():
            G.wait(ao, glr_done)
            a = G.do(nc.gpsimd.memset, T5, 1.0)
            G.wait(a)
            m_tok = G.do(nc.gpsimd.memset, T5.rearrange("p (c n) -> p c n", n=64)[:, :, 0:1], 0.0)
            for q in range(2):
                b, pb, tk = lw[q]
                ea, d_prev = [], []
                for m in range(2):
                    h = 2 * q + m
                    src = pb[:, m * T:m * T + T]
                    S.wait(tk, ao, *d_prev)
                    ea.append(S.do(act, T4[:, h * T:h * T + T], src, ACT.Abs, bias=col("gla_gate_b", h)))
                    V.wait(ea[-1], ao)
                    d = V.do(ts, T0[:, h * T:h * T + T], src, col("gla_gate_b", h), 0.0, ADD, MIN)
                    d_prev = [d]
                free(b, d, ea[1])
                e, la = T4[:, 2 * q * T:2 * q * T + 2 * T], T0[:, 2 * q * T:2 * q * T + 2 * T]
                S.wait(ea[1])
                c = S.do(act, e, e, ACT.Exp, scale=-1.0)
                S.wait(c)
                c = S.do(act, e, e, ACT.Ln, bias=one_c)
                V.wait(d, c)
                la_tok.append(V.do(tt, la, la, e, SUB))
                yield
            V.wait(m_tok, *la_tok)
            gk["bc"] = bc_tok = V.do(nc.vector.tensor_tensor_scan, T1, T5, T0, 0.0, MUL, ADD)
            yield
            S.wait(bc_tok)
            gk["ebl"] = S.do(act, EBL.unsqueeze(2), BC[:, :, 63:64], ACT.Exp, scale=1.0 / 16)
            V.wait(bc_tok)
            gk["dd"] = V.do(tt, T3.rearrange("p (c n) -> p c n", n=64), BC[:, :, 63:64].to_broadcast([P, 16, 64]),
                            BC, SUB)
            gk["e2"] = S.do(act, T2, T1, ACT.Exp, scale=-1.0 / 16)
            yield
            gk["e1"] = S.do(act, T0, T1, ACT.Exp, scale=1.0 / 16)
            yield
            S.wait(gk["dd"])
            gk["e3"] = S.do(act, T3, T3, ACT.Exp, scale=1.0 / 16)
            yield
            V.wait(*qk_tok[0:4], gk["e2"])
            gk["ki"] = V.do(tt, T2, T2, GK, MUL)
            yield
            V.wait(gk["e1"])
            gk["qd"] = V.do(tt, GQ, GQ, T0, MUL)
            yield
            V.wait(gk["e3"])
            gk["ke"] = V.do(tt, T3, T3, GK, MUL)
            yield

        bg_rate[0] = 1
        bg.append(decay())
        for j in range(1, 4):
            qk_unit(j)
        for j in range(4):
            gv_tok = cols_N(Unit("oin"), GV[:, :, 256 * j:256 * j + 256], [ao, glr_done])
        bg_flush()
        bc_tok, ebl_tok, dd, e1, e2, e3, ki, qd, ke = (gk[k] for k in ("bc", "ebl", "dd", "e1", "e2", "e3", "ki",
                                                                        "qd", "ke"))

        g_toks = []

        def gate_unit():
            j = len(g_toks)
            if j == 8:
                return

            def ev(pb, tk):
                r = silu_t(pb, tk, f2(GT[:, 2 * j:2 * j + 2, :]), [ao])
                g_toks.append(r)
                return [r]
            cols_T(Unit("oin"), None, ev)

        S.quiet(nc.scalar.preload_act_table_set, "silu_and_others")
        PE.wait(ke, ki, qd)
        att_tok, kt_tok = [], []
        AT = T5.rearrange("p (b h t) -> p b h t", b=2, h=4)
        KT = T4.rearrange("p (b h t) -> p b h t", b=2, h=4)
        for blk in range(2):
            b, pb = bank()
            for h in range(4):
                sl = slice(h * T + blk * P, h * T + blk * P + P)
                tk = PE.do(tr, pb[:, h * P:h * P + P], T3[:, sl], ident)
            S.wait(tk, *la_tok)
            r = S.do(act, KT[:, blk], v3(pb[:, :], 4), ACT.Copy)
            free(b, r)
            kt_tok.append(r)
        t3_done = tk
        for blk in range(2):
            b, pb = bank()
            for h in range(4):
                sl = slice(h * T + blk * P, h * T + blk * P + P)
                tk = mmf(pb[:, h * P:h * P + P], T2[:, sl], GQ[:, sl])
            S.wait(tk, bc_tok)
            r = S.do(act, AT[:, blk], v3(pb[:, :], 4), ACT.Copy)
            free(b, r)
            G.wait(r)
            r = G.do(nc.gpsimd.affine_select, out=AT[:, blk], in_=AT[:, blk], compare_op=ALU.is_ge, fill=0.0,
                     base=0, pattern=[[0, 4], [1, P]], channel_multiplier=-1)
            G.wait(r)
            r = G.do(nc.gpsimd.memset, AT[0:64, blk, :, 64:128], 0.0)
            att_tok.append(r)
        att_pe = tk

        ST = [v3(GK, 4), v3(T0, 4), v3(T1, 4)]
        PE.wait(*kt_tok, gv_tok)
        st_tok = []
        prev = None
        for c in range(3):
            gate_unit()
            rr = slice(64 * (c % 2), 64 * (c % 2) + 64)
            cur_t = []
            for q in range(2):
                b, pb = bank()
                for m in range(2):
                    h = 2 * q + m
                    tk = mmf(pb[:, m * T:m * T + T], KT[rr, c // 2, h, :], GV[rr, c // 2, h * T:h * T + T])
                for m in range(2):
                    h = 2 * q + m
                    V.wait(tk, ke, qd, dd, ebl_tok, e3, e1, e2)
                    if c == 0:
                        r = V.do(nc.vector.tensor_copy, ST[0][:, h, :], pb[:, m * T:m * T + T])
                    else:
                        V.wait(*prev)
                        r = V.do(stt, out=ST[c][:, h, :], in0=ST[c - 1][:, h, :],
                                 scalar=EBL[:, 4 * h + c:4 * h + c + 1], in1=pb[:, m * T:m * T + T],
                                 op0=MUL, op1=ADD)
                    cur_t.append(r)
                free(b, r)
            prev = cur_t
            st_tok.append(cur_t)
        gate_unit()

        YC = v3(ar(16384, 2048), 8)
        PE.wait(*att_tok)
        yc_tok = []
        for h in range(4):
            b, pb = bank()
            for v in range(2):
                for blk in range(2):
                    tk = mmf(pb[:, v * T + blk * P:v * T + blk * P + P], GV[:, blk, h * T + v * P:h * T + v * P + P],
                             AT[:, blk, h, :], start=(v == 0 and blk == 0), stop=False)
            for v in range(2):
                for c in range(1, 4):
                    PE.wait(*st_tok[c - 1])
                    tk = mmf(pb[:, v * T + 64 * c:v * T + 64 * c + 64], ST[c - 1][:, h, v * P:v * P + P],
                             GQ[:, h * T + 64 * c:h * T + 64 * c + 64], start=False, stop=(c == 3))
            S.wait(tk, t3_done, att_pe)
            r = S.do(act, YC[:, 2 * h:2 * h + 2, :], v3(pb[:, :], 2), ACT.Copy)
            free(b, r)
            yc_tok.append(r)
        gla_pe = tk
        yf = []

        sqs = []
        for n in range(8):
            i = nsq[0] % 8
            nsq[0] += 1
            S.wait(*sq_free[i], yc_tok[n // 2])
            sqs.append((i, S.do(act, SQT[:, i, :], YC[:, n, :], ACT.Square)))
        gate_unit()
        b, pb = bank()
        for n, (i, t) in enumerate(sqs):
            PE.wait(t)
            for m in range(2):
                c = 2 * (n // 2) + m
                tk = mmf(pb[:, c:c + 1], SQT[:, i, m * P:m * P + P], ones[:, 0:1], n == 0 and m == 0, n % 2 == 1)
            sq_free[i] = [tk]
        a, z = rsqrt(RS[:, 0:8], pb[:, 0:8], 1.0 / 256, [tk], (RS[:, 8:16], RS[:, 16:24]))
        free(b, a)
        gate_unit()
        for q in range(2):
            b, pb = bank()
            for c in range(4):
                tk = spread(pb, c * P, RS[:, 4 * q + c:4 * q + c + 1], z)
            for m in range(2):
                h = 2 * q + m
                for v in range(2):
                    n = 2 * h + v
                    V.wait(tk)
                    a = V.do(stt, out=YC[:, n, :], in0=YC[:, n, :], scalar=col("gla_norm_g", n),
                             in1=pb[:, m * T:m * T + T], op0=MUL, op1=MUL)
                    V.wait(a, g_toks[n // 2])
                    r = V.do(tt, GT[:, n, :], GT[:, n, :], YC[:, n, :], MUL)
                yf.append(r)
            free(b, a)
            gate_unit()
        while len(g_toks) < 8:
            gate_unit()
        S.quiet(nc.scalar.preload_act_table_set, "natural_log_exp_and_others")
        for j in range(4):
            sv_tok = cols_N(Unit("oin"), SV_[:, :, 256 * j:256 * j + 256], [ao])

        sqk_tok = []

        def sqk_units(q):
            for dst, sc in ((SQ_, float(P) ** -0.5), (SK_, 1.0)):
                def ev(pb, tk):
                    S.wait(tk, ao)
                    r = S.do(act, dst[:, 2 * q:2 * q + 2, :], v3(pb[:, :], 2), ACT.Copy, scale=sc)
                    sqk_tok.append(r)
                    return [r]
                h_last[:] = [cols_T(Unit("oin"), None, ev)]
                yield

        h_last = [None]
        sb_free = [[gla_pe], [gla_pe]]

        def sb_scores(h):
            b, pb = bank()
            PE.wait(*sqk_tok)
            mmf(pb[:, 0:256], SK_[:, h, 0:128], SQ_[:, h, :], True, True)
            tk = mmf(pb[:, 256:384], SK_[:, h, 128:256], SQ_[:, h, 128:256], False, True)
            o = 18432 + 768 * (h % 2)
            e, sp = ar(o, 384), ar(o + 384, 384)
            S.wait(tk, *sb_free[h % 2])
            a = S.do(act, e, pb[:, 0:384], ACT.Abs)
            S.wait(a)
            c = S.do(act, e, e, ACT.Exp, scale=-1.0)
            S.wait(c)
            c = S.do(act, e, e, ACT.Ln, bias=one_c)
            V.wait(c, *sb_free[h % 2])
            d = V.do(stt, out=sp, in0=pb[:, 0:384], scalar=0.0, in1=e, op0=MAX, op1=ADD)
            G.wait(d)
            for o2 in (0, 256):
                m = G.do(nc.gpsimd.affine_select, out=sp[:, o2:o2 + P], in_=sp[:, o2:o2 + P], compare_op=ALU.is_gt,
                         fill=0.0, base=0, pattern=[[1, P]], channel_multiplier=-1)
            return b, pb, sp, e, m, d, a

        def sb_weights(st):
            b, pb, sp, w, m, d, a = st
            PE.wait(m, d, a)
            mmf(pb[:, 0:256], negU, sp[:, 0:256], False, False)
            mmf(pb[:, 128:256], negones, sp[:, 256:384], False, False)
            tk = mmf(pb[:, 256:384], negU, sp[:, 256:384], False, True)
            S.wait(tk, d)
            r = S.do(act, w, pb[:, 0:384], ACT.Exp)
            free(b, r)
            G.wait(r)
            for o2 in (0, 256):
                m = G.do(nc.gpsimd.affine_select, out=w[:, o2:o2 + P], in_=w[:, o2:o2 + P], compare_op=ALU.is_gt,
                         fill=0.0, base=0, pattern=[[1, P]], channel_multiplier=-1)
            return w, m, r

        def sb_out(h, w, m, r, pb, half):
            PE.wait(m, r)
            o = pb[:, half * T:half * T + T]
            mmf(o, SV_[:, 0, h * P:h * P + P], w[:, 0:256], half == 0, False)
            tk = mmf(o[:, 128:256], SV_[:, 1, h * P:h * P + P], w[:, 256:384], False, True)
            sb_free[h % 2] = [tk]
            return tk

        places = []
        out_n = [0]

        def place_to(n):
            while len(places) < min(n, len(yf)):
                q = len(places)
                places.append(ypair(f2(GT[:, 2 * q:2 * q + 2, :]), [yf[q]]))

        def out_unit():
            j = out_n[0]
            out_n[0] += 1
            place_to(j + 2)
            return acc_rows(Unit("oout"), places[j], j == 0, j == 7, tail=fin if j == 7 else None)

        for _ in sqk_units(0):
            pass
        PE.wait(sv_tok)
        for q in range(4):
            if q == 3:
                place_to(3)
            s0 = sb_scores(2 * q)
            s1 = sb_scores(2 * q + 1)
            fill = sqk_units(q + 1) if q < 3 else None
            if q < 3:
                next(fill)
            else:
                h_free.append(h_last[0])
                out_unit()
            w0 = sb_weights(s0)
            w1 = sb_weights(s1)
            if q < 3:
                next(fill)
            else:
                out_unit()
            b, pb = bank()
            sb_out(2 * q, *w0, pb, 0)
            tk = sb_out(2 * q + 1, *w1, pb, 1)
            j = 4 + q
            g2 = f2(GT[:, 2 * j:2 * j + 2, :])
            V.wait(tk, g_toks[j])
            a = V.do(tt, g2, g2, pb[:, :], MUL)
            free(b, a)
            yf.append(a)
        fg = col("final_g", 0, 8)
        FG = RS[:, 16:32]
        FG2 = FG.rearrange("p (k e) -> p k e", e=2)
        V.wait(vc_tok)
        V.do(ts, FG2[:, :, 0:1], fg.unsqueeze(2), 0.0, 1.0, MUL, ADD)
        f_tok = V.do(tt, FG2[:, :, 1:2], fg.unsqueeze(2), fg.unsqueeze(2), MUL)
        PE.wait(f_tok)
        fin = Finish(lambda: (M1[:, 16:24], [ada_out[5]]), FG2)
        while out_n[0] < 8:
            tk = out_unit()
        ada_flush()
        S.quiet(nc.scalar.preload_act_table_set, "silu_and_others")
        odd_done = tk

        b, pb, r = fin.b, fin.pb, fin.tok
        pm = pb[:, 0:4].rearrange("p (m e) -> p m e", e=2)
        a, z = rsqrt(RS[:, 0:2].unsqueeze(2), pm[:, :, 0:1], 1.0 / D, [r],
                     (RS[:, 2:4].unsqueeze(2), RS[:, 4:6].unsqueeze(2)))
        V.wait(z)
        a = V.do(tt, RS[:, 6:8], RS[:, 0:2], RS[:, 0:2], MUL)
        V.wait(a)
        a = V.do(tt, RS[:, 6:8].unsqueeze(2), RS[:, 6:8].unsqueeze(2), pm[:, :, 1:2], MUL)
        free(b, a)
        _, z2 = rsqrt(RS[:, 8:10], RS[:, 6:8], 1.0 / D, [a], (RS[:, 2:4], RS[:, 4:6]))
        V.wait(z2)
        z2 = V.do(tt, RS[:, 8:10], RS[:, 8:10], RS[:, 0:2], MUL)
        warm(12)
        x_norm = spread_r(z2, 8)
        x_new = spread_r(z)

        def update_x():
            b, rb, tk = x_new
            for k in range(8):
                V.wait(tk, *x_tok[k], *h_tok)
                a = V.do(stt, out=xT[:, k, :], in0=xT[:, k, :], scalar=fg[:, k:k + 1], in1=rb, op0=MUL, op1=MUL)
                x_tok[k] = [a]
                if k == 7:
                    free(b, a)
                if k % 2 == 1:
                    yield

        ao = odd_done
        COS = v3(ar(2048, 4096), 16)
        SIN = v3(ar(6144, 4096), 16)
        BT = [v3(ar(10240 + 512 * i, 512), 4) for i in range(2)]
        CT = [v3(ar(11264 + 512 * i, 512), 4) for i in range(3)]
        BR = [v3(ar(12800 + 256 * i, 256), 16) for i in range(2)]
        BB = [v3(ar(13312 + 512 * i, 512), 16) for i in range(2)]
        CR = [v3(ar(14336 + 256 * i, 256), 4) for i in range(2)]
        CM = [ar(14848 + 512 * i, 512) for i in range(2)]
        LC = v3(ar(20288, 16 * 12), 12)
        S5T = [ar(15872 + 256 * i, 256) for i in range(3)]
        G.wait(ao)
        for i, nm in enumerate(("ssm_b_re_2", "ssm_b_im_2")):
            small(G, nc.gpsimd.dma_start, nm, BR[i], I[nm][0].rearrange("(j e) p c -> (e p) j c", e=2))
        for i, nm in enumerate(("ssm_c_re_2", "ssm_c_im_2")):
            small(G, nc.gpsimd.dma_start, nm, CR[i], I[nm][0].rearrange("(m g) c p -> (g c) m p", g=8))

        def s5_coefs():
            lre, lim = col("lam_re", 0, 16), col("lam_im", 0, 16)
            A_, TH, _, SN, CN, T1_, T2_, T3_, CFR, CFI, X1, X2 = (LC[:, i, :] for i in range(12))
            V.wait(dt_tok, vc_tok, vc2_tok, ao)
            a = V.do(tt, TH, lim, DTC, MUL)
            V.wait(a)
            a = V.do(ts, T1_, TH, 1.0 / TWO_PI, MAGIC, MUL, ADD)
            V.wait(a)
            a = V.do(ts, T1_, T1_, MAGIC, None, SUB)
            V.wait(a)
            a = V.do(stt, out=TH, in0=T1_, scalar=-TP_HI, in1=TH, op0=MUL, op1=ADD)
            V.wait(a)
            a = V.do(stt, out=TH, in0=T1_, scalar=-TP_LO, in1=TH, op0=MUL, op1=ADD)
            V.wait(a)
            a = V.do(ts, TH, TH, float(np.pi), -float(np.pi), MIN, MAX)
            yield
            S.wait(a)
            sn = S.do(act, SN, TH, ACT.Sin)
            c = S.do(act, CN, TH, ACT.Abs)
            S.wait(c)
            cn = S.do(act, CN, CN, ACT.Sin, scale=-1.0, bias=hpi_c)
            yield
            V.wait(sn, cn, rr_tok)
            a = V.do(tt, CN, CN, RR[:, :], MUL)
            b_ = V.do(tt, SN, SN, RR[:, :], MUL)
            V.wait(a, b_)
            a = V.do(ts, CN, CN, 1.0, None, SUB)
            c = V.do(tt, T2_, lre, lre, MUL)
            d = V.do(tt, T3_, lim, lim, MUL)
            V.wait(a, c, d)
            a = V.do(tt, T2_, T2_, T3_, ADD)
            V.wait(a)
            yield
            a = V.do(nc.vector.reciprocal, T2_, T2_)
            c = V.do(tt, X1, CN, lre, MUL)
            d = V.do(tt, X2, SN, lim, MUL)
            V.wait(c, d, a)
            c = V.do(tt, CFR, X1, X2, ADD)
            yield
            V.wait(c)
            d = V.do(tt, X1, SN, lre, MUL)
            e = V.do(tt, X2, CN, lim, MUL)
            V.wait(d, e)
            d = V.do(tt, CFI, X1, X2, SUB)
            V.wait(d, c)
            c = V.do(tt, CFR, CFR, T2_, MUL)
            d = V.do(tt, CFI, CFI, T2_, MUL)
            s5c["co"] = (TH, CFR, CFI, [c, d])
            yield

        def s5_blocks(CFR, CFI, cf_tok):
            bd = lambda x: x.unsqueeze(2).to_broadcast([P, 16, 16])
            t = [v3(S5T[i], 16) for i in range(3)]
            G.wait(ao)
            z = [G.do(nc.gpsimd.memset, BB[i].rearrange("p a n -> p (a n)"), 0.0) for i in range(2)]
            V.wait(s_small["ssm_b_re_2"], s_small["ssm_b_im_2"], *cf_tok, *z)
            a = V.do(tt, t[0], BR[0], bd(CFR), MUL)
            b_ = V.do(tt, t[1], BR[1], bd(CFI), MUL)
            V.wait(a, b_)
            yield
            for e in range(2):
                r = slice(64 * e, 64 * e + 64)
                a = V.do(tt, BB[0][r, :, 16 * e:16 * e + 16], t[0][r], t[1][r], SUB)
            yield
            V.wait(a)
            c = V.do(tt, t[0], BR[0], bd(CFI), MUL)
            b_ = V.do(tt, t[1], BR[1], bd(CFR), MUL)
            V.wait(c, b_)
            yield
            for e in range(2):
                r = slice(64 * e, 64 * e + 64)
                c = V.do(tt, BB[1][r, :, 16 * e:16 * e + 16], t[0][r], t[1][r], ADD)
            yield
            yield
            PE.wait(c, a)
            res = []
            for i in range(2):
                b, pb = bank()
                for m in range(4):
                    tk = PE.do(tr, pb[:, m * P:m * P + P], BB[i][:, 4 * m:4 * m + 4, :].rearrange("p a n -> p (a n)"),
                               ident)
                S.wait(tk)
                r = S.do(act, BT[i].rearrange("p a n -> p (a n)"), pb[:, :], ACT.Copy)
                free(b, r)
                res.append(r)
                yield
            V.wait(s_small["ssm_c_re_2"], s_small["ssm_c_im_2"])
            for i in range(2):
                cm = CM[i].rearrange("p (m e n) -> p m e n", m=4, e=2)
                for e in range(2):
                    c = V.do(ts, cm[:, :, e, :], CR[i], cst[:, C_M2 + e:C_M2 + e + 1], None, MUL)
                yield
                b, pb = bank()
                PE.wait(c)
                for m in range(4):
                    tk = PE.do(tr, pb[:, m * P:m * P + P], CM[i][:, m * P:m * P + P], ident)
                S.wait(tk)
                if i == 0:
                    r = S.do(act, CT[0].rearrange("p a n -> p (a n)"), pb[:, :], ACT.Copy)
                else:
                    r = S.do(act, CT[2].rearrange("p a n -> p (a n)"), pb[:, :], ACT.Copy, scale=-1.0)
                free(b, r)
                res.append(r)
                yield
            s5c["blk"] = res

        tab_tok = {}

        def s5_tables(TH, j0, toks):
            js = (j0, j0 + 1)
            x_ = {j: ar(16640 + 256 * (j % 4), 256) for j in js}
            k_ = {j: ar(17664 + 256 * (j % 4), 256) for j in js}
            a = {}
            for j in js:
                S.wait(*toks, *tab_tok.get(j - 4, []))
                a[j] = S.do(act, x_[j], tvec, ACT.Copy, scale=TH[:, j:j + 1])
            yield
            for j in js:
                V.wait(a[j])
                a[j] = V.do(ts, k_[j], x_[j], 1.0 / TWO_PI, MAGIC, MUL, ADD)
            for j in js:
                V.wait(a[j])
                a[j] = V.do(ts, k_[j], k_[j], MAGIC, None, SUB)
            yield
            for h in (-TP_HI, -TP_LO):
                for j in js:
                    V.wait(a[j])
                    a[j] = V.do(stt, out=x_[j], in0=k_[j], scalar=h, in1=x_[j], op0=MUL, op1=ADD)
                yield
            for j in js:
                V.wait(a[j])
                a[j] = V.do(ts, x_[j], x_[j], float(np.pi), -float(np.pi), MIN, MAX)
            yield
            c = {}
            for j in js:
                S.wait(a[j])
                a[j] = S.do(act, SIN[:, j, :], x_[j], ACT.Sin)
                c[j] = S.do(act, COS[:, j, :], x_[j], ACT.Abs)
            yield
            for j in js:
                S.wait(c[j])
                c[j] = S.do(act, COS[:, j, :], COS[:, j, :], ACT.Sin, scale=-1.0, bias=hpi_c)
                tab_tok[j] = [a[j], c[j]]
            yield

        s5c = {}

        def ffn(tag, fin):
            pend = None
            for blk in range(12):
                new = None
                if blk < 11:
                    bks = [bank(), bank()]
                    for part, nm in enumerate((f"{tag}g", f"{tag}u")):
                        u = Unit(nm)
                        for half in range(2):
                            H, L = u.piece(half)
                            for m in range(2):
                                for kk in range(4):
                                    sl = slice(m * P, m * P + P)
                                    tk = mm3(bks[m][1][:, part * T:part * T + T], (H[:, kk, sl], L[:, kk, sl]),
                                             hpair(4 * half + kk), part == 0 and half == 0 and kk == 0,
                                             half == 1 and kk == 3)
                            u.done(half, tk)
                    o = 512 * (blk % 4)
                    toks = []
                    for m in range(2):
                        pb = bks[m][1]
                        f = ar(o + T * m, T)
                        r = silu_t(pb, tk, f, f_free[blk % 4], T)
                        V.wait(r)
                        r = V.do(tt, f, f, pb[:, T:2 * T], MUL)
                        free(bks[m][0], r)
                        toks.append(r)
                    new = (ypair(ar(o, 512), toks), blk)
                    f_free[blk % 4] = [new[0][1]]
                    last_h = tk
                if pend is not None:
                    tk = acc_rows(Unit(f"{tag}d"), pend[0], pend[1] == 0, pend[1] == 10,
                                  tail=fin if pend[1] == 10 else None)
                pend = new
            h_free.append(last_h)
            return tk

        HG = PC[:, 32:40]

        def ffn_layer(tag, mo, gname, x_norm=None, fin=None):
            M = M2[:, mo:mo + 24]
            c0 = 6 + mo // 8
            ada_flush()
            V.wait(*h_tok)
            g = mod_cols(M, gname, 0, GS, [ada_out[c0 + 1]])
            if x_norm is None:
                norm_mod(fin, GS, M[:, 0:8], [g, ada_out[c0]])
            else:
                V.wait(g)
                g = V.do(tt, GS, GS, fg, MUL)
                free(x_norm[0], modulate(x_norm[1], GS, M[:, 0:8], [x_norm[2], g, ada_out[c0]]))

            def gate():
                return HG, [V.wait(*st_tok[-1], ada_out[c0 + 2]).do(ts, HG, M[:, 16:24], 0.5, None, MUL)]
            fin = Finish(gate)
            tk = ffn(tag, fin)
            ada_flush()
            return tk, fin

        f_free = [[ao]] * 4

        def s5_prep():
            yield from update_x()
            yield from s5_coefs()
            TH, CFR, CFI, t = s5c["co"]
            yield from s5_blocks(CFR, CFI, t)
            for j in range(0, 16, 2):
                yield from s5_tables(TH, j, t)

        bg_rate[0] = 1.25
        bg.append(s5_prep())
        f1_done, fin = ffn_layer("f1", 0, "ffn1_norm", x_norm)
        bg_flush()

        M = M2[:, 24:48]
        ada_flush()
        V.wait(*h_tok)
        g = mod_cols(M, "mix_norm", 0, GS, [ada_out[10]])
        norm_mod(fin, GS, M[:, 0:8], [g, ada_out[9]])
        UT = v3(ar(12800, 1024), 4)
        BG = v3(ar(13824, 1024), 4)
        ZP = v3(ar(14848, 1032), 4)
        YCV = v3(ar(15880, 1024), 4)
        YS = v3(ar(16904, 1024), 4)
        PT = [[ar(512 * i, 512) for i in range(4)], [ar(17928 + 512 * i, 512) for i in range(4)]]
        prep_done = [s5c["blk"][-1]] + tab_tok[14] + tab_tok[15]
        u_tok = []

        def win_u(j):
            def ev(pb, tk):
                S.wait(tk, f1_done, *prep_done)
                r = S.do(act, UT[:, 2 * j:2 * j + 2, :], v3(pb[:, :], 2), ACT.Copy)
                u_tok.append(r)
                return [r]
            return cols_T(Unit("win"), None, ev)

        cv = {}
        cv_tok = []

        def win_c(j):
            def ev(pb, tk):
                S.wait(tk, *prep_done)
                r = S.do(act, ZP[:, 2 * j:2 * j + 2, 2:258], v3(pb[:, :], 2), ACT.Copy)
                cv[("c", j)] = r
                return [r]
            return cols_T(Unit("win"), None, ev)

        def win_v(j):
            def ev(pb, tk):
                V.wait(tk, cv[("c", j)])
                r = V.do(tt, ZP[:, 2 * j:2 * j + 2, 2:258], ZP[:, 2 * j:2 * j + 2, 2:258], v3(pb[:, :], 2), MUL)
                cv[("z", j)] = r
                return [r]
            return cols_T(Unit("win"), None, ev)

        def win_b(j):
            def ev(pb, tk):
                S.wait(tk, *prep_done)
                r = S.do(act, BG[:, 2 * j:2 * j + 2, :], v3(pb[:, :], 2), ACT.Copy)
                cv[("b", j)] = r
                return [r]
            return cols_T(Unit("win"), None, ev)

        G.wait(*prep_done)
        zp_tok = G.do(nc.gpsimd.memset, ZP[:, :, 0:2], 0.0)

        def conv_pair(j):
            y = YCV[:, 2 * j:2 * j + 2, :]
            V.wait(cv[("z", j)], cv[("b", j)], zp_tok)
            a = {}
            for n in (2 * j, 2 * j + 1):
                a[n] = V.do(ts, YCV[:, n, :], ZP[:, n, 2:258], col("conv_w", 8 + n), None, MUL)
            yield
            for d in (1, 0):
                for n in (2 * j, 2 * j + 1):
                    V.wait(a[n])
                    a[n] = V.do(stt, out=YCV[:, n, :], in0=ZP[:, n, d:d + 256], scalar=col("conv_w", 4 * d + n),
                                in1=YCV[:, n, :], op0=MUL, op1=ADD)
                yield
            V.wait(a[2 * j + 1])
            a = V.do(tt, y, y, BG[:, 2 * j:2 * j + 2, :], MUL)
            cv_tok.extend([a, a])
            yield

        def rms_half(tiles, toks, gname):
            return scale_half(tiles, norm_r(tiles, toks, 512), gname)

        def scale_half(tiles, r, gname):
            b, rb, tk = r
            res = []
            V.wait(tk)
            for n in range(4):
                res.append(V.do(stt, out=tiles[n], in0=tiles[n], scalar=col(gname, n), in1=rb, op0=MUL, op1=MUL))
            free(b, res[-1])
            return res

        pt_free = [[], []]
        ys_toks = []
        gelu_tok = []
        gt = nc.gpsimd.tensor_tensor

        def s5_in(p):
            m = p // 2
            bks = [bank(), bank()]
            if p == 0:
                PE.wait(*s5c["blk"])
            PE.wait(u_tok[m // 2])
            for e in range(2):
                jj = (2 * p + e) % 4
                r = slice(32 * jj, 32 * jj + 32)
                if e == 1:
                    PE.wait(tk)
                for i in range(2):
                    tk = mmf(bks[i][1][:, e * T:e * T + T], BT[i][r, m, :], UT[r, m, :], e == 0, True)
            return bks, tk

        def s5_rot(p, bks, tk):
            p1, p2, p3, p4 = PT[p % 2]
            C_, S_ = (f2(x[:, 2 * p:2 * p + 2, :]) for x in (COS, SIN))
            (b0, re), (b1, im) = bks
            V.wait(tk, *tab_tok[2 * p], *tab_tok[2 * p + 1], *pt_free[p % 2], *f_free_all)
            a1 = V.do(tt, p1, re[:, :], C_, MUL)
            a2 = V.do(tt, p2, im[:, :], S_, MUL)
            yield
            G.wait(a1, a2)
            g1 = G.do(gt, p1, p1, p2, ADD)
            a3 = V.do(tt, p3, im[:, :], C_, MUL)
            free(b1, a3)
            a4 = V.do(tt, p4, re[:, :], S_, MUL)
            free(b0, a4)
            G.wait(a3, a4)
            g2 = G.do(gt, p3, p3, p4, SUB)
            st[p] = (g1, g2)
            yield

        def s5_scan(p):
            p1, p2, p3, p4 = PT[p % 2]
            C_, S_ = (f2(x[:, 2 * p:2 * p + 2, :]) for x in (COS, SIN))
            g1, g2 = st[p]
            scan = nc.vector.tensor_tensor_scan
            for dst, src, g in ((p2, p1, g1), (p4, p3, g2)):
                V.wait(g)
                for e in range(2):
                    sl = slice(e * T, e * T + T)
                    rb = RR[:, 2 * p + e:2 * p + e + 1].to_broadcast([P, T])
                    s = V.do(scan, dst[:, sl], rb, src[:, sl], 0.0, MUL, ADD)
            yield
            V.wait(s)
            V.do(tt, p1, C_, p2, MUL)
            a1 = V.do(tt, p3, C_, p4, MUL)
            yield
            V.wait(a1)
            a2 = V.do(tt, p4, S_, p4, MUL)
            G.wait(a2)
            g1 = G.do(gt, p1, p1, p4, SUB)
            a3 = V.do(tt, p2, S_, p2, MUL)
            G.wait(a3)
            g2 = G.do(gt, p3, p3, p2, ADD)
            st[p] = (g1, g2)
            yield

        def s5_out(p):
            m = p // 2
            p1, p2, p3, p4 = PT[p % 2]
            if p % 2 == 0:
                s5o[:] = bank()
            b, pb = s5o
            PE.wait(*st[p])
            for e in range(2):
                jj = (2 * p + e) % 4
                r = slice(32 * jj, 32 * jj + 32)
                sl = slice(e * T, e * T + T)
                mmf(pb[r, 0:T], CT[0][:, m, r], p1[:, sl], True, False)
                tk = mmf(pb[r, 0:T], CT[2][:, m, r], p3[:, sl], False, True)
            pt_free[p % 2] = [tk]
            if p % 2 == 1:
                V.wait(tk, *prep_done)
                ys_toks.append(V.do(stt, out=YS[:, m, :], in0=UT[:, m, :], scalar=col("ssm_d", m),
                                    in1=pb[:, 0:T], op0=MUL, op1=ADD))
                free(b, ys_toks[-1])

        def gelu(m):
            y, e = YS[:, m, :], SQT[:, 4 + m, :]
            S.wait(ys_toks[m], *sq_free[4 + m])
            a = S.do(act, e, y, ACT.Square)
            yield
            V.wait(a)
            a = V.do(ts, e, e, GELU_C * 0.044715, GELU_C, MUL, ADD)
            V.wait(a)
            a = V.do(tt, e, e, y, MUL)
            S.wait(a)
            a = S.do(act, e, e, ACT.Tanh, scale=0.5)
            yield
            V.wait(a)
            a = V.do(ts, e, e, 0.5, 0.5, MUL, ADD)
            V.wait(a)
            a = V.do(tt, y, y, e, MUL)
            sq_free[4 + m] = [a]
            gelu_tok.append(a)
            yield

        st = {}
        s5o = [None, None]
        f_free_all = [f1_done]
        win_u(0)
        jobs = [lambda: win_u(1), lambda: win_c(0), lambda: win_v(0), lambda: win_b(0),
                lambda: win_c(1), lambda: win_v(1), lambda: win_b(1)]
        bg_rate[0] = 3
        for p in range(7):
            r = s5_in(p)
            if p > 0:
                bg.append(s5_scan(p - 1))
            bg.append(s5_rot(p, *r))
            if p in (3, 5):
                bg.append(gelu(p // 2 - 1))
            if p == 4:
                bg.append(conv_pair(0))
            last_h = jobs[p]()
            bg_flush()
            if p > 0:
                s5_out(p - 1)
        h_free.append(last_h)
        r = s5_in(7)
        bg.append(conv_pair(1))
        bg_flush()
        b0, pb0 = bank()
        r0 = sumsq(pb0, 0, [YCV[:, n, :] for n in range(4)], [[t] for t in cv_tok])
        bg.append(s5_scan(6))
        bg_flush()
        a, z = rsqrt(RS[:, 0:2], pb0[:, 0:2], 1.0 / 512, [r0], (RS[:, 2:4], RS[:, 4:6]))
        free(b0, a)
        rb = spread_r(z)
        s5_out(6)
        cvn = scale_half([YCV[:, n, :] for n in range(4)], rb, "out_norm_conv")
        pl = [ypair(f2(YCV[:, 0:2, :]), [cvn[1]]), ypair(f2(YCV[:, 2:4, :]), [cvn[3]])]
        bg.append(s5_rot(7, *r))
        bg_flush()
        gl = [ypair(f2(YS[:, 0:2, :]), [gelu_tok[1]])]
        bg.extend([gelu(2), s5_scan(7)])
        bg_flush()
        acc_rows(Unit("wout"), pl[0], True, False)
        s5_out(7)
        NGB = PC[:, 40:44]
        V.wait(vc2_tok, ebl_tok)
        nb = V.do(ts, NGB, col("glu_b", 0, 4), 0.5, None, MUL)
        bg.append(gelu(3))
        bg_flush()
        gl.append(ypair(f2(YS[:, 2:4, :]), [gelu_tok[3]]))
        u = Unit("glu")
        bks = [bank(), bank()]
        V.wait(gl[1][1])
        half_y = [V.do(ts, YS[:, n, :], YS[:, n, :], 0.5, None, MUL) for n in range(4)]
        for half in range(2):
            H, L = u.piece(half)
            i, t = gl[half]
            PE.wait(t)
            for n in range(4):
                for kk in range(2):
                    sl = slice(n * P, n * P + P)
                    tk = mm3(bks[n // 2][1][:, (n % 2) * T:(n % 2) * T + T], (H[:, kk, sl], L[:, kk, sl]),
                             (YH[:, i, kk, :], YL[:, i, kk, :]), half == 0 and kk == 0 and n % 2 == 0,
                             half == 1 and kk == 1)
            yfree[i] = [tk]
            u.done(half, tk)
        S.wait(tk, nb, *cv_tok)
        gtk = []
        for n in range(4):
            r = S.do(act, BG[:, n, :], bks[n // 2][1][:, (n % 2) * T:(n % 2) * T + T], ACT.Tanh,
                     scale=0.5, bias=NGB[:, n:n + 1])
            if n % 2 == 1:
                free(bks[n // 2][0], r)
            V.wait(r, *half_y)
            gtk.append(V.do(stt, out=YS[:, n, :], in0=BG[:, n, :], scalar=1.0, in1=YS[:, n, :], op0=ADD, op1=MUL))

        ssn = []

        def ssm_norm():
            ssn.extend(rms_half([YS[:, n, :] for n in range(4)], [[t] for t in gtk], "out_norm_ssm"))
            yield
            ny[0] += 1
            pl.extend([ypair(f2(YS[:, 0:2, :]), [ssn[1]]), ypair(f2(YS[:, 2:4, :]), [ssn[3]])])
            yield

        u = Unit("wout")
        bg_rate[0] = 0
        acc_rows(u, pl[1], False, False, mid=ssm_norm())
        fin = Finish(lambda: (M[:, 16:24], [ada_out[11]]))
        for q in range(2):
            tk = acc_rows(Unit("wout"), pl[2 + q], False, q == 1, tail=fin if q == 1 else None)
        ada_flush()
        f_free[:] = [[tk]] * 4
        bg_rate[0] = 1

        f2_done, fin = ffn_layer("f2", 48, "ffn2_norm", fin=fin)

        OUT = v3(ar(4096, 2048), 2)
        st = []
        FX = v3(ar(6144, 2048), 8)
        for k in range(8):
            V.wait(*x_tok[k], ys_toks[-1])
            st.append(V.do(ts, FX[:, k, :], xT[:, k, :], col("final_norm", k), None, MUL))
        z = fin.norm()
        outs = []
        for m in range(2):
            for q in range(2):
                b, pb = bank()
                for kk in range(4):
                    k = 4 * q + kk
                    PE.wait(st[k])
                    tk = PE.do(tr, pb[:, kk * P:kk * P + P], FX[:, k, m * P:m * P + P], ident)
                if q == 0:
                    S.wait(tk, z)
                    o_tok = S.do(act, OUT[:, m, 512 * q:512 * q + 512], pb[:, :], ACT.Copy, scale=RS[:, m:m + 1])
                else:
                    V.wait(tk, z)
                    o_tok = V.do(ts, OUT[:, m, 512 * q:512 * q + 512], pb[:, :], RS[:, m:m + 1], None, MUL)
                free(b, o_tok)
                S.wait(o_tok)
                so = sem(f"s_out{m}{q}")
                S.dma(nc.scalar.dma_start, out[0, m * P:m * P + P, 512 * q:512 * q + 512],
                      OUT[:, m, 512 * q:512 * q + 512], so)
                outs.append((so, 16))
        S.wait(*outs)

        assert cur[0] == len(units)
        for i, (nm, src, k, n) in enumerate(units):
            for h in range(2):
                g = 2 * i + h
                if g >= RING:
                    SP.wait(unit_free[g - RING])
                SP.dma(nc.sync.dma_start, v3(slot(i, h), k // 2), src[:, h * k // 2:(h + 1) * k // 2, :],
                       s_ring[g % RING])

        block = ctx.enter_context(nc.Block())

        @block.sync
        def _(eng):
            SP.emit(eng)

        @block.tensor
        def _(eng):
            PE.emit(eng)

        @block.vector
        def _(eng):
            V.emit(eng)

        @block.scalar
        def _(eng):
            S.emit(eng)

        @block.gpsimd
        def _(eng):
            G.emit(eng)


_INS = ["x", "c", "ada_w", "ada_b", "norm_g", "even_in_w", "pool_w", "pool_scale", "sgu_norm_g", "sgu_w", "sgu_b",
        "even_out_w", "odd_in_w", "gla_gate_w", "gla_gate_b", "gla_norm_g", "odd_out_w", "final_g", "cond_2",
        "w_mod_2", "b_mod_2", "ffn1_norm_2", "ffn1_w_gate_2", "ffn1_w_up_2", "ffn1_w_down_2", "mix_norm_2",
        "w_in_2", "conv_w_2", "lambda_re_2", "lambda_im_2", "log_dt_2", "ssm_b_re_2", "ssm_b_im_2", "ssm_c_re_2",
        "ssm_c_im_2", "ssm_d_2", "glu_w_2", "glu_b_2", "out_norm_conv_2", "out_norm_ssm_2", "w_out_2",
        "ffn2_norm_2", "ffn2_w_gate_2", "ffn2_w_up_2", "ffn2_w_down_2", "final_norm_2"]


def kernel(**inputs):
    import concourse.bacc as _bacc
    from concourse.bass_utils import run_bass_kernel_spmd as _run

    nc = _bacc.Bacc("TRN2", target_bir_lowering=False, num_devices=1)
    arrays, aps = {}, {}
    given = {n: np.ascontiguousarray(inputs[n]) for n in _INS}
    given["consts"] = constants()
    for name, a in given.items():
        arrays[f"in_{name}"] = a
        aps[name] = nc.dram_tensor(f"in_{name}", a.shape, mybir.dt.from_np(a.dtype), kind="ExternalInput").ap()
    out = nc.dram_tensor("out_0", (1, T, D), F32, kind="ExternalOutput").ap()
    build(nc, aps, out)
    r = _run(nc, [arrays], core_ids=[0])
    return r.results[0]["out_0"]
```
